# Optimizing a Trainium2 kernel written in Bass

```python
import jax, jax.numpy as jnp
from jax import lax
import numpy as np

D_MODEL = 1024
BATCH = 1
SEQ = 512
DEPTH = 1

PLE_DIM = 256
D_MIX = D_MODEL
CONV_CH = D_MIX // 2
CONV_GROUPS = 8
CONV_WIDTH = 31
ATTN_WIDTH = D_MIX - CONV_CH
HEAD_DIM = 64
N_HEADS = ATTN_WIDTH // HEAD_DIM
ROT_DIM = HEAD_DIM // 4
ROPE_THETA = 500000.0
MOBA_BLOCK = 256
MOBA_TOPK = 3
Q_CHUNK = 16
N_GROUPS = 4
EXPERTS_PER_GROUP = 8
N_EXPERTS = N_GROUPS * EXPERTS_PER_GROUP
TOPK_IN_GROUP = 2
D_EXPERT = D_MODEL // 4
IN_COLS = 2 * CONV_CH + 3 * ATTN_WIDTH
EPS = 1e-6

kernel_name = 'hymba_conformer_moba_hmoe_block'

def rms_norm(x, g):
    xf = x.astype(jnp.float32)
    y = xf * lax.rsqrt(jnp.mean(xf * xf, axis=-1, keepdims=True) + EPS)
    return (y * g.astype(jnp.float32)).astype(x.dtype)

def layer_norm(x, g, b):
    xf = x.astype(jnp.float32)
    mu = jnp.mean(xf, axis=-1, keepdims=True)
    var = jnp.mean(jnp.square(xf - mu), axis=-1, keepdims=True)
    y = (xf - mu) * lax.rsqrt(var + EPS) * g.astype(jnp.float32) + b.astype(jnp.float32)
    return y.astype(x.dtype)

def rope_tables(seq):
    pos = jnp.arange(seq, dtype=jnp.float32)
    inv_freq = jnp.power(jnp.float32(ROPE_THETA), -jnp.arange(0, ROT_DIM, 2, dtype=jnp.float32) / ROT_DIM)
    ang = pos[:, None] * inv_freq[None, :]
    return jnp.cos(ang), jnp.sin(ang)

def partial_rope(t, cos, sin):
    half = ROT_DIM // 2
    tf = t.astype(jnp.float32)
    t1 = tf[..., :half]
    t2 = tf[..., half:ROT_DIM]
    out = jnp.concatenate([t1 * cos - t2 * sin, t2 * cos + t1 * sin, tf[..., ROT_DIM:]], axis=-1)
    return out.astype(t.dtype)

def conformer_conv(a, gate, w_dw, b_dw, ln_g, ln_b):
    u = a * jax.nn.sigmoid(gate)
    kern = w_dw[:, None, :].astype(u.dtype)
    y = lax.conv_general_dilated(u, kern, window_strides=(1,), padding=[(CONV_WIDTH - 1, 0)],
                                 dimension_numbers=('NWC', 'WIO', 'NWC'),
                                 feature_group_count=CONV_CH)
    y = y + b_dw.astype(y.dtype)
    y = layer_norm(y, ln_g, ln_b)
    return jax.nn.silu(y)

def moba_attention(q, k, v):
    B, H, S, dh = q.shape
    nb = -(-S // MOBA_BLOCK)
    s_pad = nb * MOBA_BLOCK
    pad = s_pad - S
    padw = ((0, 0), (0, 0), (0, pad), (0, 0))
    qp, kp, vp = jnp.pad(q, padw), jnp.pad(k, padw), jnp.pad(v, padw)
    kb = kp.reshape(B, H, nb, MOBA_BLOCK, dh)
    vb = vp.reshape(B, H, nb, MOBA_BLOCK, dh)
    neg = jnp.finfo(jnp.float32).min

    k_mean = jnp.mean(kb.astype(jnp.float32), axis=3)
    q_blk = jnp.arange(s_pad) // MOBA_BLOCK
    gate = jnp.einsum('bhsd,bhnd->bhsn', qp.astype(jnp.float32), k_mean)
    past = jnp.arange(nb)[None, :] < q_blk[:, None]
    gate = jnp.where(past, gate, neg)
    n_sel = min(MOBA_TOPK, nb)
    _, sel = lax.top_k(gate, n_sel)
    sel_valid = sel < q_blk[:, None]

    n_chunks = s_pad // Q_CHUNK
    q_c = jnp.moveaxis(qp.reshape(B, H, n_chunks, Q_CHUNK, dh), 2, 0)
    sel_c = jnp.moveaxis(sel.reshape(B, H, n_chunks, Q_CHUNK, n_sel), 2, 0)
    val_c = jnp.moveaxis(sel_valid.reshape(B, H, n_chunks, Q_CHUNK, n_sel), 2, 0)
    scale = HEAD_DIM ** -0.5
    gather_blocks = jax.vmap(jax.vmap(lambda blocks, idx: blocks[idx]))
    q_off = jnp.arange(Q_CHUNK)
    k_off = jnp.arange(MOBA_BLOCK)

    def attend_chunk(args):
        c, qc, selc, validc = args
        start = c * Q_CHUNK
        blk = start // MOBA_BLOCK
        in_blk = start % MOBA_BLOCK + q_off
        k_sel = gather_blocks(kb, selc).astype(jnp.float32)
        v_sel = gather_blocks(vb, selc).astype(jnp.float32)
        k_own = lax.dynamic_index_in_dim(kb, blk, axis=2, keepdims=False).astype(jnp.float32)
        v_own = lax.dynamic_index_in_dim(vb, blk, axis=2, keepdims=False).astype(jnp.float32)
        qf = qc.astype(jnp.float32) * scale
        s_sel = jnp.einsum('bhqd,bhqnkd->bhqnk', qf, k_sel)
        s_sel = jnp.where(validc[..., None], s_sel, neg).reshape(B, H, Q_CHUNK, n_sel * MOBA_BLOCK)
        s_own = jnp.einsum('bhqd,bhkd->bhqk', qf, k_own)
        s_own = jnp.where(k_off[None, :] <= in_blk[:, None], s_own, neg)
        probs = jax.nn.softmax(jnp.concatenate([s_sel, s_own], axis=-1), axis=-1)
        p_sel = probs[..., :n_sel * MOBA_BLOCK].reshape(B, H, Q_CHUNK, n_sel, MOBA_BLOCK)
        p_own = probs[..., n_sel * MOBA_BLOCK:]
        out = (jnp.einsum('bhqnk,bhqnkd->bhqd', p_sel, v_sel)
               + jnp.einsum('bhqk,bhkd->bhqd', p_own, v_own))
        return out.astype(qc.dtype)

    out = lax.map(attend_chunk, (jnp.arange(n_chunks), q_c, sel_c, val_c))
    out = jnp.moveaxis(out, 0, 2).reshape(B, H, s_pad, dh)
    return out[:, :, :S]

def hier_moe(h, w_group, b_group, w_erouter, b_erouter, w_gate, w_up, w_down):
    hf = h.astype(jnp.float32)
    g_logits = hf @ w_group.astype(jnp.float32) + b_group.astype(jnp.float32)
    g_probs = jax.nn.softmax(g_logits, axis=-1)
    g_idx = jnp.argmax(g_logits, axis=-1)
    g_w = jnp.take_along_axis(g_probs, g_idx[..., None], axis=-1)
    e_all = jnp.einsum('bsd,gde->bsge', hf, w_erouter.astype(jnp.float32)) + b_erouter.astype(jnp.float32)
    e_logits = jnp.take_along_axis(e_all, g_idx[..., None, None], axis=2)[:, :, 0]
    top_vals, top_idx = lax.top_k(e_logits, TOPK_IN_GROUP)
    top_w = jax.nn.softmax(top_vals, axis=-1) * g_w
    expert_id = g_idx[..., None] * EXPERTS_PER_GROUP + top_idx
    gates = jnp.sum(jax.nn.one_hot(expert_id, N_EXPERTS, dtype=jnp.float32) * top_w[..., None], axis=-2)
    y = jnp.zeros(h.shape, jnp.float32)
    for e in range(N_EXPERTS):
        hid = jax.nn.silu(h @ w_gate[e]) * (h @ w_up[e])
        y = y + gates[..., e:e + 1] * (hid @ w_down[e]).astype(jnp.float32)
    return y.astype(h.dtype)

def setup_inputs(seed: int = 0) -> dict:
    key = jax.random.key(seed)
    ks = jax.random.split(key, 24)
    f32 = jnp.float32
    nrm = lambda k, shape, s: jax.random.normal(k, shape, f32) * s
    L = DEPTH
    return {
        'x': nrm(ks[0], (BATCH, SEQ, D_MODEL), 1.0),
        'p': nrm(ks[1], (DEPTH, BATCH, SEQ, PLE_DIM), 1.0),
        'g_mix': 1.0 + nrm(ks[2], (L, D_MODEL), 0.02),
        'w_in': nrm(ks[3], (L, D_MODEL, IN_COLS), D_MODEL ** -0.5),
        'w_dw': nrm(ks[4], (L, CONV_WIDTH, CONV_CH), CONV_WIDTH ** -0.5),
        'b_dw': nrm(ks[5], (L, CONV_CH), 0.02),
        'conv_ln_g': 1.0 + nrm(ks[6], (L, CONV_CH), 0.02),
        'conv_ln_b': nrm(ks[7], (L, CONV_CH), 0.02),
        'beta_conv': 1.0 + nrm(ks[8], (L, CONV_CH), 0.02),
        'beta_attn': 1.0 + nrm(ks[9], (L, ATTN_WIDTH), 0.02),
        'w_out': nrm(ks[10], (L, D_MIX, D_MODEL), D_MIX ** -0.5),
        'g_ffn': 1.0 + nrm(ks[11], (L, D_MODEL), 0.02),
        'w_group': nrm(ks[12], (L, D_MODEL, N_GROUPS), D_MODEL ** -0.5),
        'b_group': nrm(ks[13], (L, N_GROUPS), 0.01),
        'w_erouter': nrm(ks[14], (L, N_GROUPS, D_MODEL, EXPERTS_PER_GROUP), D_MODEL ** -0.5),
        'b_erouter': nrm(ks[15], (L, N_GROUPS, EXPERTS_PER_GROUP), 0.01),
        'w_gate': nrm(ks[16], (L, N_EXPERTS, D_MODEL, D_EXPERT), D_MODEL ** -0.5),
        'w_up': nrm(ks[17], (L, N_EXPERTS, D_MODEL, D_EXPERT), D_MODEL ** -0.5),
        'w_down': nrm(ks[18], (L, N_EXPERTS, D_EXPERT, D_MODEL), D_EXPERT ** -0.5),
        'g_ple': 1.0 + nrm(ks[19], (L, D_MODEL), 0.02),
        'w_ple_gate': nrm(ks[20], (L, D_MODEL, D_MODEL), D_MODEL ** -0.5),
        'b_ple_gate': nrm(ks[21], (L, D_MODEL), 0.02),
        'w_ple_proj': nrm(ks[22], (L, PLE_DIM, D_MODEL), PLE_DIM ** -0.5),
        'g_final': 1.0 + nrm(ks[23], (D_MODEL,), 0.02),
    }

def reference(x, p, g_mix, w_in, w_dw, b_dw, conv_ln_g, conv_ln_b, beta_conv, beta_attn, w_out,
              g_ffn, w_group, b_group, w_erouter, b_erouter, w_gate, w_up, w_down,
              g_ple, w_ple_gate, b_ple_gate, w_ple_proj, g_final):
    B, S, _ = x.shape
    cos, sin = rope_tables(S)
    splits = [CONV_CH, 2 * CONV_CH, 2 * CONV_CH + ATTN_WIDTH, 2 * CONV_CH + 2 * ATTN_WIDTH]
    to_heads = lambda t: t.reshape(B, S, N_HEADS, HEAD_DIM).transpose(0, 2, 1, 3)
    for i in range(DEPTH):
        h = rms_norm(x, g_mix[i])
        proj = h @ w_in[i]
        c_val, c_gate, q, k, v = jnp.split(proj, splits, axis=-1)
        conv_out = conformer_conv(c_val, c_gate, w_dw[i], b_dw[i], conv_ln_g[i], conv_ln_b[i])
        q = partial_rope(to_heads(q), cos, sin)
        k = partial_rope(to_heads(k), cos, sin)
        attn = moba_attention(q, k, to_heads(v))
        attn = attn.transpose(0, 2, 1, 3).reshape(B, S, ATTN_WIDTH)
        mixed = jnp.concatenate([rms_norm(conv_out, beta_conv[i]), rms_norm(attn, beta_attn[i])], axis=-1)
        x = x + mixed @ w_out[i]
        x = x + hier_moe(rms_norm(x, g_ffn[i]), w_group[i], b_group[i], w_erouter[i], b_erouter[i],
                         w_gate[i], w_up[i], w_down[i])
        gate = jax.nn.sigmoid(rms_norm(x, g_ple[i]) @ w_ple_gate[i] + b_ple_gate[i])
        x = x + (p[i] @ w_ple_proj[i]) * gate
    return rms_norm(x, g_final)


_drawn_inputs = setup_inputs


def setup_inputs(seed=0):
    import zlib

    import numpy as np

    out = dict(_drawn_inputs(seed))
    spreads = {}
    factors = {'conv_ln_g': 10.525,
     'conv_ln_b': 11.102,
     'beta_conv': 11.3,
     'beta_attn': 10.546,
     'b_group': 31.334,
     'b_erouter': 34.079,
     'g_ple': 64.0,
     'b_ple_gate': 64.0,
     'g_final': 8.495,
     'g_ffn': 4.983}
    for name, (base, spread) in spreads.items():
        noise = np.random.default_rng([zlib.crc32(name.encode()), seed]).standard_normal(out[name].shape)
        drawn = base * np.exp(spread * noise) if base else spread * noise
        out[name] = __import__('jax').numpy.asarray(drawn.astype(out[name].dtype))
    for name, factor in factors.items():
        out[name] = (out[name] * factor).astype(out[name].dtype)
    return out
```

```python
from contextlib import ExitStack

import concourse.bass as bass
import concourse.mybir as mybir
import numpy as np

F32 = mybir.dt.float32
I32 = mybir.dt.int32
ALU = mybir.AluOpType
ACT = mybir.ActivationFunctionType
AX = mybir.AxisListType

P = 128
D = 1024
S = 512
TT = S // P
DK = D // P
CH = 512
CM = CH // P
NH = 8
DH = 64
TAPS = 31
EPS = 1e-6
NG, NE, EG = 4, 32, 8
NR = NG + NE
F = 256
FK = F // P
CAP = 64
PAIRS = NE // 2
PD = 256
PK = PD // P
NOWHERE = 4 * S
FAR = 3.0e38
ROT, THETA = 16, 500000.0

C_ID, C_UP, C_ROT, C_IOTA = 0, P, 2 * P, 3 * P
C_MASK = 4 * P
C_COS = C_MASK + S
C_SIN = C_COS + S
C_RANK = C_SIN + S
C_PAR = C_RANK + NE
C_GRP = C_PAR + NE
C_TOK = C_GRP + NG
C_ROW = C_TOK + TT
C_THR = C_ROW + 2 * TT
C_EPS = C_THR + 7
C_END = C_EPS + 1
PM = TAPS + 4
Q_BETA = CM * PM
Q_MIX, Q_FFN, Q_PLE = Q_BETA + CM, Q_BETA + CM + DK, Q_BETA + CM + 2 * DK
Q_RB = Q_BETA + CM + 3 * DK
Q_END = Q_RB + 1


def constants():
    c = np.zeros((P, C_END), np.float32)
    i = np.arange(P)
    c[:, C_ID:C_ID + P] = np.eye(P)
    c[:, C_UP:C_UP + P] = i[:, None] < i[None, :]
    for m in range(P):
        d = m % DH
        if d < ROT // 2:
            c[m + ROT // 2, C_ROT + m] = -1.0
        elif d < ROT:
            c[m - ROT // 2, C_ROT + m] = 1.0
    c[:, C_IOTA:C_IOTA + P] = i[None, :]
    c[:, C_MASK + S - P:C_MASK + S] = np.where(i[None, :] <= i[:, None], 0.0, -FAR)
    inv = np.power(np.float32(THETA), -np.arange(0, ROT, 2, dtype=np.float32) / np.float32(ROT))
    ang = np.arange(S, dtype=np.float32)[:, None] * inv[None, :]
    d = i % DH
    turned = d < ROT
    c[:, C_COS:C_COS + S] = np.where(turned[:, None], np.cos(ang).T[d % (ROT // 2)], 1.0)
    c[:, C_SIN:C_SIN + S] = np.where(turned[:, None], np.sin(ang).T[d % (ROT // 2)], 0.0)
    e = np.arange(NE)
    c[:, C_RANK:C_RANK + NE] = NE - e
    c[:, C_PAR:C_PAR + NE] = e % 2
    c[:, C_GRP:C_GRP + NG] = NG - np.arange(NG)
    c[:, C_TOK:C_TOK + TT] = i[:, None] + P * np.arange(TT)[None, :]
    tok = i[:, None] + P * np.arange(TT)[None, :]
    c[:, C_ROW:C_ROW + 2 * TT] = (NOWHERE - tok[:, :, None] - S * np.arange(2)[None, None, :]).reshape(P, 2 * TT)
    c[:, C_THR:C_THR + 7] = CAP * np.arange(1, 8)
    c[:, C_EPS] = EPS
    return c


class Banks:

    def __init__(self, full, free):
        self.full, self.free = full, free
        self.place, self.count = {}, [0] * len(full)

    def use(self, name, bank):
        self.count[bank] += 1
        self.place[name] = (bank, self.count[bank])

    def bank(self, name):
        return self.place[name][0]

    def wait_full(self, eng, name):
        b, n = self.place[name]
        eng.wait_ge(self.full[b], n)

    def wait_free(self, eng, name):
        b, n = self.place[name]
        if n > 1:
            eng.wait_ge(self.free[b], n - 1)

    def wait_emptied(self, eng, name):
        b, n = self.place[name]
        eng.wait_ge(self.free[b], n)


def plan_banks(banks):
    for k in range(DK):
        banks.use(("x", k), k)
    for m in range(CM):
        banks.use(("val", m), m)
        banks.use(("gate", m), 4 + m)
    for j in range(2 * CM + 1):
        if j < 2 * CM:
            banks.use(("raw", j), j % 2)
        if j >= 1:
            banks.use(("rot", j - 1), 2 + (j - 1) % 2)
    banks.use("mean", 0)
    for t in range(TT):
        banks.use(("v", t), 4 + t)
        if t == 0:
            banks.use("var", 1)
    banks.use("conv_sq", 2)
    for u in range(CM * TT):
        for hh in range(2):
            banks.use(("score", u, hh), 2 * (u % 2) + hh)
        if u % TT == 0:
            banks.use(("attn", u // TT), 6 + u // TT % 2)
    for u in range(CM * TT):
        for hh in range(2):
            banks.use(("probT", u, hh), 4 + hh)
    banks.use("attn_sq", 6)
    for q in range(2 * TT):
        banks.use(("outc", q), 2 * (q % 3))
        banks.use(("outa", q), 2 * (q % 3) + 1)
    for t in range(TT):
        for kh in range(2):
            banks.use(("h2", t, kh), 6 + kh)
    banks.use("logitT", 0)
    banks.use("logit", 1)
    for q in range(2 * TT):
        banks.use(("ple", q), 4 + q % 4)
    banks.use("rank", 2)
    banks.use("count", 3)
    for t in range(TT):
        for kh in range(2):
            banks.use(("h3", t, kh), 2 * (t % 2) + kh)
    for q in range(2 * TT):
        banks.use(("pgate", q), 4 + q % 4)


def build(nc, x, w_in, w_out, w_r, w_gate, w_up, w_down, w_pg, w_pp, pT, b_pg, g_final, prm, cst, out):
    ctx = ExitStack()
    with ctx:
        def sb(name, shape, dt=F32):
            return ctx.enter_context(nc.sbuf_tensor(name, shape, dt))

        def sem(name):
            return ctx.enter_context(nc.semaphore(name))

        rows_d = nc.dram_tensor("rows_d", [S, D], F32).ap()
        y_d = nc.dram_tensor("y_d", [2 * S, D], F32).ap()

        xs = sb("xs", [P, TT, D])
        mix = sb("mix", [P, 2 * CM * S])
        wring = sb("wring", [P, 2, 2, 3 * 2048])
        arena = sb("arena", [P, 14592])
        c = sb("c", [P, C_END])
        ones = sb("ones", [P, P])
        pr = sb("pr", [P, Q_END])
        wr = sb("wr", [P, DK, NR])
        lnr = sb("lnr", [P, S])
        mean_w = sb("mean_w", [P, P])
        sq = sb("sq", [P, 4, TT])
        ss = sb("ss", [P, 4, TT])
        rs = sb("rs", [P, 4, TT])
        gsq = sb("gsq", [P, TT])
        gss = sb("gss", [P, 2, TT])
        grs = sb("grs", [P, 2, TT])
        nmax = sb("nmax", [P, 2, 2])
        psum_p = sb("psum_p", [P, 2, 2])
        pinv = sb("pinv", [P, 2, 2])
        lg = sb("lg", [P, TT, NR])
        rt = sb("rt", [P, 8, TT, NE])
        hot = sb("hot", [P, 2, TT, NE])
        pairhot = sb("pairhot", [P, 2 * TT, PAIRS])
        numhot = sb("numhot", [P, 2 * TT, 2, PAIRS])
        sm = sb("sm", [P, 24, TT])
        slot = sb("slot", [P, TT, 2])
        cmax = sb("cmax", [P, 2])
        over = sb("over", [P, 8])
        rounds = sb("rounds", [P, 1], I32)
        tlist = sb("tlist", [P, 2, PAIRS], I32)
        tcur = sb("tcur", [P, 2], I32)
        ycur = sb("ycur", [P, 2], I32)

        def ar(lo, n):
            return arena[:, lo:lo + n]

        ident = c[:, C_ID:C_ID + P]
        logT = lnr[0:NR, :]
        mixc = mix[:, 0:CM * S].rearrange("p (m t) -> p m t", m=CM)
        mixa = mix[:, CM * S:2 * CM * S].rearrange("p (m t) -> p m t", m=CM)
        plep = mix[:, :].rearrange("p (t n) -> p t n", t=TT)
        hT = ar(0, DK * S).rearrange("p (k t) -> p k t", k=DK)
        prob = ar(0, 2048).rearrange("p (b h k) -> p b h k", b=2, h=2)
        probT = ar(2048, 2048).rearrange("p (b h k) -> p b h k", b=2, h=2)
        xg = ar(0, 2 * D).rearrange("p (b n) -> p b n", b=2)
        xgT = ar(2048, 2 * D).rearrange("p (b k t) -> p b k t", b=2, k=DK)
        qz = ar(4096, NH * S).rearrange("p (h t) -> p h t", h=NH)
        xn = ar(4096, TT * D).rearrange("p (t k n) -> p t k n", t=TT, k=DK)
        xn_rows = ar(4096, TT * D).rearrange("p (t n) -> p t n", t=TT)
        yb = ar(4096, 2 * D).rearrange("p (b n) -> p b n", b=2)
        sil = ar(6144, 2 * F).rearrange("p (b n) -> p b n", b=2)
        hid = ar(6656, 2 * F).rearrange("p (b k n) -> p b k n", b=2, k=FK)
        hidT = ar(7168, 2 * F).rearrange("p (b k t) -> p b k t", b=2, k=FK)
        kT = ar(8192, CM * S).rearrange("p (m t) -> p m t", m=CM)
        wpp = ar(8192, PK * D).rearrange("p (k n) -> p k n", k=PK)
        vr = ar(10240, TT * CH).rearrange("p (t n) -> p t n", t=TT)
        pTs = ar(10240, PK * S).rearrange("p (k t) -> p k t", k=PK)
        onehot = ar(11264, 2 * TT * P).rearrange("p (j n) -> p j n", j=2 * TT)
        U = S + TAPS - 1
        u = ar(12288, CM * U).rearrange("p (m t) -> p m t", m=CM)
        sqa = ar(12288, CM * S).rearrange("p (m t) -> p m t", m=CM)
        sg = mixa
        qraw = mixa[:, 0:2, :]
        qsin = mixa[:, 2:4, :]
        sqc = mixa

        junk0 = mix[:, 0:D]
        junk = ar(12288, D)

        flat = [wring[:, s].rearrange("p a n -> p (a n)") for s in range(2)]
        win = [flat[i // 3][:, (i % 3) * 4096:(i % 3 + 1) * 4096].rearrange("p (k n) -> p k n", k=DK)
               for i in range(5)]
        woc = flat[1][:, 8192:12288].rearrange("p (m n) -> p m n", m=CM)
        woa = flat[1][:, 0:4096].rearrange("p (m n) -> p m n", m=CM)
        wpg = flat[0][:, 0:DK * D].rearrange("p (k n) -> p k n", k=DK)
        yg = flat[1][:, 0:8 * D].rearrange("p (j n) -> p j n", j=8)
        gfin = flat[1][:, 8 * D:9 * D]
        brow = flat[1][0:1, 9 * D:10 * D]
        sgate = flat[1][:, 10 * D:12 * D].rearrange("p (b n) -> p b n", b=4)
        up_w = [[wring[:, s, a, 0:4096].rearrange("p (w k n) -> p w k n", w=2, k=DK) for a in range(2)]
                for s in range(2)]
        dn_w = [[wring[:, s, a, 4096:6144].rearrange("p (k n) -> p k n", k=FK) for a in range(2)]
                for s in range(2)]

        pb = [ctx.enter_context(nc.psum_tensor(f"bank{i}", [P, 512], F32)) for i in range(8)]
        banks = Banks([sem(f"bank_full{i}") for i in range(8)], [sem(f"bank_free{i}") for i in range(8)])
        plan_banks(banks)

        def bk(name):
            return pb[banks.bank(name)]

        def filled(ins, name):
            ins.then_inc(banks.full[banks.bank(name)], 1)

        def emptied(ins, name):
            ins.then_inc(banks.free[banks.bank(name)], 1)

        x_loaded = [sem(f"x_loaded{t}") for t in range(TT)]
        win_loaded = [sem(f"win_loaded{i}") for i in range(5)]
        woc_loaded, woa_loaded = sem("woc_loaded"), sem("woa_loaded")
        const_loaded = sem("const_loaded")
        prm_loaded = sem("prm_loaded")
        ple_loaded = sem("ple_loaded")
        pg_loaded = sem("pg_loaded")
        last_loaded = sem("last_loaded")
        pads_set = sem("pads_set")
        qz_set = sem("qz_set")
        root_ready = sem("root_ready")
        xn_ready = sem("xn_ready")
        tap_done = sem("tap_done")
        qcos_done = sem("qcos_done")
        rope_done = sem("rope_done")
        csq_ready = sem("csq_ready")
        lnr_ready = sem("lnr_ready")
        z_ready = sem("z_ready")
        silu_ready = sem("silu_ready")
        osq_ready = sem("osq_ready")
        mixc_ready = sem("mixc_ready")
        exp_ready = sem("exp_ready")
        pinv_ready = sem("pinv_ready")
        prob_ready = sem("prob_ready")
        sqa_ready = sem("sqa_ready")
        groot_ready = sem("groot_ready")
        attended = sem("attended")
        rs_ready = sem("rs_ready")
        rows_stored = sem("rows_stored")
        rstep = sem("rstep")
        exp_in = sem("exp_in")
        exp_out = sem("exp_out")
        chosen = sem("chosen")
        list_in = sem("list_in")
        list_ready = sem("list_ready")
        list_full = sem("list_full")
        rounds_ready = sem("rounds_ready")
        up_loaded = [[sem(f"up_loaded{s}{a}") for a in range(2)] for s in range(2)]
        dn_loaded = [[sem(f"dn_loaded{s}{a}") for a in range(2)] for s in range(2)]
        sp_go = sem("sp_go")
        pool_go = sem("pool_go")
        tcur_ready = sem("tcur_ready")
        ycur_ready = sem("ycur_ready")
        gathered = [sem(f"gathered{s}") for s in range(2)]
        xgT_full = sem("xgT_full")
        xgT_ready = sem("xgT_ready")
        up_done = sem("up_done")
        sil_ready = sem("sil_ready")
        hid_ready = sem("hid_ready")
        hidT_full = sem("hidT_full")
        hidT_ready = sem("hidT_ready")
        down_done = [sem(f"down_done{s}") for s in range(2)]
        ya_ready, yd_ready = sem("ya_ready"), sem("yd_ready")
        y_stored = [sem(f"y_stored{s}") for s in range(2)]
        yg_loaded = [sem(f"yg_loaded{t}") for t in range(TT)]
        x2_ready = sem("x2_ready")
        x3_ready = sem("x3_ready")
        o_ready = sem("o_ready")
        out_stored = sem("out_stored")

        def wait(eng, s, v):
            if not isinstance(v, int) or v > 0:
                eng.wait_ge(s, v)

        def expert_rounds(eng, one_round, between):
            one_round(0, True)
            eng.wait_ge(rounds_ready, 1)
            n = eng.value_load(rounds[0:1, 0:1], min_val=1, max_val=S // CAP)
            with eng.If(n > 1):
                with eng.Fori(1, n) as r:
                    between(r)
                    one_round(r, False)
            return n

        def expert_pairs(eng, r, first, pair):
            if first:
                for s in range(2):
                    pair(s, s, s, 0, False)
            with eng.Fori(1 if first else 0, PAIRS // 2 - 1) as i:
                for s in range(2):
                    pair(r * PAIRS + 2 * i + s, 2 * i + s, s, r * (PAIRS // 2) + i, False)
            for s in range(2):
                pair(r * PAIRS + PAIRS - 2 + s, PAIRS - 2 + s, s, r * (PAIRS // 2) + PAIRS // 2 - 1, s == 1)

        block = ctx.enter_context(nc.Block())

        @block.sync
        def _(sp):
            for t in range(TT):
                sp.dma_start(xs[:, t, :], x[t * P:(t + 1) * P, :]).then_inc(x_loaded[t], 16)
            w_in_k = w_in.rearrange("(p k) n -> p k n", k=DK)
            for i in range(5):
                sp.dma_start(win[i], w_in_k[:, :, i * 512:(i + 1) * 512]).then_inc(win_loaded[i], 16)
            sp.dma_start(woc, w_out[0:CH, :].rearrange("(m p) n -> p m n", p=P)).then_inc(woc_loaded, 16)

            def load_up(s, e):
                for a in range(2):
                    for w, src in enumerate((w_gate, w_up)):
                        sp.dma_start(up_w[s][a][:, w],
                                     src[bass.ds(e + a, 1)].rearrange("e (p k) n -> p (e k) n", k=DK)
                                     ).then_inc(up_loaded[s][a], 16)

            def load_down(s, e):
                for a in range(2):
                    sp.dma_start(dn_w[s][a],
                                 w_down[bass.ds(e + a, 1)].rearrange("e (p k) n -> p (e k) n", k=FK)
                                 ).then_inc(dn_loaded[s][a], 16)

            banks.wait_full(sp, ("raw", 3))
            load_up(0, 0)
            load_down(0, 0)
            banks.wait_full(sp, ("raw", 7))
            sp.dma_start(woa, w_out[CH:2 * CH, :].rearrange("(m p) n -> p m n", p=P)).then_inc(woa_loaded, 16)
            banks.wait_full(sp, ("attn", CM - 1))
            sp.dma_start(wpp, w_pp.rearrange("(p k) n -> p k n", k=PK)).then_inc(ple_loaded, 16)
            sp.dma_start(pTs, pT.rearrange("(p k) n -> p k n", k=PK)).then_inc(ple_loaded, 16)
            banks.wait_full(sp, ("outa", 2 * TT - 1))
            load_up(1, 2)
            load_down(1, 2)

            def one_round(r, first):
                half = PAIRS // 2
                if not first:
                    for s in range(2):
                        sp.wait_ge(up_done, r * PAIRS + s - 1)
                        sp.sem_inc(sp_go, 1)
                        load_up(s, 2 * s)
                        sp.wait_ge(down_done[s], r * half)
                        sp.sem_inc(sp_go, 1)
                        load_down(s, 2 * s)
                with sp.Fori(1, half) as i:
                    for s in range(2):
                        n = r * PAIRS + 2 * i + s
                        sp.wait_ge(up_done, n - 1)
                        sp.sem_inc(sp_go, 1)
                        load_up(s, 4 * i + 2 * s)
                        sp.wait_ge(down_done[s], r * half + i)
                        sp.sem_inc(sp_go, 1)
                        load_down(s, 4 * i + 2 * s)

            n = expert_rounds(sp, one_round, lambda r: None)
            sp.wait_ge(down_done[0], n * (PAIRS // 2))
            sp.sem_inc(sp_go, 1)
            pg = w_pg.rearrange("(p k) n -> p k n", k=DK)
            for k in range(0, DK, 2):
                sp.dma_start(wpg[:, k:k + 2, :], pg[:, k:k + 2, :]).then_inc(pg_loaded, 16)
            sp.wait_ge(down_done[1], n * (PAIRS // 2))
            sp.sem_inc(sp_go, 1)
            for s in range(2):
                sp.wait_ge(y_stored[s], n * (8 * PAIRS))
                sp.sem_inc(sp_go, 1)
            y_rows = y_d.rearrange("(k t p) n -> p t k n", k=2, p=P)
            for t in range(TT):
                sp.dma_start(yg[:, 2 * t:2 * t + 2, :], y_rows[:, t]).then_inc(yg_loaded[t], 16)
            sp.dma_start(gfin, g_final.partition_broadcast(P)).then_inc(last_loaded, 16)
            sp.dma_start(brow, b_pg).then_inc(last_loaded, 16)
            for t in range(TT):
                sp.wait_ge(o_ready, t + 1)
                sp.dma_start(out[t * P:(t + 1) * P, :], xn_rows[:, t, :]).then_inc(out_stored, 16)
            sp.wait_ge(out_stored, 16 * TT)

        @block.gpsimd
        def _(pool):
            qz_h = qz.rearrange("p (m h) t -> p m h t", h=2)
            banks.wait_full(pool, ("x", DK - 1))
            pool.memset(qz_h[64:128, :, 0, :], 0.0).then_inc(qz_set, 1)
            pool.wait_ge(qz_set, 1)
            pool.memset(qz_h[0:64, :, 1, :], 0.0).then_inc(qz_set, 1)
            pool.wait_ge(qz_set, 2)
            pool.wait_ge(const_loaded, 32)
            for j in range(2 * CM):
                b = j % 2
                banks.wait_full(pool, ("rot", j))
                if j >= 1:
                    pool.wait_ge(rope_done, 2 * j if j <= CM else CM + j)
                pool.tensor_tensor(qraw[:, b, :], qraw[:, b, :], c[:, C_COS:C_COS + S], ALU.mult).then_inc(qcos_done, 1)
                pool.wait_ge(qcos_done, j + 1)
                banks.wait_emptied(pool, ("rot", j))
                if j < CM:
                    for hh in range(2):
                        rows = slice(hh * DH, (hh + 1) * DH)
                        if hh == 1:
                            pool.wait_ge(rope_done, 2 * j + 1)
                        pool.tensor_tensor(qz[rows, 2 * j + hh, :], qraw[rows, b, :], qsin[rows, b, :],
                                           ALU.add).then_inc(rope_done, 1)
                else:
                    pool.tensor_tensor(kT[:, j - CM, :], qraw[:, b, :], qsin[:, b, :], ALU.add).then_inc(rope_done, 1)
            pool.wait_ge(rope_done, 3 * CM)
            for m in range(CM):
                pool.wait_ge(osq_ready, m + 1)
                pool.tensor_scalar(mixc[:, m, :], mixc[:, m, :], pr[:, m * PM + TAPS + 3:m * PM + TAPS + 4],
                                   None, ALU.mult).then_inc(mixc_ready, 1)
            for t in range(TT):
                pool.wait_ge(xn_ready, TT + t + 1)
                pool.dma_start(rows_d[t * P:(t + 1) * P, :], xn_rows[:, t, :]).then_inc(rows_stored, 16)
            pool.wait_ge(rows_stored, 16 * TT)

            def gather(n, g, s, h):
                wait(pool, xgT_full, n - 1)
                pool.sem_inc(pool_go, 1)
                wait(pool, gathered[s], 16 * h)
                pool.sem_inc(pool_go, 1)
                pool.tensor_copy(tcur[:, s:s + 1], tlist[:, 0, bass.ds(g, 1)]).then_inc(tcur_ready, 1)
                pool.wait_ge(tcur_ready, n + 1)
                pool.sem_inc(pool_go, 1)
                pool.indirect_dma_start(xg[:, s, :], None, rows_d,
                                        bass.IndirectOffsetOnAxis(ap=tcur[:, s:s + 1], axis=0)
                                        ).then_inc(gathered[s], 16)

            def scatter(n, g, s, h):
                pool.wait_ge(ya_ready, n + 1)
                pool.sem_inc(pool_go, 1)
                pool.wait_ge(yd_ready, n + 1)
                pool.sem_inc(pool_go, 1)
                wait(pool, y_stored[s], 16 * h)
                pool.sem_inc(pool_go, 1)
                pool.tensor_copy(ycur[:, s:s + 1], tlist[:, 1, bass.ds(g, 1)]).then_inc(ycur_ready, 1)
                pool.wait_ge(ycur_ready, n + 1)
                pool.sem_inc(pool_go, 1)
                pool.indirect_dma_start(y_d, bass.IndirectOffsetOnAxis(ap=ycur[:, s:s + 1], axis=0), yb[:, s, :], None,
                                        bounds_check=2 * S - 1, oob_is_err=False).then_inc(y_stored[s], 16)

            def one_round(r, first):
                pool.wait_ge(list_ready, r + 1)
                pool.sem_inc(pool_go, 1)
                half = PAIRS // 2
                for s in range(2):
                    gather(r * PAIRS + s, s, s, r * half)
                with pool.Fori(1, half) as i:
                    for s in range(2):
                        gather(r * PAIRS + 2 * i + s, 2 * i + s, s, r * half + i)
                        scatter(r * PAIRS + 2 * i + s - 2, 2 * i + s - 2, s, r * half + i - 1)
                for s in range(2):
                    scatter(r * PAIRS + PAIRS - 2 + s, PAIRS - 2 + s, s, r * half + half - 1)

            expert_rounds(pool, one_round, lambda r: None)

        @block.scalar
        def _(act):
            act.dma_start(c[:, 0:C_MASK], cst[:, 0:C_MASK]).then_inc(const_loaded, 16)
            act.dma_start(c[:, C_MASK:C_END], cst[:, C_MASK:C_END]).then_inc(const_loaded, 16)
            act.dma_start(pr[:], prm).then_inc(prm_loaded, 16)
            act.dma_start(wr[:], w_r.rearrange("(p k) n -> p k n", k=DK)).then_inc(prm_loaded, 16)
            eps = c[:, C_EPS:C_EPS + 1]

            def mean_root(which, t, unused):
                act.activation(unused, xs[:, t, :], ACT.Square, accum_out=sq[:, which, t:t + 1]).then_inc(root_ready, 1)
                act.wait_ge(root_ready, 2 * (which * TT + t) + 1)
                act.activation(ss[:, which, t:t + 1], sq[:, which, t:t + 1], ACT.Sqrt, scale=1.0 / D, bias=eps).then_inc(root_ready, 1)

            act.wait_ge(const_loaded, 32)
            for t in range(TT):
                act.wait_ge(x_loaded[t], 16)
                mean_root(0, t, junk0)
            act.wait_ge(prm_loaded, 32)
            for k in range(1, DK, 2):
                banks.wait_full(act, ("x", k))
                emptied(act.activation(hT[:, k, :], bk(("x", k))[:], ACT.Copy, scale=pr[:, Q_MIX + k:Q_MIX + k + 1]), ("x", k))
            for m in range(CM):
                banks.wait_full(act, ("gate", m))
                emptied(act.activation(sg[:, m, :], bk(("gate", m))[:], ACT.Sigmoid), ("gate", m))
            for j in range(2 * CM):
                banks.wait_full(act, ("raw", j))
                banks.wait_emptied(act, ("val", CM - 1))
                if j >= 2:
                    act.wait_ge(rope_done, 2 * (j - 1) if j <= CM else CM + j - 1)
                emptied(act.activation(qraw[:, j % 2, :], bk(("raw", j))[:], ACT.Copy), ("raw", j))
            act.wait_ge(rope_done, 3 * CM)
            banks.wait_emptied(act, "mean")
            for m in range(CM):
                act.activation(sqc[:, m, :], mixc[:, m, :], ACT.Square).then_inc(csq_ready, 1)
            banks.wait_full(act, ("v", 0))
            emptied(act.activation(vr[:, 0, :], bk(("v", 0))[:], ACT.Copy), ("v", 0))
            banks.wait_full(act, "var")
            emptied(act.activation(lnr[:], bk("var")[:], ACT.Sqrt, bias=eps), "var")
            banks.wait_full(act, ("v", 1))
            emptied(act.activation(vr[:, 1, :], bk(("v", 1))[:], ACT.Copy), ("v", 1))
            for m in range(CM):
                act.wait_ge(z_ready, m + 1)
                base = m * PM + TAPS
                act.activation(mixc[:, m, :], mixc[:, m, :], ACT.Silu, scale=pr[:, base + 1:base + 2],
                               bias=pr[:, base + 2:base + 3]).then_inc(silu_ready, 1)
            for m in range(CM):
                act.wait_ge(silu_ready, m + 1)
                act.activation(sqc[:, m, :], mixc[:, m, :], ACT.Square).then_inc(osq_ready, 1)
            for t in range(2, TT):
                banks.wait_full(act, ("v", t))
                emptied(act.activation(vr[:, t, :], bk(("v", t))[:], ACT.Copy), ("v", t))

            def exps(u_):
                i, b = u_ % TT, u_ % 2
                n = P * (i + 1)
                for hh in range(2):
                    banks.wait_emptied(act, ("score", u_, hh))
                    act.activation(prob[:, b, hh, 0:n], prob[:, b, hh, 0:n], ACT.Exp, scale=-1.0,
                                   bias=nmax[:, b, hh:hh + 1], accum_out=psum_p[:, b, hh:hh + 1]).then_inc(exp_ready, 1)

            def probs_out(u_):
                m, i, b = u_ // TT, u_ % TT, u_ % 2
                n = P * (i + 1)
                if u_ >= 2:
                    mb, ib = (u_ - 2) // TT, (u_ - 2) % TT
                    if ib == TT - 1:
                        banks.wait_full(act, ("attn", mb))
                    else:
                        act.wait_ge(attended, mb * (TT - 1) + ib + 1)
                for hh in range(2):
                    banks.wait_full(act, ("probT", u_, hh))
                    emptied(act.activation(probT[:, b, hh, 0:n], bk(("probT", u_, hh))[:, 0:n], ACT.Copy), ("probT", u_, hh))
                if i == 1 and m >= 1:
                    attn_sq(m - 1)

            def attn_sq(m):
                banks.wait_full(act, ("attn", m))
                act.activation(sqa[:, m, :], bk(("attn", m))[:], ACT.Square).then_inc(sqa_ready, 1)

            units = CM * TT
            for u_ in range(units + 1):
                if u_ < units:
                    exps(u_)
                if u_ >= 1:
                    probs_out(u_ - 1)
            attn_sq(CM - 1)
            act.activation(gss[:, 0, :], gsq[:], ACT.Sqrt, scale=1.0 / CH, bias=eps).then_inc(groot_ready, 1)
            banks.wait_full(act, "attn_sq")
            emptied(act.activation(gss[:, 1, :], bk("attn_sq")[:, 0:TT], ACT.Sqrt, scale=1.0 / CH, bias=eps), "attn_sq")
            for t in range(TT):
                banks.wait_emptied(act, ("outa", 2 * t + 1))
                mean_root(1, t, junk)
            banks.wait_full(act, "logitT")
            emptied(act.activation(logT, bk("logitT")[0:NR, :], ACT.Identity, bias=pr[0:NR, Q_RB:Q_RB + 1]), "logitT")

            def ple_out(q):
                banks.wait_full(act, ("ple", q))
                if q == 0:
                    banks.wait_full(act, ("outa", 2 * TT - 1))
                emptied(act.activation(plep[:, q // 2, (q % 2) * 512:(q % 2 + 1) * 512], bk(("ple", q))[:], ACT.Copy),
                        ("ple", q))

            act.wait_ge(exp_in, 1)
            act.activation(rt[:, 0, :, 0:NG], rt[:, 0, :, 0:NG], ACT.Exp).then_inc(exp_out, 1)
            act.wait_ge(exp_in, 2)
            act.activation(sm[:, 6, :], sm[:, 6, :], ACT.Exp).then_inc(exp_out, 1)
            for q in range(2 * TT):
                ple_out(q)

            def pair(n, g, s, h, last):
                act.wait_ge(up_done, n + 1)
                wait(act, hid_ready, n - 1)
                act.activation(sil[:, s, :], pb[2 + s][:, 0:F], ACT.Silu).then_inc(sil_ready, 1)
                act.wait_ge(hidT_full, n + 1)
                wait(act, down_done[s], h)
                act.activation(hidT[:, s], pb[4 + s][:, 0:F].rearrange("p (k t) -> p k t", k=FK), ACT.Copy).then_inc(hidT_ready, 1)
                act.wait_ge(down_done[s], h + 1)
                wait(act, y_stored[s], 16 * h)
                act.activation(yb[:, s, 0:512], pb[6][:], ACT.Copy).then_inc(ya_ready, 1)

            expert_rounds(act, lambda r, first: expert_pairs(act, r, first, pair), lambda r: None)

            for t in range(TT):
                act.wait_ge(x2_ready, 2 * (t + 1))
                mean_root(2, t, junk)
            for q in range(2 * TT):
                banks.wait_full(act, ("pgate", q))
                if q >= 4:
                    act.wait_ge(x3_ready, 2 * (q - 3))
                emptied(act.activation(sgate[:, q % 4, :], bk(("pgate", q))[:], ACT.Sigmoid), ("pgate", q))
            for t in range(TT):
                act.wait_ge(x3_ready, 4 * (t + 1))
                mean_root(3, t, junk)

        @block.vector
        def _(dve):
            dve.memset(ones[:], 1.0).then_inc(pads_set, 1)
            dve.memset(mean_w[:], 1.0 / CH).then_inc(pads_set, 1)
            dve.memset(u[:, :, 0:TAPS - 1], 0.0).then_inc(pads_set, 1)
            rsn = [0]

            def recip(out_ap, in_ap):
                dve.reciprocal(out_ap, in_ap).then_inc(rs_ready, 1)
                rsn[0] += 1
                dve.wait_ge(rs_ready, rsn[0])

            def permuted(ap):
                return ap.rearrange("p (n k) -> p k n", k=DK)

            def inverse(which, t):
                dve.wait_ge(root_ready, 2 * (which * TT + t) + 2)
                recip(rs[:, which, t:t + 1], ss[:, which, t:t + 1])

            def normal_rows(which, t):
                inverse(which, t)
                dve.tensor_scalar(xn[:, t], permuted(xs[:, t, :]), rs[:, which, t:t + 1], None, ALU.mult).then_inc(xn_ready, 1)

            for t in range(TT):
                normal_rows(0, t)
            dve.wait_ge(prm_loaded, 32)
            for k in range(0, DK, 2):
                banks.wait_full(dve, ("x", k))
                emptied(dve.tensor_scalar(hT[:, k, :], bk(("x", k))[:], pr[:, Q_MIX + k:Q_MIX + k + 1], None, ALU.mult), ("x", k))
            taps = [0]

            def glu(m):
                banks.wait_full(dve, ("val", m))
                banks.wait_emptied(dve, ("gate", m))
                if m == 0:
                    dve.wait_ge(pads_set, 3)
                emptied(dve.tensor_tensor(u[:, m, TAPS - 1:U], bk(("val", m))[:], sg[:, m, :], ALU.mult), ("val", m))

            def tap(m, j):
                for mm in (m, m + 1):
                    w = pr[:, mm * PM + j:mm * PM + j + 1]
                    if j == 0:
                        ins = dve.tensor_scalar(mixc[:, mm, :], u[:, mm, 0:S], w, pr[:, mm * PM + TAPS:mm * PM + TAPS + 1],
                                                ALU.mult, ALU.add)
                    else:
                        dve.wait_ge(tap_done, taps[0] - 1)
                        ins = dve.scalar_tensor_tensor(out=mixc[:, mm, :], in0=u[:, mm, j:j + S], scalar=w,
                                                       in1=mixc[:, mm, :], op0=ALU.mult, op1=ALU.add)
                    ins.then_inc(tap_done, 1)
                    taps[0] += 1

            def turn(j):
                banks.wait_full(dve, ("rot", j))
                if j >= 2:
                    dve.wait_ge(rope_done, 2 * (j - 1) if j <= CM else CM + j - 1)
                emptied(dve.tensor_tensor(qsin[:, j % 2, :], bk(("rot", j))[:], c[:, C_SIN:C_SIN + S], ALU.mult), ("rot", j))

            glu(0)
            glu(1)
            banks.wait_emptied(dve, ("val", 1))
            for j in range(TAPS):
                tap(0, j)
                if j == 12:
                    glu(2)
                if j == 22:
                    glu(3)
            banks.wait_emptied(dve, ("val", 3))
            done = 0
            for j in range(TAPS):
                tap(2, j)
                if j % 5 == 4 and done < 6:
                    turn(done)
                    done += 1
            for j in range(done, 2 * CM):
                turn(j)
            banks.wait_full(dve, "mean")
            for m in range(CM):
                ins = dve.tensor_tensor(mixc[:, m, :], mixc[:, m, :], bk("mean")[:], ALU.subtract)
            emptied(ins, "mean")
            banks.wait_emptied(dve, "var")
            dve.reciprocal(lnr[:], lnr[:]).then_inc(lnr_ready, 1)
            dve.wait_ge(lnr_ready, 1)
            dve.wait_ge(csq_ready, CM)
            for m in range(CM):
                dve.tensor_tensor(mixc[:, m, :], mixc[:, m, :], lnr[:], ALU.mult).then_inc(z_ready, 1)

            def scores(u_):
                i, b = u_ % TT, u_ % 2
                n = P * (i + 1)
                for hh in range(2):
                    banks.wait_full(dve, ("score", u_, hh))
                    if u_ >= 2 and hh == 0:
                        banks.wait_full(dve, ("probT", u_ - 2, 1))
                    ins = nc.vector.tensor_tensor_reduce(out=prob[:, b, hh, 0:n], in0=bk(("score", u_, hh))[:, 0:n],
                                                         in1=c[:, C_MASK + S - n:C_MASK + S], scale=-1.0 / 8, scalar=FAR,
                                                         op0=ALU.add, op1=ALU.min, accum_out=nmax[:, b, hh:hh + 1])
                    emptied(ins, ("score", u_, hh))

            def normalise(u_):
                i, b = u_ % TT, u_ % 2
                n = P * (i + 1)
                dve.wait_ge(exp_ready, 2 * u_ + 2)
                dve.reciprocal(pinv[:, b, :], psum_p[:, b, :]).then_inc(pinv_ready, 1)
                dve.wait_ge(pinv_ready, u_ + 1)
                for hh in range(2):
                    dve.tensor_scalar(prob[:, b, hh, 0:n], prob[:, b, hh, 0:n], pinv[:, b, hh:hh + 1], None,
                                      ALU.mult).then_inc(prob_ready, 1)

            def attn_out(m):
                dve.wait_ge(sqa_ready, m + 1)
                emptied(dve.tensor_scalar(mixa[:, m, :], bk(("attn", m))[:], pr[:, Q_BETA + m:Q_BETA + m + 1], None,
                                          ALU.mult), ("attn", m))

            banks.wait_full(dve, "conv_sq")
            emptied(dve.tensor_copy(gsq[:], bk("conv_sq")[:, 0:TT]), "conv_sq")
            units = CM * TT
            for u_ in range(units + 1):
                if u_ < units:
                    scores(u_)
                if u_ >= 1:
                    normalise(u_ - 1)
                    if (u_ - 1) % TT == 1 and u_ - 1 > TT:
                        attn_out((u_ - 1) // TT - 1)
            attn_out(CM - 1)
            dve.wait_ge(groot_ready, 1)
            recip(grs[:, 0, :], gss[:, 0, :])
            banks.wait_emptied(dve, "attn_sq")
            recip(grs[:, 1, :], gss[:, 1, :])

            def add_scaled(name, w, t, half):
                cols = xs[:, t, half * 512:(half + 1) * 512]
                emptied(dve.scalar_tensor_tensor(out=cols, in0=bk(name)[:], scalar=grs[:, w, t:t + 1], in1=cols,
                                                 op0=ALU.mult, op1=ALU.add), name)
                banks.wait_emptied(dve, name)

            def columns_out(kind, t, gains):
                for kh in range(2):
                    name = (kind, t, kh)
                    banks.wait_full(dve, name)
                    emptied(dve.tensor_tensor(
                        hT[:, 4 * kh:4 * kh + 4, t * P:(t + 1) * P], bk(name)[:].rearrange("p (k n) -> p k n", k=4),
                        pr[:, gains + 4 * kh:gains + 4 * kh + 4].rearrange("p (k n) -> p k n", n=1).broadcast_to([P, 4, P]),
                        ALU.mult), name)

            for q in range(2 * TT):
                t, half = q // 2, q % 2
                banks.wait_full(dve, ("outc", q))
                add_scaled(("outc", q), 0, t, half)
                banks.wait_full(dve, ("outa", q))
                add_scaled(("outa", q), 1, t, half)
                if half == 0 and t >= 1:
                    normal_rows(1, t - 1)
                if half == 1 and t >= 2:
                    columns_out("h2", t - 2, Q_FFN)
            normal_rows(1, TT - 1)
            columns_out("h2", TT - 2, Q_FFN)
            columns_out("h2", TT - 1, Q_FFN)

            n = [0]

            def step(ins):
                n[0] += 1
                ins.then_inc(rstep, 1)
                dve.wait_ge(rstep, n[0])

            def wide(ap, k):
                return ap.rearrange("p (t n) -> p t n", n=1).broadcast_to([P, TT, k])

            def table(col, k):
                return c[:, col:col + k].rearrange("p (a n) -> p a n", a=1).broadcast_to([P, TT, k])

            def first_hot(out_ap, in_ap, top, scratch, weights, k):
                step(dve.tensor_tensor(scratch, in_ap, wide(top, k), ALU.is_equal))
                step(dve.tensor_tensor(scratch, scratch, table(weights, k), ALU.mult))
                step(dve.tensor_reduce(sm[:, 0, :], scratch, AX.X, ALU.max))
                step(dve.tensor_tensor(out_ap, scratch, wide(sm[:, 0, :], k), ALU.is_equal))

            banks.wait_full(dve, "logit")
            emptied(dve.tensor_copy(lg[:], bk("logit")[:, 0:TT * NR].rearrange("p (t n) -> p t n", t=TT)), "logit")
            banks.wait_emptied(dve, "logit")
            grp = lg[:, :, 0:NG]
            step(dve.tensor_reduce(sm[:, 1, :], grp, AX.X, ALU.max))
            dve.tensor_tensor(rt[:, 0, :, 0:NG], grp, wide(sm[:, 1, :], NG), ALU.subtract).then_inc(exp_in, 1)
            first_hot(rt[:, 1, :, 0:NG], grp, sm[:, 1, :], rt[:, 2, :, 0:NG], C_GRP, NG)
            step(dve.tensor_scalar(rt[:, 2, :, 0:NG], rt[:, 1, :, 0:NG], -1.0, FAR, ALU.add, ALU.mult))
            for t in range(TT):
                ins = dve.tensor_tensor(
                    rt[:, 3, t, :].rearrange("p (g e) -> p g e", g=NG), lg[:, t, NG:NR].rearrange("p (g e) -> p g e", g=NG),
                    rt[:, 2, t, 0:NG].rearrange("p (g e) -> p g e", e=1).broadcast_to([P, NG, EG]), ALU.add)
            step(ins)
            step(dve.tensor_reduce(sm[:, 2, :], rt[:, 3], AX.X, ALU.max))
            first_hot(hot[:, 0], rt[:, 3], sm[:, 2, :], rt[:, 4], C_RANK, NE)
            step(dve.tensor_scalar(rt[:, 4], hot[:, 0], -FAR, None, ALU.mult))
            step(dve.tensor_tensor(rt[:, 5], rt[:, 3], rt[:, 4], ALU.add))
            step(dve.tensor_reduce(sm[:, 3, :], rt[:, 5], AX.X, ALU.max))
            first_hot(hot[:, 1], rt[:, 5], sm[:, 3, :], rt[:, 4], C_RANK, NE)
            dve.tensor_tensor(rt[:, 6], hot[:, 0], hot[:, 1], ALU.add).then_inc(chosen, 1)
            dve.tensor_tensor(sm[:, 6, :], sm[:, 3, :], sm[:, 2, :], ALU.subtract).then_inc(exp_in, 1)
            for k in range(2):
                step(dve.tensor_tensor(rt[:, 5], hot[:, k], table(C_PAR, NE), ALU.mult))
                dve.tensor_reduce(sm[:, 10 + k, :], rt[:, 5], AX.X, ALU.add).then_inc(rstep, 1)
                n[0] += 1
                for t in range(TT):
                    ins = dve.tensor_reduce(pairhot[:, 2 * t + k, :], hot[:, k, t, :].rearrange("p (g e) -> p g e", e=2), AX.X, ALU.add)
                step(ins)
            for k in range(2):
                dve.tensor_tensor(numhot[:, k::2, 0, :], pairhot[:, k::2, :], wide(c[:, C_TOK:C_TOK + TT], PAIRS),
                                  ALU.mult).then_inc(rstep, 1)
                n[0] += 1
            step(dve.tensor_tensor(numhot[:, :, 1, :], pairhot[:], c[:, C_ROW:C_ROW + 2 * TT].rearrange("p (j n) -> p j n", n=1)
                                   .broadcast_to([P, 2 * TT, PAIRS]), ALU.mult))
            banks.wait_full(dve, "rank")
            for k in range(2):
                ins = dve.tensor_tensor(rt[:, 4 + k], hot[:, k], bk("rank")[:, 0:TT * NE].rearrange("p (t n) -> p t n", t=TT), ALU.mult)
                if k == 0:
                    step(ins)
                else:
                    emptied(ins, "rank")
                    banks.wait_emptied(dve, "rank")
                step(dve.tensor_reduce(sm[:, 12 + k, :], rt[:, 4 + k], AX.X, ALU.add))
            banks.wait_full(dve, "count")
            emptied(dve.tensor_reduce(cmax[:, 0:1], bk("count")[:, 0:NE], AX.X, ALU.max), "count")
            banks.wait_emptied(dve, "count")
            step(dve.tensor_scalar(over[:, 0:7], c[:, C_THR:C_THR + 7], cmax[:, 0:1], None, ALU.is_lt))
            step(dve.tensor_reduce(cmax[:, 1:2], over[:, 0:7], AX.X, ALU.add))
            dve.tensor_scalar(rounds[:], cmax[:, 1:2], 1.0, None, ALU.add).then_inc(rounds_ready, 1)

            def list_inputs(step):
                for k in range(2):
                    step(dve.tensor_scalar(sm[:, 16, :], sm[:, 12 + k, :], 0.0, None, ALU.is_lt))
                    step(dve.tensor_scalar(sm[:, 17, :], sm[:, 12 + k, :], float(CAP), None, ALU.is_ge))
                    step(dve.tensor_tensor(sm[:, 16, :], sm[:, 16, :], sm[:, 17, :], ALU.add))
                    step(dve.scalar_tensor_tensor(out=sm[:, 18, :], in0=sm[:, 10 + k, :], scalar=float(CAP),
                                                  in1=sm[:, 12 + k, :], op0=ALU.mult, op1=ALU.add))
                    step(dve.scalar_tensor_tensor(out=slot[:, :, k], in0=sm[:, 16, :], scalar=4.0 * S, in1=sm[:, 18, :],
                                                  op0=ALU.mult, op1=ALU.add))
                dve.tensor_tensor(
                    onehot, c[:, C_IOTA:C_IOTA + P].rearrange("p (a n) -> p a n", a=1).broadcast_to([P, 2 * TT, P]),
                    slot[:].rearrange("p t k -> p (t k)").rearrange("p (j n) -> p j n", n=1).broadcast_to([P, 2 * TT, P]),
                    ALU.is_equal).then_inc(list_in, 1)

            def list_out():
                dve.tensor_copy(tlist[:, 0, :], pb[0][:, 0:PAIRS])
                dve.tensor_scalar(tlist[:, 1, :], pb[0][:, PAIRS:2 * PAIRS], -1.0, float(NOWHERE), ALU.mult,
                                  ALU.add).then_inc(list_ready, 1)

            list_inputs(step)
            dve.wait_ge(list_full, 1)
            list_out()
            dve.wait_ge(exp_out, 2)
            step(dve.tensor_reduce(sm[:, 4, :], rt[:, 0, :, 0:NG], AX.X, ALU.add))
            step(dve.tensor_scalar(sm[:, 5, :], sm[:, 6, :], 1.0, None, ALU.add))
            step(dve.tensor_tensor(sm[:, 4, :], sm[:, 4, :], sm[:, 5, :], ALU.mult))
            step(dve.reciprocal(sm[:, 20, :], sm[:, 4, :]))
            step(dve.tensor_tensor(sm[:, 21, :], sm[:, 20, :], sm[:, 6, :], ALU.mult))

            def x_out(n_, s):
                dve.wait_ge(xgT_full, n_ + 1)
                wait(dve, up_done, n_ - 1)
                for kh in range(2):
                    dve.tensor_tensor(
                        xgT[:, s, 4 * kh:4 * kh + 4, :], pb[kh][:].rearrange("p (k n) -> p k n", k=4),
                        pr[:, Q_FFN + 4 * kh:Q_FFN + 4 * kh + 4].rearrange("p (k n) -> p k n", n=1).broadcast_to([P, 4, P]),
                        ALU.mult).then_inc(xgT_ready, 1)

            def pair(n_, g, s, h, last):
                dve.wait_ge(sil_ready, n_ + 1)
                wait(dve, hidT_full, n_ - 1)
                dve.tensor_tensor(hid[:, s], sil[:, s, :].rearrange("p (n k) -> p k n", k=FK),
                                  pb[2 + s][:, F:2 * F].rearrange("p (n k) -> p k n", k=FK), ALU.mult).then_inc(hid_ready, 1)
                if not last:
                    x_out(n_ + 1, 1 - s)
                dve.wait_ge(down_done[s], h + 1)
                wait(dve, y_stored[s], 16 * h)
                dve.tensor_copy(yb[:, s, 512:D], pb[7][:]).then_inc(yd_ready, 1)

            def one_round(r, first):
                x_out(r * PAIRS, 0)
                expert_pairs(dve, r, first, pair)

            nb = n[0]

            def between(r):
                for k in range(2):
                    dve.tensor_scalar(sm[:, 12 + k, :], sm[:, 12 + k, :], -float(CAP), None, ALU.add).then_inc(rstep, 1)
                base = nb + (r - 1) * 12
                m = [2]
                dve.wait_ge(rstep, base + 2)

                def rs_step(ins):
                    m[0] += 1
                    ins.then_inc(rstep, 1)
                    dve.wait_ge(rstep, base + m[0])

                list_inputs(rs_step)
                dve.wait_ge(list_full, r + 1)
                dve.wait_ge(ycur_ready, r * PAIRS)
                list_out()

            expert_rounds(dve, one_round, between)

            for t in range(TT):
                dve.wait_ge(yg_loaded[t], 16)
                for k in range(2):
                    dve.scalar_tensor_tensor(out=xs[:, t, :], in0=yg[:, 2 * t + k, :], scalar=sm[:, 20 + k, t:t + 1],
                                             in1=xs[:, t, :], op0=ALU.mult, op1=ALU.add).then_inc(x2_ready, 1)
                    dve.wait_ge(x2_ready, 2 * t + k + 1)
            for t in range(TT + 1):
                if t < TT:
                    normal_rows(2, t)
                if t >= 1:
                    columns_out("h3", t - 1, Q_PLE)
            x3 = 0
            for q in range(2 * TT):
                t, half = q // 2, q % 2
                name = ("pgate", q)
                cols = slice(half * 512, (half + 1) * 512)
                banks.wait_emptied(dve, name)
                dve.tensor_tensor(sgate[:, q % 4, :], sgate[:, q % 4, :], plep[:, t, cols], ALU.mult).then_inc(x3_ready, 1)
                x3 += 1
                dve.wait_ge(x3_ready, x3)
                dve.tensor_tensor(xs[:, t, cols], xs[:, t, cols], sgate[:, q % 4, :], ALU.add).then_inc(x3_ready, 1)
                x3 += 1
            dve.wait_ge(last_loaded, 32)
            for t in range(TT):
                inverse(3, t)
                dve.scalar_tensor_tensor(out=xn_rows[:, t, :], in0=xs[:, t, :], scalar=rs[:, 3, t:t + 1], in1=gfin,
                                         op0=ALU.mult, op1=ALU.mult).then_inc(o_ready, 1)

        @block.tensor
        def _(pe):
            pe.wait_ge(const_loaded, 32)
            pe.wait_ge(xn_ready, TT)
            for k in range(DK):
                for t in range(TT):
                    ins = pe.transpose(bk(("x", k))[:, t * P:(t + 1) * P], xn[:, t, k, :], ident)
                filled(ins, ("x", k))
            for k in range(DK):
                banks.wait_emptied(pe, ("x", k))

            def project(name, chunk, m):
                banks.wait_free(pe, name)
                for k in range(DK):
                    ins = pe.matmul(bk(name)[:], win[chunk][:, k, m * P:(m + 1) * P], hT[:, k, :],
                                    start=(k == 0), stop=(k == DK - 1))
                filled(ins, name)

            for m in range(CM):
                for i, name in enumerate(("val", "gate")):
                    pe.wait_ge(win_loaded[i], 16)
                    project((name, m), i, m)

            def rotate(j):
                banks.wait_free(pe, ("rot", j))
                banks.wait_emptied(pe, ("raw", j))
                filled(pe.matmul(bk(("rot", j))[:], c[:, C_ROT:C_ROT + P], qraw[:, j % 2, :], start=True, stop=True), ("rot", j))

            for j in range(2 * CM + 1):
                if j < 2 * CM:
                    pe.wait_ge(win_loaded[2 + j // CM], 16)
                    project(("raw", j), 2 + j // CM, j % CM)
                if j >= 1:
                    rotate(j - 1)

            def channel_sum(name, src):
                banks.wait_free(pe, name)
                for t in range(TT):
                    for m in range(CM):
                        ins = pe.matmul(bk(name)[:, t:t + 1], src[:, m, t * P:(t + 1) * P], ones[:, 0:1],
                                        start=(m == 0), stop=(m == CM - 1))
                filled(ins, name)

            pe.wait_ge(win_loaded[4], 16)
            pe.wait_ge(tap_done, CM * TAPS)
            banks.wait_free(pe, "mean")
            for m in range(CM):
                ins = pe.matmul(bk("mean")[:], mean_w[:], mixc[:, m, :], start=(m == 0), stop=(m == CM - 1))
            filled(ins, "mean")

            def values(t):
                banks.wait_free(pe, ("v", t))
                for k in range(DK):
                    ins = pe.matmul(bk(("v", t))[:], hT[:, k, t * P:(t + 1) * P], win[4][:, k, :],
                                    start=(k == 0), stop=(k == DK - 1))
                filled(ins, ("v", t))

            values(0)
            banks.wait_free(pe, "var")
            pe.wait_ge(csq_ready, CM)
            for m in range(CM):
                ins = pe.matmul(bk("var")[:], mean_w[:], sqc[:, m, :], start=(m == 0), stop=(m == CM - 1))
            filled(ins, "var")
            for t in range(1, TT):
                values(t)
            pe.wait_ge(osq_ready, CM)
            channel_sum("conv_sq", sqc)

            pe.wait_ge(qz_set, 2)
            pe.wait_ge(rope_done, 3 * CM)

            def score(u_):
                m, i = u_ // TT, u_ % TT
                n = P * (i + 1)
                for hh in range(2):
                    name = ("score", u_, hh)
                    banks.wait_free(pe, name)
                    filled(pe.matmul(bk(name)[:, 0:n], qz[:, 2 * m + hh, i * P:(i + 1) * P], kT[:, m, 0:n],
                                     start=True, stop=True), name)

            def transpose_probs(u_):
                m, i, b = u_ // TT, u_ % TT, u_ % 2
                for hh in range(2):
                    name = ("probT", u_, hh)
                    pe.wait_ge(prob_ready, 2 * u_ + hh + 1)
                    banks.wait_free(pe, name)
                    for j in range(i + 1):
                        ins = pe.transpose(bk(name)[:, j * P:(j + 1) * P], prob[:, b, hh, j * P:(j + 1) * P], ident)
                    filled(ins, name)

            def attend(u_):
                m, i, b = u_ // TT, u_ % TT, u_ % 2
                name = ("attn", m)
                if i == 0:
                    banks.wait_free(pe, name)
                for hh in range(2):
                    pt = ("probT", u_, hh)
                    banks.wait_emptied(pe, pt)
                for j in range(i + 1):
                    for hh in range(2):
                        ins = pe.matmul(bk(name)[hh * DH:(hh + 1) * DH, i * P:(i + 1) * P],
                                        vr[:, j, (2 * m + hh) * DH:(2 * m + hh + 1) * DH],
                                        probT[:, b, hh, j * P:(j + 1) * P], start=(j == 0), stop=(j == i))
                if i == TT - 1:
                    filled(ins, name)
                else:
                    ins.then_inc(attended, 1)

            for t in range(TT):
                banks.wait_emptied(pe, ("v", t))
            units = CM * TT
            for u_ in range(units + 2):
                if u_ < units:
                    score(u_)
                if 1 <= u_ <= units:
                    transpose_probs(u_ - 1)
                if u_ >= 2:
                    attend(u_ - 2)
            pe.wait_ge(sqa_ready, CM)
            channel_sum("attn_sq", sqa)

            def out_part(name, t, half, src, w):
                banks.wait_free(pe, name)
                for m in range(CM):
                    ins = pe.matmul(bk(name)[:], src[:, m, t * P:(t + 1) * P], w[:, m, half * 512:(half + 1) * 512],
                                    start=(m == 0), stop=(m == CM - 1))
                filled(ins, name)

            def turn_rows(kind, t, first):
                pe.wait_ge(xn_ready, first + t + 1)
                for kh in range(2):
                    name = (kind, t, kh)
                    banks.wait_free(pe, name)
                    for k in range(4):
                        ins = pe.transpose(bk(name)[:, k * P:(k + 1) * P], xn[:, t, 4 * kh + k, :], ident)
                    filled(ins, name)

            pe.wait_ge(woc_loaded, 16)
            pe.wait_ge(woa_loaded, 16)
            pe.wait_ge(mixc_ready, CM)
            banks.wait_emptied(pe, ("attn", CM - 1))
            for q in range(2 * TT):
                t, half = q // 2, q % 2
                out_part(("outc", q), t, half, mixc, woc)
                out_part(("outa", q), t, half, mixa, woa)
                if half == 1 and t >= 1:
                    turn_rows("h2", t - 1, TT)
            turn_rows("h2", TT - 1, TT)

            for kh in range(2):
                name = ("h2", TT - 1, kh)
                banks.wait_emptied(pe, name)
            banks.wait_free(pe, "logitT")
            for k in range(DK):
                ins = pe.matmul(bk("logitT")[0:NR, :], wr[:, k, :], hT[:, k, :], start=(k == 0), stop=(k == DK - 1))
            filled(ins, "logitT")

            def ple(q):
                t, half = q // 2, q % 2
                banks.wait_free(pe, ("ple", q))
                for k in range(PK):
                    ins = pe.matmul(bk(("ple", q))[:], pTs[:, k, t * P:(t + 1) * P], wpp[:, k, half * 512:(half + 1) * 512],
                                    start=(k == 0), stop=(k == PK - 1))
                filled(ins, ("ple", q))

            pe.wait_ge(ple_loaded, 32)
            ple(0)
            banks.wait_emptied(pe, "logitT")
            banks.wait_free(pe, "logit")
            for t in range(TT):
                ins = pe.transpose(bk("logit")[:, t * NR:(t + 1) * NR], logT[:, t * P:(t + 1) * P], ident[0:NR, 0:NR])
            filled(ins, "logit")
            for q in range(1, 4):
                ple(q)
            pe.wait_ge(chosen, 1)
            banks.wait_free(pe, "rank")
            for t in range(TT):
                for j in range(t + 1):
                    ins = pe.matmul(bk("rank")[:, t * NE:(t + 1) * NE], ones[:] if j < t else c[:, C_UP:C_UP + P],
                                    rt[:, 6, j, :], start=(j == 0), stop=(j == t))
            filled(ins, "rank")
            banks.wait_free(pe, "count")
            for t in range(TT):
                ins = pe.matmul(bk("count")[:, 0:NE], ones[:], rt[:, 6, t, :], start=(t == 0), stop=(t == TT - 1))
            filled(ins, "count")
            for q in range(4, 2 * TT):
                ple(q)

            def token_list(bank):
                for j in range(2 * TT):
                    ins = pe.matmul(bank[:, 0:2 * PAIRS], onehot[:, j, :], numhot[:, j].rearrange("p a g -> p (a g)"),
                                    start=(j == 0), stop=(j == 2 * TT - 1))
                return ins

            pe.wait_ge(list_in, 1)
            token_list(pb[0]).then_inc(list_full, 1)

            def turn_tokens(n, s, h):
                if isinstance(n, int) and n == 0:
                    pe.wait_ge(list_ready, 1)
                else:
                    pe.wait_ge(xgT_ready, 2 * n)
                pe.wait_ge(gathered[s], 16 * h + 16)
                for k in range(DK):
                    ins = pe.transpose(pb[k // 4][:, k % 4 * P:(k % 4 + 1) * P], xg[:, s, k * P:(k + 1) * P], ident)
                ins.then_inc(xgT_full, 1)

            def pair(n, g, s, h, last):
                pe.wait_ge(xgT_ready, 2 * (n + 1))
                wait(pe, hid_ready, n - 1)
                for a in range(2):
                    pe.wait_ge(up_loaded[s][a], 32 * h + 32)
                for k in range(DK):
                    for a in range(2):
                        ins = pe.matmul(pb[2 + s][a * CAP:(a + 1) * CAP, :], xgT[:, s, k, a * CAP:(a + 1) * CAP],
                                        up_w[s][a][:, :, k, :], start=(k == 0), stop=(k == DK - 1))
                ins.then_inc(up_done, 1)
                if not last:
                    turn_tokens(n + 1, 1 - s, h + s)
                pe.wait_ge(hid_ready, n + 1)
                wait(pe, hidT_ready, n - 1)
                for k in range(FK):
                    ins = pe.transpose(pb[4 + s][:, k * P:(k + 1) * P], hid[:, s, k, :], ident)
                ins.then_inc(hidT_full, 1)
                pe.wait_ge(hidT_ready, n + 1)
                wait(pe, ya_ready, n)
                wait(pe, yd_ready, n)
                for a in range(2):
                    pe.wait_ge(dn_loaded[s][a], 16 * h + 16)
                for half in range(2):
                    for k in range(FK):
                        for a in range(2):
                            ins = pe.matmul(pb[6 + half][a * CAP:(a + 1) * CAP, :], hidT[:, s, k, a * CAP:(a + 1) * CAP],
                                            dn_w[s][a][:, k, half * 512:(half + 1) * 512], start=(k == 0), stop=(k == FK - 1))
                ins.then_inc(down_done[s], 1)

            def one_round(r, first):
                if first:
                    pe.wait_ge(rounds_ready, 1)
                    for q in range(4, 2 * TT):
                        banks.wait_emptied(pe, ("ple", q))
                turn_tokens(r * PAIRS, 0, r * (PAIRS // 2))
                expert_pairs(pe, r, first, pair)

            def between(r):
                pe.wait_ge(list_in, r + 1)
                pe.wait_ge(xgT_ready, 2 * PAIRS * r)
                token_list(pb[0]).then_inc(list_full, 1)
                pe.wait_ge(list_ready, r + 1)

            total = expert_rounds(pe, one_round, between)
            pe.wait_ge(ya_ready, total * PAIRS)
            pe.wait_ge(yd_ready, total * PAIRS)

            def gate(q):
                t, half = q // 2, q % 2
                name = ("pgate", q)
                banks.wait_free(pe, name)
                for k in range(DK):
                    pe.matmul(bk(name)[:], hT[:, k, t * P:(t + 1) * P], wpg[:, k, half * 512:(half + 1) * 512],
                              start=(k == 0), stop=False)
                filled(pe.matmul(bk(name)[:], ones[0:1, :], brow[:, half * 512:(half + 1) * 512], start=False, stop=True), name)

            for t in range(TT + 1):
                if t < TT:
                    turn_rows("h3", t, 2 * TT)
                if t == 0:
                    pe.wait_ge(pg_loaded, 16 * DK // 2)
                    pe.wait_ge(last_loaded, 32)
                if t >= 1:
                    for kh in range(2):
                        name = ("h3", t - 1, kh)
                        banks.wait_emptied(pe, name)
                    gate(2 * (t - 1))
                    gate(2 * t - 1)


def kernel(x, p, g_mix, w_in, w_dw, b_dw, conv_ln_g, conv_ln_b, beta_conv, beta_attn, w_out, g_ffn, w_group, b_group,
           w_erouter, b_erouter, w_gate, w_up, w_down, g_ple, w_ple_gate, b_ple_gate, w_ple_proj, g_final):
    import concourse.bacc as bacc
    from concourse.bass_utils import run_bass_kernel_spmd

    a = np.asarray
    by_channel = np.concatenate([a(w_dw)[0].T, a(b_dw)[0][:, None], a(conv_ln_g)[0][:, None], a(conv_ln_b)[0][:, None],
                                 a(beta_conv)[0][:, None]], axis=1).reshape(CM, P, PM)
    router_bias = np.concatenate([a(b_group)[0], a(b_erouter)[0].reshape(NE), np.zeros(P - NR, np.float32)])
    prm = np.concatenate([by_channel.transpose(1, 0, 2).reshape(P, CM * PM), a(beta_attn)[0].reshape(CM, P).T,
                          a(g_mix)[0].reshape(P, DK), a(g_ffn)[0].reshape(P, DK), a(g_ple)[0].reshape(P, DK),
                          router_bias[:, None]], axis=1)
    w_r = np.concatenate([a(w_group)[0], a(w_erouter)[0].transpose(1, 0, 2).reshape(D, NE)], axis=1)
    arrays = {
        "x_in": a(x)[0], "w_in_in": a(w_in)[0], "w_out_in": a(w_out)[0], "w_r_in": w_r, "w_gate_in": a(w_gate)[0],
        "w_up_in": a(w_up)[0], "w_down_in": a(w_down)[0], "w_pg_in": a(w_ple_gate)[0], "w_pp_in": a(w_ple_proj)[0],
        "pT_in": a(p)[0, 0].T, "b_pg_in": a(b_ple_gate), "g_final_in": a(g_final), "prm_in": prm, "cst_in": constants(),
    }
    arrays = {name: np.ascontiguousarray(v) for name, v in arrays.items()}
    nc = bacc.Bacc("TRN2", target_bir_lowering=False, num_devices=1)
    args = [nc.dram_tensor(name, v.shape, mybir.dt.from_np(v.dtype), kind="ExternalInput").ap() for name, v in arrays.items()]
    out = nc.dram_tensor("out_rows", (S, D), F32, kind="ExternalOutput").ap()
    build(nc, *args, out)
    result = run_bass_kernel_spmd(nc, [arrays], core_ids=[0])
    return result.results[0]["out_rows"].reshape(1, S, D)
```

```python
from contextlib import ExitStack

import concourse.bass as bass
import concourse.mybir as mybir
import numpy as np

F32 = mybir.dt.float32
I32 = mybir.dt.int32
ALU = mybir.AluOpType
ACT = mybir.ActivationFunctionType
AX = mybir.AxisListType

P = 128
D = 1024
S = 512
TT = S // P
DK = D // P
CH = 512
CM = CH // P
NH = 8
DH = 64
TAPS = 31
EPS = 1e-6
NG, NE, EG = 4, 32, 8
NR = NG + NE
F = 256
FK = F // P
CAP = 64
PAIRS = NE // 2
MORE = 2 * S // CAP
ITERS = MORE // 4
ALLP = PAIRS + 2 * ITERS + 2
PD = 256
PK = PD // P
NOWHERE = 4 * S
FAR = 3.0e38
ROT, THETA = 16, 500000.0

C_ID, C_UP, C_ROT, C_IOTA = 0, P, 2 * P, 3 * P
C_MASK = 4 * P
C_COS = C_MASK + S
C_SIN = C_COS + S
C_RANK = C_SIN + S
C_EXP = C_RANK + NE
C_GRP = C_EXP + NE
C_TOK = C_GRP + NG
C_ROW = C_TOK + 2 * TT
C_THR = C_ROW + 2 * TT
C_TWO = C_THR + 7
C_FOUR = C_TWO + ALLP - 1
C_EPS = C_FOUR + ITERS
C_END = C_EPS + 1
PM = TAPS + 4
Q_BETA = CM * PM
Q_MIX, Q_FFN, Q_PLE = Q_BETA + CM, Q_BETA + CM + DK, Q_BETA + CM + 2 * DK
Q_RB = Q_BETA + CM + 3 * DK
Q_END = Q_RB + 1


def constants():
    c = np.zeros((P, C_END), np.float32)
    i = np.arange(P)
    c[:, C_ID:C_ID + P] = np.eye(P)
    c[:, C_UP:C_UP + P] = i[:, None] < i[None, :]
    for m in range(P):
        d = m % DH
        if d < ROT // 2:
            c[m + ROT // 2, C_ROT + m] = -1.0
        elif d < ROT:
            c[m - ROT // 2, C_ROT + m] = 1.0
    c[:, C_IOTA:C_IOTA + P] = i[None, :]
    c[:, C_MASK + S - P:C_MASK + S] = np.where(i[None, :] <= i[:, None], 0.0, -FAR)
    inv = np.power(np.float32(THETA), -np.arange(0, ROT, 2, dtype=np.float32) / np.float32(ROT))
    ang = np.arange(S, dtype=np.float32)[:, None] * inv[None, :]
    d = i % DH
    turned = d < ROT
    c[:, C_COS:C_COS + S] = np.where(turned[:, None], np.cos(ang).T[d % (ROT // 2)], 1.0)
    c[:, C_SIN:C_SIN + S] = np.where(turned[:, None], np.sin(ang).T[d % (ROT // 2)], 0.0)
    e = np.arange(NE)
    c[:, C_RANK:C_RANK + NE] = NE - e
    c[:, C_EXP:C_EXP + NE] = e
    c[:, C_GRP:C_GRP + NG] = NG - np.arange(NG)
    tok = i[:, None] + P * np.arange(TT)[None, :]
    c[:, C_TOK:C_TOK + 2 * TT] = np.tile(tok, (1, 2))
    c[:, C_ROW:C_ROW + 2 * TT] = NOWHERE - np.concatenate([tok, tok + S], axis=1)
    c[:, C_THR:C_THR + 7] = CAP * np.arange(1, 8)
    c[:, C_TWO:C_TWO + ALLP - 1] = 2 * np.arange(1, ALLP)
    c[:, C_FOUR:C_FOUR + ITERS] = 4 * np.arange(ITERS)
    c[:, C_EPS] = EPS
    return c


class Banks:

    def __init__(self, full, free):
        self.full, self.free = full, free
        self.place, self.count = {}, [0] * len(full)

    def use(self, name, bank):
        self.count[bank] += 1
        self.place[name] = (bank, self.count[bank])

    def bank(self, name):
        return self.place[name][0]

    def wait_full(self, eng, name):
        b, n = self.place[name]
        eng.wait_ge(self.full[b], n)

    def wait_free(self, eng, name):
        b, n = self.place[name]
        if n > 1:
            eng.wait_ge(self.free[b], n - 1)

    def wait_emptied(self, eng, name):
        b, n = self.place[name]
        eng.wait_ge(self.free[b], n)


def plan_banks(banks):
    for k in range(DK):
        banks.use(("x", k), k)
    for m in range(CM):
        banks.use(("val", m), m)
        banks.use(("gate", m), 4 + m)
    for j in range(2 * CM + 1):
        if j < 2 * CM:
            banks.use(("raw", j), j % 2)
        if j >= 1:
            banks.use(("rot", j - 1), 2 + (j - 1) % 2)
    banks.use("mean", 0)
    for t in range(TT):
        banks.use(("v", t), 4 + t)
        if t == 0:
            banks.use("var", 1)
    banks.use("conv_sq", 2)
    for u in range(CM * TT):
        for hh in range(2):
            banks.use(("score", u, hh), 2 * (u % 2) + hh)
        if u % TT == 0:
            banks.use(("attn", u // TT), 6 + u // TT % 2)
    for u in range(CM * TT):
        for hh in range(2):
            banks.use(("probT", u, hh), 4 + hh)
    banks.use("attn_sq", 6)
    for q in range(2 * TT):
        banks.use(("outc", q), 2 * (q % 3))
        banks.use(("outa", q), 2 * (q % 3) + 1)
    for t in range(TT):
        for kh in range(2):
            banks.use(("h2", t, kh), 6 + kh)
    banks.use("logitT", 0)
    banks.use("logit", 1)
    for q in range(2 * TT):
        banks.use(("ple", q), 4 + q % 4)
    banks.use("count", 3)
    banks.use("rank", 2)
    banks.use("base", 1)
    banks.use("items", 3)
    for t in range(TT):
        for kh in range(2):
            banks.use(("h3", t, kh), 2 * (t % 2) + kh)
    for q in range(2 * TT):
        banks.use(("pgate", q), 4 + q % 4)


def build(nc, x, w_in, w_out, w_r, w_gate, w_up, w_down, w_pg, w_pp, pT, b_pg, g_final, prm, cst, out):
    ctx = ExitStack()
    with ctx:
        def sb(name, shape, dt=F32):
            return ctx.enter_context(nc.sbuf_tensor(name, shape, dt))

        def sem(name):
            return ctx.enter_context(nc.semaphore(name))

        rows_d = nc.dram_tensor("rows_d", [S, D], F32).ap()
        y_d = nc.dram_tensor("y_d", [2 * S, D], F32).ap()

        xs = sb("xs", [P, TT, D])
        mix = sb("mix", [P, 2 * CM * S])
        wring = sb("wring", [P, 2, 2, 3 * 2048])
        arena = sb("arena", [P, 14592])
        c = sb("c", [P, C_END])
        ones = sb("ones", [P, P])
        pr = sb("pr", [P, Q_END])
        wr = sb("wr", [P, DK, NR])
        lnr = sb("lnr", [P, S])
        mean_w = sb("mean_w", [P, P])
        sq = sb("sq", [P, 4, TT])
        ss = sb("ss", [P, 4, TT])
        rs = sb("rs", [P, 4, TT])
        gsq = sb("gsq", [P, TT])
        gss = sb("gss", [P, 2, TT])
        grs = sb("grs", [P, 2, TT])
        nmax = sb("nmax", [P, 2, 2])
        psum_p = sb("psum_p", [P, 2, 2])
        pinv = sb("pinv", [P, 2, 2])
        lg = sb("lg", [P, TT, NR])
        rt = sb("rt", [P, 8, TT, NE])
        hot = sb("hot", [P, 2, TT, NE])
        sm = sb("sm", [P, 8, TT])
        by8 = sb("by8", [P, 14, 2 * TT])
        gw = sb("gw", [P, 2, TT])
        ecnt = sb("ecnt", [NE, 32])
        xb = sb("xb", [NE, P])
        ihot = sb("ihot", [NE, 3, MORE])
        fcnt = sb("fcnt", [P, 8])
        iters = sb("iters", [P, 1], I32)
        eid = sb("eid", [1, MORE], I32)
        tlist = sb("tlist", [P, 2, ALLP], I32)
        tcur = sb("tcur", [P, 2], I32)
        ycur = sb("ycur", [P, 2], I32)

        def ar(lo, n):
            return arena[:, lo:lo + n]

        ident = c[:, C_ID:C_ID + P]
        logT = lnr[0:NR, :]
        mixc = mix[:, 0:CM * S].rearrange("p (m t) -> p m t", m=CM)
        mixa = mix[:, CM * S:2 * CM * S].rearrange("p (m t) -> p m t", m=CM)
        plep = mix[:, :].rearrange("p (t n) -> p t n", t=TT)
        hT = ar(0, DK * S).rearrange("p (k t) -> p k t", k=DK)
        prob = ar(0, 2048).rearrange("p (b h k) -> p b h k", b=2, h=2)
        probT = ar(2048, 2048).rearrange("p (b h k) -> p b h k", b=2, h=2)
        xg = ar(0, 2 * D).rearrange("p (b n) -> p b n", b=2)
        xgT = ar(2048, 2 * D).rearrange("p (b k t) -> p b k t", b=2, k=DK)
        qz = ar(4096, NH * S).rearrange("p (h t) -> p h t", h=NH)
        xn = ar(4096, TT * D).rearrange("p (t k n) -> p t k n", t=TT, k=DK)
        xn_rows = ar(4096, TT * D).rearrange("p (t n) -> p t n", t=TT)
        yb = ar(4096, 2 * D).rearrange("p (b n) -> p b n", b=2)
        sil = ar(6144, 2 * F).rearrange("p (b n) -> p b n", b=2)
        hid = ar(6656, 2 * F).rearrange("p (b k n) -> p b k n", b=2, k=FK)
        hidT = ar(7168, 2 * F).rearrange("p (b k t) -> p b k t", b=2, k=FK)
        kT = ar(8192, CM * S).rearrange("p (m t) -> p m t", m=CM)
        wpp = ar(8192, PK * D).rearrange("p (k n) -> p k n", k=PK)
        vr = ar(10240, TT * CH).rearrange("p (t n) -> p t n", t=TT)
        pTs = ar(10240, PK * S).rearrange("p (k t) -> p k t", k=PK)
        onehot = ar(11264, 2 * TT * P).rearrange("p (j n) -> p j n", j=2 * TT)
        U = S + TAPS - 1
        u = ar(12288, CM * U).rearrange("p (m t) -> p m t", m=CM)
        sqa = ar(12288, CM * S).rearrange("p (m t) -> p m t", m=CM)
        free = 12288 + D
        cmp8 = ar(free, 2 * TT * ALLP).rearrange("p (j g) -> p j g", j=2 * TT)
        pairhot = ar(free + 2 * TT * ALLP, 2 * TT * ALLP).rearrange("p (j g) -> p j g", j=2 * TT)
        numhot = ar(free + 4 * TT * ALLP, 4 * TT * ALLP).rearrange("p (j a g) -> p j a g", j=2 * TT, a=2)
        sg = mixa
        qraw = mixa[:, 0:2, :]
        qsin = mixa[:, 2:4, :]
        sqc = mixa

        junk0 = mix[:, 0:D]
        junk = ar(12288, D)

        flat = [wring[:, s].rearrange("p a n -> p (a n)") for s in range(2)]
        win = [flat[i // 3][:, (i % 3) * 4096:(i % 3 + 1) * 4096].rearrange("p (k n) -> p k n", k=DK)
               for i in range(5)]
        woc = flat[1][:, 8192:12288].rearrange("p (m n) -> p m n", m=CM)
        woa = flat[1][:, 0:4096].rearrange("p (m n) -> p m n", m=CM)
        wpg = flat[0][:, 0:DK * D].rearrange("p (k n) -> p k n", k=DK)
        yg = flat[1][:, 0:8 * D].rearrange("p (j n) -> p j n", j=8)
        gfin = flat[1][:, 8 * D:9 * D]
        brow = flat[1][0:1, 9 * D:10 * D]
        sgate = flat[1][:, 10 * D:12 * D].rearrange("p (b n) -> p b n", b=4)
        up_w = [[wring[:, s, a, 0:4096].rearrange("p (w k n) -> p w k n", w=2, k=DK) for a in range(2)]
                for s in range(2)]
        dn_w = [[wring[:, s, a, 4096:6144].rearrange("p (k n) -> p k n", k=FK) for a in range(2)]
                for s in range(2)]

        pb = [ctx.enter_context(nc.psum_tensor(f"bank{i}", [P, 512], F32)) for i in range(8)]
        banks = Banks([sem(f"bank_full{i}") for i in range(8)], [sem(f"bank_free{i}") for i in range(8)])
        plan_banks(banks)

        def bk(name):
            return pb[banks.bank(name)]

        def filled(ins, name):
            ins.then_inc(banks.full[banks.bank(name)], 1)

        def emptied(ins, name):
            ins.then_inc(banks.free[banks.bank(name)], 1)

        x_loaded = [sem(f"x_loaded{t}") for t in range(TT)]
        win_loaded = [sem(f"win_loaded{i}") for i in range(5)]
        woc_loaded, woa_loaded = sem("woc_loaded"), sem("woa_loaded")
        const_loaded = sem("const_loaded")
        prm_loaded = sem("prm_loaded")
        ple_loaded = sem("ple_loaded")
        pg_loaded = sem("pg_loaded")
        last_loaded = sem("last_loaded")
        pads_set = sem("pads_set")
        qz_set = sem("qz_set")
        root_ready = sem("root_ready")
        xn_ready = sem("xn_ready")
        tap_done = sem("tap_done")
        qcos_done = sem("qcos_done")
        rope_done = sem("rope_done")
        csq_ready = sem("csq_ready")
        lnr_ready = sem("lnr_ready")
        z_ready = sem("z_ready")
        silu_ready = sem("silu_ready")
        osq_ready = sem("osq_ready")
        mixc_ready = sem("mixc_ready")
        exp_ready = sem("exp_ready")
        pinv_ready = sem("pinv_ready")
        prob_ready = sem("prob_ready")
        sqa_ready = sem("sqa_ready")
        groot_ready = sem("groot_ready")
        attended = sem("attended")
        rs_ready = sem("rs_ready")
        rows_stored = sem("rows_stored")
        rstep = sem("rstep")
        exp_in = sem("exp_in")
        exp_out = sem("exp_out")
        chosen = sem("chosen")
        list_in = sem("list_in")
        list_ready = sem("list_ready")
        list_full = sem("list_full")
        base_in = sem("base_in")
        item_in = sem("item_in")
        up_loaded = [[sem(f"up_loaded{s}{a}") for a in range(2)] for s in range(2)]
        dn_loaded = [[sem(f"dn_loaded{s}{a}") for a in range(2)] for s in range(2)]
        sp_go = sem("sp_go")
        pool_go = sem("pool_go")
        tcur_ready = sem("tcur_ready")
        ycur_ready = sem("ycur_ready")
        gathered = [sem(f"gathered{s}") for s in range(2)]
        xgT_full = sem("xgT_full")
        xgT_ready = sem("xgT_ready")
        up_done = sem("up_done")
        sil_ready = sem("sil_ready")
        hid_ready = sem("hid_ready")
        hidT_full = sem("hidT_full")
        hidT_ready = sem("hidT_ready")
        down_done = [sem(f"down_done{s}") for s in range(2)]
        ya_ready, yd_ready = sem("ya_ready"), sem("yd_ready")
        y_stored = [sem(f"y_stored{s}") for s in range(2)]
        yg_loaded = [sem(f"yg_loaded{t}") for t in range(TT)]
        x2_ready = sem("x2_ready")
        x3_ready = sem("x3_ready")
        o_ready = sem("o_ready")
        out_stored = sem("out_stored")

        def wait(eng, s, v):
            if not isinstance(v, int) or v > 0:
                eng.wait_ge(s, v)

        def further(eng):
            banks.wait_emptied(eng, "items")
            return eng.value_load(iters[0:1, 0:1], min_val=0, max_val=ITERS)

        def expert_pairs(eng, pair, before):
            half = PAIRS // 2
            for s in range(2):
                pair(s, s, 0, False)
            with eng.Fori(1, half - 1) as i:
                for s in range(2):
                    pair(2 * i + s, s, i, False)
            for s in range(2):
                pair(PAIRS - 2 + s, s, half - 1, s == 1)
            steps = further(eng)
            with eng.If(steps > 0):
                with eng.Fori(0, steps) as i:
                    before(2 * i + PAIRS, i + half)
                    for s in range(2):
                        pair(2 * i + PAIRS + s, s, i + half, s == 1)
            return steps

        block = ctx.enter_context(nc.Block())

        @block.sync
        def _(sp):
            for t in range(TT):
                sp.dma_start(xs[:, t, :], x[t * P:(t + 1) * P, :]).then_inc(x_loaded[t], 16)
            w_in_k = w_in.rearrange("(p k) n -> p k n", k=DK)
            for i in range(5):
                sp.dma_start(win[i], w_in_k[:, :, i * 512:(i + 1) * 512]).then_inc(win_loaded[i], 16)
            sp.dma_start(woc, w_out[0:CH, :].rearrange("(m p) n -> p m n", p=P)).then_inc(woc_loaded, 16)

            def load_up(s, e):
                for a in range(2):
                    for w, src in enumerate((w_gate, w_up)):
                        sp.dma_start(up_w[s][a][:, w],
                                     src[bass.ds(e[a], 1)].rearrange("e (p k) n -> p (e k) n", k=DK)
                                     ).then_inc(up_loaded[s][a], 16)

            def load_down(s, e):
                for a in range(2):
                    sp.dma_start(dn_w[s][a],
                                 w_down[bass.ds(e[a], 1)].rearrange("e (p k) n -> p (e k) n", k=FK)
                                 ).then_inc(dn_loaded[s][a], 16)

            banks.wait_full(sp, ("raw", 3))
            load_up(0, (0, 1))
            load_down(0, (0, 1))
            banks.wait_full(sp, ("raw", 7))
            sp.dma_start(woa, w_out[CH:2 * CH, :].rearrange("(m p) n -> p m n", p=P)).then_inc(woa_loaded, 16)
            banks.wait_full(sp, ("attn", CM - 1))
            sp.dma_start(wpp, w_pp.rearrange("(p k) n -> p k n", k=PK)).then_inc(ple_loaded, 16)
            sp.dma_start(pTs, pT.rearrange("(p k) n -> p k n", k=PK)).then_inc(ple_loaded, 16)
            banks.wait_full(sp, ("outa", 2 * TT - 1))
            load_up(1, (2, 3))
            load_down(1, (2, 3))

            half = PAIRS // 2

            def load_pair(n, s, h, e):
                sp.wait_ge(up_done, n - 1)
                sp.sem_inc(sp_go, 1)
                load_up(s, e)
                sp.wait_ge(down_done[s], h)
                sp.sem_inc(sp_go, 1)
                load_down(s, e)

            with sp.Fori(1, half) as i:
                for s in range(2):
                    load_pair(2 * i + s, s, i, (4 * i + 2 * s, 4 * i + 2 * s + 1))
            steps = further(sp)
            with sp.If(steps > 0):
                with sp.Fori(0, steps) as i:
                    for s in range(2):
                        e = [sp.value_load(eid[0:1, bass.ds(4 * i + 2 * s + a, 1)], min_val=0, max_val=NE - 1)
                             for a in range(2)]
                        load_pair(2 * i + PAIRS + s, s, i + half, e)
            sp.wait_ge(down_done[0], steps + half)
            sp.sem_inc(sp_go, 1)
            pg = w_pg.rearrange("(p k) n -> p k n", k=DK)
            for k in range(0, DK, 2):
                sp.dma_start(wpg[:, k:k + 2, :], pg[:, k:k + 2, :]).then_inc(pg_loaded, 16)
            sp.wait_ge(down_done[1], steps + half)
            sp.sem_inc(sp_go, 1)
            for s in range(2):
                sp.wait_ge(y_stored[s], 16 * steps + 16 * half)
                sp.sem_inc(sp_go, 1)
            y_rows = y_d.rearrange("(k t p) n -> p t k n", k=2, p=P)
            for t in range(TT):
                sp.dma_start(yg[:, 2 * t:2 * t + 2, :], y_rows[:, t]).then_inc(yg_loaded[t], 16)
            sp.dma_start(gfin, g_final.partition_broadcast(P)).then_inc(last_loaded, 16)
            sp.dma_start(brow, b_pg).then_inc(last_loaded, 16)
            for t in range(TT):
                sp.wait_ge(o_ready, t + 1)
                sp.dma_start(out[t * P:(t + 1) * P, :], xn_rows[:, t, :]).then_inc(out_stored, 16)
            sp.wait_ge(out_stored, 16 * TT)

        @block.gpsimd
        def _(pool):
            qz_h = qz.rearrange("p (m h) t -> p m h t", h=2)
            banks.wait_full(pool, ("x", DK - 1))
            pool.memset(qz_h[64:128, :, 0, :], 0.0).then_inc(qz_set, 1)
            pool.wait_ge(qz_set, 1)
            pool.memset(qz_h[0:64, :, 1, :], 0.0).then_inc(qz_set, 1)
            pool.wait_ge(qz_set, 2)
            pool.wait_ge(const_loaded, 32)
            for j in range(2 * CM):
                b = j % 2
                banks.wait_full(pool, ("rot", j))
                if j >= 1:
                    pool.wait_ge(rope_done, 2 * j if j <= CM else CM + j)
                pool.tensor_tensor(qraw[:, b, :], qraw[:, b, :], c[:, C_COS:C_COS + S], ALU.mult).then_inc(qcos_done, 1)
                pool.wait_ge(qcos_done, j + 1)
                banks.wait_emptied(pool, ("rot", j))
                if j < CM:
                    for hh in range(2):
                        rows = slice(hh * DH, (hh + 1) * DH)
                        if hh == 1:
                            pool.wait_ge(rope_done, 2 * j + 1)
                        pool.tensor_tensor(qz[rows, 2 * j + hh, :], qraw[rows, b, :], qsin[rows, b, :],
                                           ALU.add).then_inc(rope_done, 1)
                else:
                    pool.tensor_tensor(kT[:, j - CM, :], qraw[:, b, :], qsin[:, b, :], ALU.add).then_inc(rope_done, 1)
            pool.wait_ge(rope_done, 3 * CM)
            for m in range(CM):
                pool.wait_ge(osq_ready, m + 1)
                pool.tensor_scalar(mixc[:, m, :], mixc[:, m, :], pr[:, m * PM + TAPS + 3:m * PM + TAPS + 4],
                                   None, ALU.mult).then_inc(mixc_ready, 1)
            for t in range(TT):
                pool.wait_ge(xn_ready, TT + t + 1)
                pool.dma_start(rows_d[t * P:(t + 1) * P, :], xn_rows[:, t, :]).then_inc(rows_stored, 16)
            pool.wait_ge(rows_stored, 16 * TT)

            def gather(n, s, h):
                wait(pool, xgT_full, n - 1)
                pool.sem_inc(pool_go, 1)
                wait(pool, gathered[s], 16 * h)
                pool.sem_inc(pool_go, 1)
                pool.tensor_copy(tcur[:, s:s + 1], tlist[:, 0, bass.ds(n, 1)]).then_inc(tcur_ready, 1)
                pool.wait_ge(tcur_ready, n + 1)
                pool.sem_inc(pool_go, 1)
                pool.indirect_dma_start(xg[:, s, :], None, rows_d,
                                        bass.IndirectOffsetOnAxis(ap=tcur[:, s:s + 1], axis=0)
                                        ).then_inc(gathered[s], 16)

            def scatter(n, s, h):
                pool.wait_ge(ya_ready, n + 1)
                pool.sem_inc(pool_go, 1)
                pool.wait_ge(yd_ready, n + 1)
                pool.sem_inc(pool_go, 1)
                wait(pool, y_stored[s], 16 * h)
                pool.sem_inc(pool_go, 1)
                pool.tensor_copy(ycur[:, s:s + 1], tlist[:, 1, bass.ds(n, 1)]).then_inc(ycur_ready, 1)
                pool.wait_ge(ycur_ready, n + 1)
                pool.sem_inc(pool_go, 1)
                pool.indirect_dma_start(y_d, bass.IndirectOffsetOnAxis(ap=ycur[:, s:s + 1], axis=0), yb[:, s, :], None,
                                        bounds_check=2 * S - 1, oob_is_err=False).then_inc(y_stored[s], 16)

            pool.wait_ge(list_ready, 1)
            half = PAIRS // 2
            for s in range(2):
                gather(s, s, 0)
            with pool.Fori(1, half) as i:
                for s in range(2):
                    gather(2 * i + s, s, i)
                    scatter(2 * i + s - 2, s, i - 1)
            for s in range(2):
                gather(PAIRS + s, s, half)
                scatter(PAIRS - 2 + s, s, half - 1)
            steps = further(pool)
            with pool.If(steps > 0):
                with pool.Fori(0, steps) as i:
                    for s in range(2):
                        gather(2 * i + PAIRS + 2 + s, s, i + half + 1)
                        scatter(2 * i + PAIRS + s, s, i + half)

        @block.scalar
        def _(act):
            act.dma_start(c[:, 0:C_MASK], cst[:, 0:C_MASK]).then_inc(const_loaded, 16)
            act.dma_start(c[:, C_MASK:C_END], cst[:, C_MASK:C_END]).then_inc(const_loaded, 16)
            act.dma_start(pr[:], prm).then_inc(prm_loaded, 16)
            act.dma_start(wr[:], w_r.rearrange("(p k) n -> p k n", k=DK)).then_inc(prm_loaded, 16)
            eps = c[:, C_EPS:C_EPS + 1]

            def mean_root(which, t, unused):
                act.activation(unused, xs[:, t, :], ACT.Square, accum_out=sq[:, which, t:t + 1]).then_inc(root_ready, 1)
                act.wait_ge(root_ready, 2 * (which * TT + t) + 1)
                act.activation(ss[:, which, t:t + 1], sq[:, which, t:t + 1], ACT.Sqrt, scale=1.0 / D, bias=eps).then_inc(root_ready, 1)

            act.wait_ge(const_loaded, 32)
            for t in range(TT):
                act.wait_ge(x_loaded[t], 16)
                mean_root(0, t, junk0)
            act.wait_ge(prm_loaded, 32)
            for k in range(1, DK, 2):
                banks.wait_full(act, ("x", k))
                emptied(act.activation(hT[:, k, :], bk(("x", k))[:], ACT.Copy, scale=pr[:, Q_MIX + k:Q_MIX + k + 1]), ("x", k))
            for m in range(CM):
                banks.wait_full(act, ("gate", m))
                emptied(act.activation(sg[:, m, :], bk(("gate", m))[:], ACT.Sigmoid), ("gate", m))
            for j in range(2 * CM):
                banks.wait_full(act, ("raw", j))
                banks.wait_emptied(act, ("val", CM - 1))
                if j >= 2:
                    act.wait_ge(rope_done, 2 * (j - 1) if j <= CM else CM + j - 1)
                emptied(act.activation(qraw[:, j % 2, :], bk(("raw", j))[:], ACT.Copy), ("raw", j))
            act.wait_ge(rope_done, 3 * CM)
            banks.wait_emptied(act, "mean")
            for m in range(CM):
                act.activation(sqc[:, m, :], mixc[:, m, :], ACT.Square).then_inc(csq_ready, 1)
            banks.wait_full(act, ("v", 0))
            emptied(act.activation(vr[:, 0, :], bk(("v", 0))[:], ACT.Copy), ("v", 0))
            banks.wait_full(act, "var")
            emptied(act.activation(lnr[:], bk("var")[:], ACT.Sqrt, bias=eps), "var")
            banks.wait_full(act, ("v", 1))
            emptied(act.activation(vr[:, 1, :], bk(("v", 1))[:], ACT.Copy), ("v", 1))
            for m in range(CM):
                act.wait_ge(z_ready, m + 1)
                base = m * PM + TAPS
                act.activation(mixc[:, m, :], mixc[:, m, :], ACT.Silu, scale=pr[:, base + 1:base + 2],
                               bias=pr[:, base + 2:base + 3]).then_inc(silu_ready, 1)
            for m in range(CM):
                act.wait_ge(silu_ready, m + 1)
                act.activation(sqc[:, m, :], mixc[:, m, :], ACT.Square).then_inc(osq_ready, 1)
            for t in range(2, TT):
                banks.wait_full(act, ("v", t))
                emptied(act.activation(vr[:, t, :], bk(("v", t))[:], ACT.Copy), ("v", t))

            def exps(u_):
                i, b = u_ % TT, u_ % 2
                n = P * (i + 1)
                for hh in range(2):
                    banks.wait_emptied(act, ("score", u_, hh))
                    act.activation(prob[:, b, hh, 0:n], prob[:, b, hh, 0:n], ACT.Exp, scale=-1.0,
                                   bias=nmax[:, b, hh:hh + 1], accum_out=psum_p[:, b, hh:hh + 1]).then_inc(exp_ready, 1)

            def probs_out(u_):
                m, i, b = u_ // TT, u_ % TT, u_ % 2
                n = P * (i + 1)
                if u_ >= 2:
                    mb, ib = (u_ - 2) // TT, (u_ - 2) % TT
                    if ib == TT - 1:
                        banks.wait_full(act, ("attn", mb))
                    else:
                        act.wait_ge(attended, mb * (TT - 1) + ib + 1)
                for hh in range(2):
                    banks.wait_full(act, ("probT", u_, hh))
                    emptied(act.activation(probT[:, b, hh, 0:n], bk(("probT", u_, hh))[:, 0:n], ACT.Copy), ("probT", u_, hh))
                if i == 1 and m >= 1:
                    attn_sq(m - 1)

            def attn_sq(m):
                banks.wait_full(act, ("attn", m))
                act.activation(sqa[:, m, :], bk(("attn", m))[:], ACT.Square).then_inc(sqa_ready, 1)

            units = CM * TT
            for u_ in range(units + 1):
                if u_ < units:
                    exps(u_)
                if u_ >= 1:
                    probs_out(u_ - 1)
            attn_sq(CM - 1)
            act.activation(gss[:, 0, :], gsq[:], ACT.Sqrt, scale=1.0 / CH, bias=eps).then_inc(groot_ready, 1)
            banks.wait_full(act, "attn_sq")
            emptied(act.activation(gss[:, 1, :], bk("attn_sq")[:, 0:TT], ACT.Sqrt, scale=1.0 / CH, bias=eps), "attn_sq")
            for t in range(TT):
                banks.wait_emptied(act, ("outa", 2 * t + 1))
                mean_root(1, t, junk)
            banks.wait_full(act, "logitT")
            emptied(act.activation(logT, bk("logitT")[0:NR, :], ACT.Identity, bias=pr[0:NR, Q_RB:Q_RB + 1]), "logitT")

            def ple_out(q):
                banks.wait_full(act, ("ple", q))
                if q == 0:
                    banks.wait_full(act, ("outa", 2 * TT - 1))
                emptied(act.activation(plep[:, q // 2, (q % 2) * 512:(q % 2 + 1) * 512], bk(("ple", q))[:], ACT.Copy),
                        ("ple", q))

            act.wait_ge(exp_in, 1)
            act.activation(rt[:, 0, :, 0:NG], rt[:, 0, :, 0:NG], ACT.Exp).then_inc(exp_out, 1)
            act.wait_ge(exp_in, 2)
            act.activation(sm[:, 6, :], sm[:, 6, :], ACT.Exp).then_inc(exp_out, 1)
            for q in range(2 * TT):
                ple_out(q)

            def pair(n, s, h, last):
                act.wait_ge(up_done, n + 1)
                wait(act, hid_ready, n - 1)
                act.activation(sil[:, s, :], pb[2 + s][:, 0:F], ACT.Silu).then_inc(sil_ready, 1)
                act.wait_ge(hidT_full, n + 1)
                wait(act, down_done[s], h)
                act.activation(hidT[:, s], pb[4 + s][:, 0:F].rearrange("p (k t) -> p k t", k=FK), ACT.Copy).then_inc(hidT_ready, 1)
                act.wait_ge(down_done[s], h + 1)
                wait(act, y_stored[s], 16 * h)
                act.activation(yb[:, s, 0:512], pb[6][:], ACT.Copy).then_inc(ya_ready, 1)

            expert_pairs(act, pair, lambda n, h: None)

            for t in range(TT):
                act.wait_ge(x2_ready, 2 * (t + 1))
                mean_root(2, t, junk)
            for q in range(2 * TT):
                banks.wait_full(act, ("pgate", q))
                if q >= 4:
                    act.wait_ge(x3_ready, 2 * (q - 3))
                emptied(act.activation(sgate[:, q % 4, :], bk(("pgate", q))[:], ACT.Sigmoid), ("pgate", q))
            for t in range(TT):
                act.wait_ge(x3_ready, 4 * (t + 1))
                mean_root(3, t, junk)

        @block.vector
        def _(dve):
            dve.memset(ones[:], 1.0).then_inc(pads_set, 1)
            dve.memset(mean_w[:], 1.0 / CH).then_inc(pads_set, 1)
            dve.memset(u[:, :, 0:TAPS - 1], 0.0).then_inc(pads_set, 1)
            rsn = [0]

            def recip(out_ap, in_ap):
                dve.reciprocal(out_ap, in_ap).then_inc(rs_ready, 1)
                rsn[0] += 1
                dve.wait_ge(rs_ready, rsn[0])

            def permuted(ap):
                return ap.rearrange("p (n k) -> p k n", k=DK)

            def inverse(which, t):
                dve.wait_ge(root_ready, 2 * (which * TT + t) + 2)
                recip(rs[:, which, t:t + 1], ss[:, which, t:t + 1])

            def normal_rows(which, t):
                inverse(which, t)
                dve.tensor_scalar(xn[:, t], permuted(xs[:, t, :]), rs[:, which, t:t + 1], None, ALU.mult).then_inc(xn_ready, 1)

            for t in range(TT):
                normal_rows(0, t)
            dve.wait_ge(prm_loaded, 32)
            for k in range(0, DK, 2):
                banks.wait_full(dve, ("x", k))
                emptied(dve.tensor_scalar(hT[:, k, :], bk(("x", k))[:], pr[:, Q_MIX + k:Q_MIX + k + 1], None, ALU.mult), ("x", k))
            taps = [0]

            def glu(m):
                banks.wait_full(dve, ("val", m))
                banks.wait_emptied(dve, ("gate", m))
                if m == 0:
                    dve.wait_ge(pads_set, 3)
                emptied(dve.tensor_tensor(u[:, m, TAPS - 1:U], bk(("val", m))[:], sg[:, m, :], ALU.mult), ("val", m))

            def tap(m, j):
                for mm in (m, m + 1):
                    w = pr[:, mm * PM + j:mm * PM + j + 1]
                    if j == 0:
                        ins = dve.tensor_scalar(mixc[:, mm, :], u[:, mm, 0:S], w, pr[:, mm * PM + TAPS:mm * PM + TAPS + 1],
                                                ALU.mult, ALU.add)
                    else:
                        dve.wait_ge(tap_done, taps[0] - 1)
                        ins = dve.scalar_tensor_tensor(out=mixc[:, mm, :], in0=u[:, mm, j:j + S], scalar=w,
                                                       in1=mixc[:, mm, :], op0=ALU.mult, op1=ALU.add)
                    ins.then_inc(tap_done, 1)
                    taps[0] += 1

            def turn(j):
                banks.wait_full(dve, ("rot", j))
                if j >= 2:
                    dve.wait_ge(rope_done, 2 * (j - 1) if j <= CM else CM + j - 1)
                emptied(dve.tensor_tensor(qsin[:, j % 2, :], bk(("rot", j))[:], c[:, C_SIN:C_SIN + S], ALU.mult), ("rot", j))

            glu(0)
            glu(1)
            banks.wait_emptied(dve, ("val", 1))
            for j in range(TAPS):
                tap(0, j)
                if j == 12:
                    glu(2)
                if j == 22:
                    glu(3)
            banks.wait_emptied(dve, ("val", 3))
            done = 0
            for j in range(TAPS):
                tap(2, j)
                if j % 5 == 4 and done < 6:
                    turn(done)
                    done += 1
            for j in range(done, 2 * CM):
                turn(j)
            banks.wait_full(dve, "mean")
            for m in range(CM):
                ins = dve.tensor_tensor(mixc[:, m, :], mixc[:, m, :], bk("mean")[:], ALU.subtract)
            emptied(ins, "mean")
            banks.wait_emptied(dve, "var")
            dve.reciprocal(lnr[:], lnr[:]).then_inc(lnr_ready, 1)
            dve.wait_ge(lnr_ready, 1)
            dve.wait_ge(csq_ready, CM)
            for m in range(CM):
                dve.tensor_tensor(mixc[:, m, :], mixc[:, m, :], lnr[:], ALU.mult).then_inc(z_ready, 1)

            def scores(u_):
                i, b = u_ % TT, u_ % 2
                n = P * (i + 1)
                for hh in range(2):
                    banks.wait_full(dve, ("score", u_, hh))
                    if u_ >= 2 and hh == 0:
                        banks.wait_full(dve, ("probT", u_ - 2, 1))
                    ins = nc.vector.tensor_tensor_reduce(out=prob[:, b, hh, 0:n], in0=bk(("score", u_, hh))[:, 0:n],
                                                         in1=c[:, C_MASK + S - n:C_MASK + S], scale=-1.0 / 8, scalar=FAR,
                                                         op0=ALU.add, op1=ALU.min, accum_out=nmax[:, b, hh:hh + 1])
                    emptied(ins, ("score", u_, hh))

            def normalise(u_):
                i, b = u_ % TT, u_ % 2
                n = P * (i + 1)
                dve.wait_ge(exp_ready, 2 * u_ + 2)
                dve.reciprocal(pinv[:, b, :], psum_p[:, b, :]).then_inc(pinv_ready, 1)
                dve.wait_ge(pinv_ready, u_ + 1)
                for hh in range(2):
                    dve.tensor_scalar(prob[:, b, hh, 0:n], prob[:, b, hh, 0:n], pinv[:, b, hh:hh + 1], None,
                                      ALU.mult).then_inc(prob_ready, 1)

            def attn_out(m):
                dve.wait_ge(sqa_ready, m + 1)
                emptied(dve.tensor_scalar(mixa[:, m, :], bk(("attn", m))[:], pr[:, Q_BETA + m:Q_BETA + m + 1], None,
                                          ALU.mult), ("attn", m))

            banks.wait_full(dve, "conv_sq")
            emptied(dve.tensor_copy(gsq[:], bk("conv_sq")[:, 0:TT]), "conv_sq")
            units = CM * TT
            for u_ in range(units + 1):
                if u_ < units:
                    scores(u_)
                if u_ >= 1:
                    normalise(u_ - 1)
                    if (u_ - 1) % TT == 1 and u_ - 1 > TT:
                        attn_out((u_ - 1) // TT - 1)
            attn_out(CM - 1)
            dve.wait_ge(groot_ready, 1)
            recip(grs[:, 0, :], gss[:, 0, :])
            banks.wait_emptied(dve, "attn_sq")
            recip(grs[:, 1, :], gss[:, 1, :])

            def add_scaled(name, w, t, half):
                cols = xs[:, t, half * 512:(half + 1) * 512]
                emptied(dve.scalar_tensor_tensor(out=cols, in0=bk(name)[:], scalar=grs[:, w, t:t + 1], in1=cols,
                                                 op0=ALU.mult, op1=ALU.add), name)
                banks.wait_emptied(dve, name)

            def columns_out(kind, t, gains):
                for kh in range(2):
                    name = (kind, t, kh)
                    banks.wait_full(dve, name)
                    emptied(dve.tensor_tensor(
                        hT[:, 4 * kh:4 * kh + 4, t * P:(t + 1) * P], bk(name)[:].rearrange("p (k n) -> p k n", k=4),
                        pr[:, gains + 4 * kh:gains + 4 * kh + 4].rearrange("p (k n) -> p k n", n=1).broadcast_to([P, 4, P]),
                        ALU.mult), name)

            for q in range(2 * TT):
                t, half = q // 2, q % 2
                banks.wait_full(dve, ("outc", q))
                add_scaled(("outc", q), 0, t, half)
                banks.wait_full(dve, ("outa", q))
                add_scaled(("outa", q), 1, t, half)
                if half == 0 and t >= 1:
                    normal_rows(1, t - 1)
                if half == 1 and t >= 2:
                    columns_out("h2", t - 2, Q_FFN)
            normal_rows(1, TT - 1)
            columns_out("h2", TT - 2, Q_FFN)
            columns_out("h2", TT - 1, Q_FFN)

            n = [0]

            def step(ins):
                n[0] += 1
                ins.then_inc(rstep, 1)
                dve.wait_ge(rstep, n[0])

            def wide(ap, k):
                return ap.rearrange("p (t n) -> p t n", n=1).broadcast_to([P, TT, k])

            def table(col, k):
                return c[:, col:col + k].rearrange("p (a n) -> p a n", a=1).broadcast_to([P, TT, k])

            def first_hot(out_ap, in_ap, top, scratch, weights, k):
                step(dve.tensor_tensor(scratch, in_ap, wide(top, k), ALU.is_equal))
                step(dve.tensor_tensor(scratch, scratch, table(weights, k), ALU.mult))
                step(dve.tensor_reduce(sm[:, 0, :], scratch, AX.X, ALU.max))
                step(dve.tensor_tensor(out_ap, scratch, wide(sm[:, 0, :], k), ALU.is_equal))

            banks.wait_full(dve, "logit")
            emptied(dve.tensor_copy(lg[:], bk("logit")[:, 0:TT * NR].rearrange("p (t n) -> p t n", t=TT)), "logit")
            banks.wait_emptied(dve, "logit")
            grp = lg[:, :, 0:NG]
            step(dve.tensor_reduce(sm[:, 1, :], grp, AX.X, ALU.max))
            dve.tensor_tensor(rt[:, 0, :, 0:NG], grp, wide(sm[:, 1, :], NG), ALU.subtract).then_inc(exp_in, 1)
            first_hot(rt[:, 1, :, 0:NG], grp, sm[:, 1, :], rt[:, 2, :, 0:NG], C_GRP, NG)
            step(dve.tensor_scalar(rt[:, 2, :, 0:NG], rt[:, 1, :, 0:NG], -1.0, FAR, ALU.add, ALU.mult))
            for t in range(TT):
                ins = dve.tensor_tensor(
                    rt[:, 3, t, :].rearrange("p (g e) -> p g e", g=NG), lg[:, t, NG:NR].rearrange("p (g e) -> p g e", g=NG),
                    rt[:, 2, t, 0:NG].rearrange("p (g e) -> p g e", e=1).broadcast_to([P, NG, EG]), ALU.add)
            step(ins)
            step(dve.tensor_reduce(sm[:, 2, :], rt[:, 3], AX.X, ALU.max))
            first_hot(hot[:, 0], rt[:, 3], sm[:, 2, :], rt[:, 4], C_RANK, NE)
            step(dve.tensor_scalar(rt[:, 4], hot[:, 0], -FAR, None, ALU.mult))
            step(dve.tensor_tensor(rt[:, 5], rt[:, 3], rt[:, 4], ALU.add))
            step(dve.tensor_reduce(sm[:, 3, :], rt[:, 5], AX.X, ALU.max))
            first_hot(hot[:, 1], rt[:, 5], sm[:, 3, :], rt[:, 4], C_RANK, NE)
            dve.tensor_tensor(rt[:, 6], hot[:, 0], hot[:, 1], ALU.add).then_inc(chosen, 1)
            dve.tensor_tensor(sm[:, 6, :], sm[:, 3, :], sm[:, 2, :], ALU.subtract).then_inc(exp_in, 1)
            def over8(ap, k):
                return ap.rearrange("p (j n) -> p j n", n=1).broadcast_to([P, 2 * TT, k])

            def table8(col, k):
                return c[:, col:col + k].rearrange("p (a n) -> p a n", a=1).broadcast_to([P, 2 * TT, k])

            hot8 = hot[:].rearrange("p k t n -> p (k t) n")
            rt8 = rt[:, 4:6].rearrange("p k t n -> p (k t) n")
            E, R, O, X, G, IT, H, KEY, T0, T1 = (by8[:, i, :] for i in range(10))
            step(dve.tensor_tensor(rt8, hot8, table8(C_EXP, NE), ALU.mult))
            step(dve.tensor_reduce(E, rt8, AX.X, ALU.add))
            banks.wait_full(dve, "count")
            xc = ecnt[:, 8:9]
            emptied(dve.tensor_scalar(ecnt[:, 0:7], c[0:NE, C_THR:C_THR + 7], bk("count")[0:NE, 0:1], None, ALU.is_lt), "count")
            banks.wait_emptied(dve, "count")
            step(dve.tensor_reduce(xc, ecnt[:, 0:7], AX.X, ALU.add))
            dve.tensor_scalar(xb[:], ones[0:NE, :], xc, None, ALU.mult).then_inc(base_in, 1)
            banks.wait_full(dve, "rank")
            emptied(dve.tensor_tensor(
                rt[:, 4:6].rearrange("p k t n -> p k (t n)"), hot[:].rearrange("p k t n -> p k (t n)"),
                bk("rank")[:, 0:TT * NE].rearrange("p (a n) -> p a n", a=1).broadcast_to([P, 2, TT * NE]), ALU.mult), "rank")
            banks.wait_emptied(dve, "rank")
            step(dve.tensor_reduce(R, rt8, AX.X, ALU.add))
            step(dve.tensor_tensor(cmp8[:, :, 0:7], over8(R, 7), table8(C_THR, 7), ALU.is_ge))
            step(dve.tensor_reduce(X, cmp8[:, :, 0:7], AX.X, ALU.add))
            banks.wait_full(dve, "base")
            base = bk("base")
            step(dve.tensor_tensor(rt8, hot8, base[:, 0:NE].rearrange("p (a n) -> p a n", a=1).broadcast_to([P, 2 * TT, NE]),
                                   ALU.mult))
            step(dve.tensor_copy(ecnt[:, 9:10], base[0:NE, NE + 1:NE + 2]))
            step(dve.tensor_scalar(fcnt[:, 0:ITERS], c[:, C_FOUR:C_FOUR + ITERS], base[:, NE:NE + 1], None, ALU.is_lt))
            step(dve.tensor_reduce(fcnt[:, 4:5], fcnt[:, 0:ITERS], AX.X, ALU.add))
            step(dve.tensor_tensor(ecnt[:, 10:11], ecnt[:, 9:10], xc, ALU.add))
            step(dve.tensor_scalar(ihot[:, 0, :], c[0:NE, C_IOTA:C_IOTA + MORE], ecnt[:, 9:10], None, ALU.is_ge))
            step(dve.tensor_scalar(ihot[:, 1, :], c[0:NE, C_IOTA:C_IOTA + MORE], ecnt[:, 10:11], None, ALU.is_lt))
            dve.tensor_tensor(ihot[:, 2, :], ihot[:, 0, :], ihot[:, 1, :], ALU.mult).then_inc(item_in, 1)
            emptied(dve.tensor_copy(iters[:], fcnt[:, 4:5]), "base")
            step(dve.tensor_reduce(O, rt8, AX.X, ALU.add))
            step(dve.tensor_scalar(G, X, 1.0, None, ALU.is_ge))
            step(dve.tensor_tensor(T0, O, X, ALU.add))
            step(dve.scalar_tensor_tensor(out=T1, in0=T0, scalar=float(NE - 1), in1=E, op0=ALU.add, op1=ALU.subtract))
            step(dve.tensor_tensor(T1, T1, G, ALU.mult))
            step(dve.tensor_tensor(IT, T1, E, ALU.add))
            step(dve.tensor_tensor(cmp8[:, :, 0:ALLP - 1], over8(IT, ALLP - 1), table8(C_TWO, ALLP - 1), ALU.is_ge))
            step(dve.tensor_reduce(H, cmp8[:, :, 0:ALLP - 1], AX.X, ALU.add))
            step(dve.scalar_tensor_tensor(out=T0, in0=H, scalar=-2.0, in1=IT, op0=ALU.mult, op1=ALU.add))
            step(dve.tensor_tensor(T0, T0, X, ALU.subtract))
            step(dve.scalar_tensor_tensor(out=KEY, in0=T0, scalar=float(CAP), in1=R, op0=ALU.mult, op1=ALU.add))
            step(dve.tensor_tensor(pairhot[:], over8(H, ALLP), table8(C_IOTA, ALLP), ALU.is_equal))
            step(dve.tensor_tensor(numhot[:, :, 0, :], pairhot[:], over8(c[:, C_TOK:C_TOK + 2 * TT], ALLP), ALU.mult))
            step(dve.tensor_tensor(numhot[:, :, 1, :], pairhot[:], over8(c[:, C_ROW:C_ROW + 2 * TT], ALLP), ALU.mult))
            dve.tensor_tensor(onehot, table8(C_IOTA, P), over8(KEY, P), ALU.is_equal).then_inc(list_in, 1)
            dve.wait_ge(list_full, 1)
            dve.tensor_copy(tlist[:, 0, :], pb[0][:, 0:ALLP])
            dve.tensor_scalar(tlist[:, 1, :], pb[0][:, ALLP:2 * ALLP], -1.0, float(NOWHERE), ALU.mult,
                              ALU.add).then_inc(list_ready, 1)
            banks.wait_full(dve, "items")
            emptied(dve.tensor_copy(eid[:], bk("items")[0:1, 0:MORE]), "items")
            dve.wait_ge(exp_out, 2)
            step(dve.tensor_reduce(sm[:, 4, :], rt[:, 0, :, 0:NG], AX.X, ALU.add))
            step(dve.tensor_scalar(sm[:, 5, :], sm[:, 6, :], 1.0, None, ALU.add))
            step(dve.tensor_tensor(sm[:, 4, :], sm[:, 4, :], sm[:, 5, :], ALU.mult))
            step(dve.reciprocal(gw[:, 0, :], sm[:, 4, :]))
            step(dve.tensor_tensor(gw[:, 1, :], gw[:, 0, :], sm[:, 6, :], ALU.mult))

            def x_out(n_, s):
                dve.wait_ge(xgT_full, n_ + 1)
                wait(dve, up_done, n_ - 1)
                for kh in range(2):
                    dve.tensor_tensor(
                        xgT[:, s, 4 * kh:4 * kh + 4, :], pb[kh][:].rearrange("p (k n) -> p k n", k=4),
                        pr[:, Q_FFN + 4 * kh:Q_FFN + 4 * kh + 4].rearrange("p (k n) -> p k n", n=1).broadcast_to([P, 4, P]),
                        ALU.mult).then_inc(xgT_ready, 1)

            def pair(n_, s, h, last):
                dve.wait_ge(sil_ready, n_ + 1)
                wait(dve, hidT_full, n_ - 1)
                dve.tensor_tensor(hid[:, s], sil[:, s, :].rearrange("p (n k) -> p k n", k=FK),
                                  pb[2 + s][:, F:2 * F].rearrange("p (n k) -> p k n", k=FK), ALU.mult).then_inc(hid_ready, 1)
                if not last:
                    x_out(n_ + 1, 1 - s)
                dve.wait_ge(down_done[s], h + 1)
                wait(dve, y_stored[s], 16 * h)
                dve.tensor_copy(yb[:, s, 512:D], pb[7][:]).then_inc(yd_ready, 1)

            x_out(0, 0)
            steps = expert_pairs(dve, pair, lambda n_, h: x_out(n_, 0))

            for t in range(TT):
                dve.wait_ge(yg_loaded[t], 16)
                for k in range(2):
                    dve.scalar_tensor_tensor(out=xs[:, t, :], in0=yg[:, 2 * t + k, :], scalar=gw[:, k, t:t + 1],
                                             in1=xs[:, t, :], op0=ALU.mult, op1=ALU.add).then_inc(x2_ready, 1)
                    dve.wait_ge(x2_ready, 2 * t + k + 1)
            for t in range(TT + 1):
                if t < TT:
                    normal_rows(2, t)
                if t >= 1:
                    if t == 1:
                        for s in range(2):
                            dve.wait_ge(gathered[s], 16 * steps + 16 * (PAIRS // 2 + 1))
                    columns_out("h3", t - 1, Q_PLE)
            x3 = 0
            for q in range(2 * TT):
                t, half = q // 2, q % 2
                name = ("pgate", q)
                cols = slice(half * 512, (half + 1) * 512)
                banks.wait_emptied(dve, name)
                dve.tensor_tensor(sgate[:, q % 4, :], sgate[:, q % 4, :], plep[:, t, cols], ALU.mult).then_inc(x3_ready, 1)
                x3 += 1
                dve.wait_ge(x3_ready, x3)
                dve.tensor_tensor(xs[:, t, cols], xs[:, t, cols], sgate[:, q % 4, :], ALU.add).then_inc(x3_ready, 1)
                x3 += 1
            dve.wait_ge(last_loaded, 32)
            for t in range(TT):
                inverse(3, t)
                dve.scalar_tensor_tensor(out=xn_rows[:, t, :], in0=xs[:, t, :], scalar=rs[:, 3, t:t + 1], in1=gfin,
                                         op0=ALU.mult, op1=ALU.mult).then_inc(o_ready, 1)

        @block.tensor
        def _(pe):
            pe.wait_ge(const_loaded, 32)
            pe.wait_ge(xn_ready, TT)
            for k in range(DK):
                for t in range(TT):
                    ins = pe.transpose(bk(("x", k))[:, t * P:(t + 1) * P], xn[:, t, k, :], ident)
                filled(ins, ("x", k))
            for k in range(DK):
                banks.wait_emptied(pe, ("x", k))

            def project(name, chunk, m):
                banks.wait_free(pe, name)
                for k in range(DK):
                    ins = pe.matmul(bk(name)[:], win[chunk][:, k, m * P:(m + 1) * P], hT[:, k, :],
                                    start=(k == 0), stop=(k == DK - 1))
                filled(ins, name)

            for m in range(CM):
                for i, name in enumerate(("val", "gate")):
                    pe.wait_ge(win_loaded[i], 16)
                    project((name, m), i, m)

            def rotate(j):
                banks.wait_free(pe, ("rot", j))
                banks.wait_emptied(pe, ("raw", j))
                filled(pe.matmul(bk(("rot", j))[:], c[:, C_ROT:C_ROT + P], qraw[:, j % 2, :], start=True, stop=True), ("rot", j))

            for j in range(2 * CM + 1):
                if j < 2 * CM:
                    pe.wait_ge(win_loaded[2 + j // CM], 16)
                    project(("raw", j), 2 + j // CM, j % CM)
                if j >= 1:
                    rotate(j - 1)

            def channel_sum(name, src):
                banks.wait_free(pe, name)
                for t in range(TT):
                    for m in range(CM):
                        ins = pe.matmul(bk(name)[:, t:t + 1], src[:, m, t * P:(t + 1) * P], ones[:, 0:1],
                                        start=(m == 0), stop=(m == CM - 1))
                filled(ins, name)

            pe.wait_ge(win_loaded[4], 16)
            pe.wait_ge(tap_done, CM * TAPS)
            banks.wait_free(pe, "mean")
            for m in range(CM):
                ins = pe.matmul(bk("mean")[:], mean_w[:], mixc[:, m, :], start=(m == 0), stop=(m == CM - 1))
            filled(ins, "mean")

            def values(t):
                banks.wait_free(pe, ("v", t))
                for k in range(DK):
                    ins = pe.matmul(bk(("v", t))[:], hT[:, k, t * P:(t + 1) * P], win[4][:, k, :],
                                    start=(k == 0), stop=(k == DK - 1))
                filled(ins, ("v", t))

            values(0)
            banks.wait_free(pe, "var")
            pe.wait_ge(csq_ready, CM)
            for m in range(CM):
                ins = pe.matmul(bk("var")[:], mean_w[:], sqc[:, m, :], start=(m == 0), stop=(m == CM - 1))
            filled(ins, "var")
            for t in range(1, TT):
                values(t)
            pe.wait_ge(osq_ready, CM)
            channel_sum("conv_sq", sqc)

            pe.wait_ge(qz_set, 2)
            pe.wait_ge(rope_done, 3 * CM)

            def score(u_):
                m, i = u_ // TT, u_ % TT
                n = P * (i + 1)
                for hh in range(2):
                    name = ("score", u_, hh)
                    banks.wait_free(pe, name)
                    filled(pe.matmul(bk(name)[:, 0:n], qz[:, 2 * m + hh, i * P:(i + 1) * P], kT[:, m, 0:n],
                                     start=True, stop=True), name)

            def transpose_probs(u_):
                m, i, b = u_ // TT, u_ % TT, u_ % 2
                for hh in range(2):
                    name = ("probT", u_, hh)
                    pe.wait_ge(prob_ready, 2 * u_ + hh + 1)
                    banks.wait_free(pe, name)
                    for j in range(i + 1):
                        ins = pe.transpose(bk(name)[:, j * P:(j + 1) * P], prob[:, b, hh, j * P:(j + 1) * P], ident)
                    filled(ins, name)

            def attend(u_):
                m, i, b = u_ // TT, u_ % TT, u_ % 2
                name = ("attn", m)
                if i == 0:
                    banks.wait_free(pe, name)
                for hh in range(2):
                    pt = ("probT", u_, hh)
                    banks.wait_emptied(pe, pt)
                for j in range(i + 1):
                    for hh in range(2):
                        ins = pe.matmul(bk(name)[hh * DH:(hh + 1) * DH, i * P:(i + 1) * P],
                                        vr[:, j, (2 * m + hh) * DH:(2 * m + hh + 1) * DH],
                                        probT[:, b, hh, j * P:(j + 1) * P], start=(j == 0), stop=(j == i))
                if i == TT - 1:
                    filled(ins, name)
                else:
                    ins.then_inc(attended, 1)

            for t in range(TT):
                banks.wait_emptied(pe, ("v", t))
            units = CM * TT
            for u_ in range(units + 2):
                if u_ < units:
                    score(u_)
                if 1 <= u_ <= units:
                    transpose_probs(u_ - 1)
                if u_ >= 2:
                    attend(u_ - 2)
            pe.wait_ge(sqa_ready, CM)
            channel_sum("attn_sq", sqa)

            def out_part(name, t, half, src, w):
                banks.wait_free(pe, name)
                for m in range(CM):
                    ins = pe.matmul(bk(name)[:], src[:, m, t * P:(t + 1) * P], w[:, m, half * 512:(half + 1) * 512],
                                    start=(m == 0), stop=(m == CM - 1))
                filled(ins, name)

            def turn_rows(kind, t, first):
                pe.wait_ge(xn_ready, first + t + 1)
                for kh in range(2):
                    name = (kind, t, kh)
                    banks.wait_free(pe, name)
                    for k in range(4):
                        ins = pe.transpose(bk(name)[:, k * P:(k + 1) * P], xn[:, t, 4 * kh + k, :], ident)
                    filled(ins, name)

            pe.wait_ge(woc_loaded, 16)
            pe.wait_ge(woa_loaded, 16)
            pe.wait_ge(mixc_ready, CM)
            banks.wait_emptied(pe, ("attn", CM - 1))
            for q in range(2 * TT):
                t, half = q // 2, q % 2
                out_part(("outc", q), t, half, mixc, woc)
                out_part(("outa", q), t, half, mixa, woa)
                if half == 1 and t >= 1:
                    turn_rows("h2", t - 1, TT)
            turn_rows("h2", TT - 1, TT)

            for kh in range(2):
                name = ("h2", TT - 1, kh)
                banks.wait_emptied(pe, name)
            banks.wait_free(pe, "logitT")
            for k in range(DK):
                ins = pe.matmul(bk("logitT")[0:NR, :], wr[:, k, :], hT[:, k, :], start=(k == 0), stop=(k == DK - 1))
            filled(ins, "logitT")

            def ple(q):
                t, half = q // 2, q % 2
                banks.wait_free(pe, ("ple", q))
                for k in range(PK):
                    ins = pe.matmul(bk(("ple", q))[:], pTs[:, k, t * P:(t + 1) * P], wpp[:, k, half * 512:(half + 1) * 512],
                                    start=(k == 0), stop=(k == PK - 1))
                filled(ins, ("ple", q))

            pe.wait_ge(ple_loaded, 32)
            ple(0)
            banks.wait_emptied(pe, "logitT")
            banks.wait_free(pe, "logit")
            for t in range(TT):
                ins = pe.transpose(bk("logit")[:, t * NR:(t + 1) * NR], logT[:, t * P:(t + 1) * P], ident[0:NR, 0:NR])
            filled(ins, "logit")
            for q in range(1, 4):
                ple(q)
            pe.wait_ge(chosen, 1)
            banks.wait_free(pe, "count")
            for t in range(TT):
                ins = pe.matmul(bk("count")[0:NE, 0:1], rt[:, 6, t, :], ones[:, 0:1], start=(t == 0), stop=(t == TT - 1))
            filled(ins, "count")
            banks.wait_free(pe, "rank")
            for t in range(TT):
                for j in range(t + 1):
                    ins = pe.matmul(bk("rank")[:, t * NE:(t + 1) * NE], ones[:] if j < t else c[:, C_UP:C_UP + P],
                                    rt[:, 6, j, :], start=(j == 0), stop=(j == t))
            filled(ins, "rank")
            pe.wait_ge(base_in, 1)
            banks.wait_free(pe, "base")
            before_e = c[0:NE, C_UP:C_UP + NE]
            pe.matmul(bk("base")[:, 0:NE], xb[:], before_e, start=True, stop=True)
            pe.matmul(bk("base")[:, NE:NE + 1], xb[:], ones[0:NE, 0:1], start=True, stop=True)
            filled(pe.matmul(bk("base")[0:NE, NE + 1:NE + 2], before_e, ecnt[:, 8:9], start=True, stop=True), "base")
            for q in range(4, 6):
                ple(q)
            pe.wait_ge(item_in, 1)
            banks.wait_free(pe, "items")
            filled(pe.matmul(bk("items")[0:1, 0:MORE], c[0:NE, C_TOK:C_TOK + 1], ihot[:, 2, :], start=True, stop=True), "items")
            for q in range(6, 2 * TT):
                ple(q)
            pe.wait_ge(list_in, 1)
            for j in range(2 * TT):
                ins = pe.matmul(pb[0][:, 0:2 * ALLP], onehot[:, j, :], numhot[:, j].rearrange("p a g -> p (a g)"),
                                start=(j == 0), stop=(j == 2 * TT - 1))
            ins.then_inc(list_full, 1)

            def turn_tokens(n, s, h):
                if isinstance(n, int) and n == 0:
                    pe.wait_ge(list_ready, 1)
                else:
                    pe.wait_ge(xgT_ready, 2 * n)
                pe.wait_ge(gathered[s], 16 * h + 16)
                for k in range(DK):
                    ins = pe.transpose(pb[k // 4][:, k % 4 * P:(k % 4 + 1) * P], xg[:, s, k * P:(k + 1) * P], ident)
                ins.then_inc(xgT_full, 1)

            def pair(n, s, h, last):
                pe.wait_ge(xgT_ready, 2 * (n + 1))
                wait(pe, hid_ready, n - 1)
                for a in range(2):
                    pe.wait_ge(up_loaded[s][a], 32 * h + 32)
                for k in range(DK):
                    for a in range(2):
                        ins = pe.matmul(pb[2 + s][a * CAP:(a + 1) * CAP, :], xgT[:, s, k, a * CAP:(a + 1) * CAP],
                                        up_w[s][a][:, :, k, :], start=(k == 0), stop=(k == DK - 1))
                ins.then_inc(up_done, 1)
                if not last:
                    turn_tokens(n + 1, 1 - s, h + s)
                pe.wait_ge(hid_ready, n + 1)
                wait(pe, hidT_ready, n - 1)
                for k in range(FK):
                    ins = pe.transpose(pb[4 + s][:, k * P:(k + 1) * P], hid[:, s, k, :], ident)
                ins.then_inc(hidT_full, 1)
                pe.wait_ge(hidT_ready, n + 1)
                wait(pe, ya_ready, n)
                wait(pe, yd_ready, n)
                for a in range(2):
                    pe.wait_ge(dn_loaded[s][a], 16 * h + 16)
                for half in range(2):
                    for k in range(FK):
                        for a in range(2):
                            ins = pe.matmul(pb[6 + half][a * CAP:(a + 1) * CAP, :], hidT[:, s, k, a * CAP:(a + 1) * CAP],
                                            dn_w[s][a][:, k, half * 512:(half + 1) * 512], start=(k == 0), stop=(k == FK - 1))
                ins.then_inc(down_done[s], 1)

            banks.wait_emptied(pe, "items")
            for q in range(4, 2 * TT):
                banks.wait_emptied(pe, ("ple", q))
            turn_tokens(0, 0, 0)
            steps = expert_pairs(pe, pair, lambda n, h: turn_tokens(n, 0, h))
            pe.wait_ge(ya_ready, 2 * steps + PAIRS)
            pe.wait_ge(yd_ready, 2 * steps + PAIRS)

            def gate(q):
                t, half = q // 2, q % 2
                name = ("pgate", q)
                banks.wait_free(pe, name)
                for k in range(DK):
                    pe.matmul(bk(name)[:], hT[:, k, t * P:(t + 1) * P], wpg[:, k, half * 512:(half + 1) * 512],
                              start=(k == 0), stop=False)
                filled(pe.matmul(bk(name)[:], ones[0:1, :], brow[:, half * 512:(half + 1) * 512], start=False, stop=True), name)

            for t in range(TT + 1):
                if t < TT:
                    turn_rows("h3", t, 2 * TT)
                if t == 0:
                    pe.wait_ge(pg_loaded, 16 * DK // 2)
                    pe.wait_ge(last_loaded, 32)
                if t >= 1:
                    for kh in range(2):
                        name = ("h3", t - 1, kh)
                        banks.wait_emptied(pe, name)
                    gate(2 * (t - 1))
                    gate(2 * t - 1)


def kernel(x, p, g_mix, w_in, w_dw, b_dw, conv_ln_g, conv_ln_b, beta_conv, beta_attn, w_out, g_ffn, w_group, b_group,
           w_erouter, b_erouter, w_gate, w_up, w_down, g_ple, w_ple_gate, b_ple_gate, w_ple_proj, g_final):
    import concourse.bacc as bacc
    from concourse.bass_utils import run_bass_kernel_spmd

    a = np.asarray
    by_channel = np.concatenate([a(w_dw)[0].T, a(b_dw)[0][:, None], a(conv_ln_g)[0][:, None], a(conv_ln_b)[0][:, None],
                                 a(beta_conv)[0][:, None]], axis=1).reshape(CM, P, PM)
    router_bias = np.concatenate([a(b_group)[0], a(b_erouter)[0].reshape(NE), np.zeros(P - NR, np.float32)])
    prm = np.concatenate([by_channel.transpose(1, 0, 2).reshape(P, CM * PM), a(beta_attn)[0].reshape(CM, P).T,
                          a(g_mix)[0].reshape(P, DK), a(g_ffn)[0].reshape(P, DK), a(g_ple)[0].reshape(P, DK),
                          router_bias[:, None]], axis=1)
    w_r = np.concatenate([a(w_group)[0], a(w_erouter)[0].transpose(1, 0, 2).reshape(D, NE)], axis=1)
    arrays = {
        "x_in": a(x)[0], "w_in_in": a(w_in)[0], "w_out_in": a(w_out)[0], "w_r_in": w_r, "w_gate_in": a(w_gate)[0],
        "w_up_in": a(w_up)[0], "w_down_in": a(w_down)[0], "w_pg_in": a(w_ple_gate)[0], "w_pp_in": a(w_ple_proj)[0],
        "pT_in": a(p)[0, 0].T, "b_pg_in": a(b_ple_gate), "g_final_in": a(g_final), "prm_in": prm, "cst_in": constants(),
    }
    arrays = {name: np.ascontiguousarray(v) for name, v in arrays.items()}
    nc = bacc.Bacc("TRN2", target_bir_lowering=False, num_devices=1)
    args = [nc.dram_tensor(name, v.shape, mybir.dt.from_np(v.dtype), kind="ExternalInput").ap() for name, v in arrays.items()]
    out = nc.dram_tensor("out_rows", (S, D), F32, kind="ExternalOutput").ap()
    build(nc, *args, out)
    result = run_bass_kernel_spmd(nc, [arrays], core_ids=[0])
    return result.results[0]["out_rows"].reshape(1, S, D)
```

```python
from contextlib import ExitStack

import concourse.bass as bass
import concourse.mybir as mybir
import numpy as np

F32 = mybir.dt.float32
F32R = mybir.dt.float32r
I32 = mybir.dt.int32
ALU = mybir.AluOpType
ACT = mybir.ActivationFunctionType
AX = mybir.AxisListType

P = 128
D = 1024
S = 512
TT = S // P
DK = D // P
CH = 512
CM = CH // P
NH = 8
DH = 64
TAPS = 31
GLU2, GLU3 = 9, 16
TURNS0, TURNS2 = (21, 25), (0, 4, 9, 14, 19, 24)
EPS = 1e-6
NG, NE, EG = 4, 32, 8
NR = NG + NE
F = 256
FK = F // P
CAP = 64
PAIRS = NE // 2
MOST = PAIRS + 2 * S // CAP
HALVES = MOST // 2
LISTS = MOST + 2
STEPS = S // CAP - 1
PD = 256
PK = PD // P
NOWHERE = 4 * S
ROOTS = 3 * TT + 2
FAR = 3.0e38
ROT, THETA = 16, 500000.0

C_ID, C_UP, C_ROT, C_IOTA = 0, P, 2 * P, 3 * P
C_MASK = 4 * P
C_COS = C_MASK + S
C_SIN = C_COS + S
C_RANK = C_SIN + S
C_SIDE = C_RANK + NE
C_GRP = C_SIDE + NE
C_TOK = C_GRP + NG
C_ROW = C_TOK + 2 * TT
C_THR = C_ROW + 2 * TT
C_TWO = C_THR + STEPS
C_EPS = C_TWO + HALVES
C_END = C_EPS + 1
PM = TAPS + 4
Q_BETA = CM * PM
Q_MIX, Q_FFN, Q_PLE = Q_BETA + CM, Q_BETA + CM + DK, Q_BETA + CM + 2 * DK
Q_RB = Q_BETA + CM + 3 * DK
Q_END = Q_RB + 1


def constants():
    c = np.zeros((P, C_END), np.float32)
    i = np.arange(P)
    c[:, C_ID:C_ID + P] = np.eye(P)
    c[:, C_UP:C_UP + P] = i[:, None] < i[None, :]
    for m in range(P):
        d = m % DH
        if d < ROT // 2:
            c[m + ROT // 2, C_ROT + m] = -1.0
        elif d < ROT:
            c[m - ROT // 2, C_ROT + m] = 1.0
    c[:, C_IOTA:C_IOTA + P] = i[None, :]
    c[:, C_MASK + S - P:C_MASK + S] = np.where(i[None, :] <= i[:, None], 0.0, -FAR)
    inv = np.power(np.float32(THETA), -np.arange(0, ROT, 2, dtype=np.float32) / np.float32(ROT))
    ang = np.arange(S, dtype=np.float32)[:, None] * inv[None, :]
    d = i % DH
    turned = d < ROT
    c[:, C_COS:C_COS + S] = np.where(turned[:, None], np.cos(ang).T[d % (ROT // 2)], 1.0)
    c[:, C_SIN:C_SIN + S] = np.where(turned[:, None], np.sin(ang).T[d % (ROT // 2)], 0.0)
    e = np.arange(NE)
    c[:, C_RANK:C_RANK + NE] = NE - e
    c[:, C_SIDE:C_SIDE + NE] = CAP * (e % 2)
    c[:, C_GRP:C_GRP + NG] = NG - np.arange(NG)
    tok = i[:, None] + P * np.arange(TT)[None, :]
    c[:, C_TOK:C_TOK + 2 * TT] = NOWHERE - np.tile(tok, (1, 2))
    c[:, C_ROW:C_ROW + 2 * TT] = NOWHERE - np.concatenate([tok, tok + S], axis=1)
    c[:, C_THR:C_THR + STEPS] = CAP * np.arange(1, STEPS + 1)
    c[:, C_TWO:C_TWO + HALVES] = 2 * np.arange(HALVES)
    c[:, C_EPS] = EPS
    return c


class Banks:

    def __init__(self, full, free):
        self.full, self.free = full, free
        self.place, self.count = {}, [0] * len(full)

    def use(self, name, bank):
        self.count[bank] += 1
        self.place[name] = (bank, self.count[bank])

    def bank(self, name):
        return self.place[name][0]

    def wait_full(self, eng, name):
        b, n = self.place[name]
        eng.wait_ge(self.full[b], n)

    def wait_free(self, eng, name):
        b, n = self.place[name]
        if n > 1:
            eng.wait_ge(self.free[b], n - 1)

    def wait_emptied(self, eng, name):
        b, n = self.place[name]
        eng.wait_ge(self.free[b], n)


def plan_banks(banks):
    for k in range(DK):
        banks.use(("x", k), k)
    for m in range(CM):
        banks.use(("val", m), m)
        banks.use(("gate", m), 4 + m)
    for j in range(2 * CM + 1):
        if j < 2 * CM:
            banks.use(("raw", j), j % 2)
        if j >= 1:
            banks.use(("rot", j - 1), 2 + (j - 1) % 2)
    banks.use("mean", 0)
    for t in range(TT):
        banks.use(("v", t), 4 + t)
        if t == 0:
            banks.use("var", 1)
    for u in range(CM * TT):
        for hh in range(2):
            banks.use(("score", u, hh), 2 * (u % 2) + hh)
            banks.use(("probT", u, hh), 4 + hh)
        if u % TT == 0:
            banks.use(("attn", u // TT), 6)
    banks.use("conv_sq", 7)
    for q in range(2 * TT):
        banks.use(("outc", q), 7)
    banks.use("attn_sq", 6)
    for q in range(2 * TT):
        banks.use(("outa", q), q % 4)
    for t in range(TT):
        for kh in range(2):
            banks.use(("h2", t, kh), 6 + kh)
    banks.use("logitT", 0)
    banks.use("logit", 1)
    for q in range(2 * TT):
        banks.use(("ple", q), 4 + q % 4)
    banks.use("count", 3)
    banks.use("rank", 2)
    for t in range(TT):
        for kh in range(2):
            banks.use(("x2", t, kh), 2 * (t % 2) + kh)
    banks.use("rootT", 7)
    for q in range(2 * TT):
        banks.use(("pgate", q), 4 + q % 3)


def build(nc, x, w_in, w_out, w_r, w_gate, w_up, w_down, w_pg, w_pp, pT, b_pg, g_final, prm, cst, out):
    ctx = ExitStack()
    with ctx:
        def sb(name, shape, dt=F32):
            return ctx.enter_context(nc.sbuf_tensor(name, shape, dt))

        def over(name, start, lo, k, n):
            return nc.alloc_sbuf_tensor_at(name, [P, k, n], F32R, offset=start + 4 * lo)

        def sem(name):
            return ctx.enter_context(nc.semaphore(name))

        rows_d = nc.dram_tensor("rows_d", [S, D], F32).ap()
        y_d = nc.dram_tensor("y_d", [2 * S, D], F32).ap()

        xs_start = nc.sbuf_base + 31
        xs_start -= xs_start % 32
        xs = sb("xs", [P, TT, D])
        mix_start = nc.sbuf_base + 32 - 1
        mix_start -= mix_start % 32
        mix = sb("mix", [P, 2 * CM * S])
        wring = sb("wring", [P, 2, 2, 3 * 2048])
        wring_start = nc.sbuf_base - 4 * 24576
        arena = sb("arena", [P, 14592])
        arena_start = nc.sbuf_base - 4 * 14592
        c = sb("c", [P, C_END])
        ones = sb("ones", [P, P])
        pr = sb("pr", [P, Q_END])
        wr = sb("wr", [P, DK, NR])
        lnr = sb("lnr", [P, S])
        mean_w = sb("mean_w", [P, P])
        sq = sb("sq", [P, 4, TT])
        ss = sb("ss", [P, 4, TT])
        rs = sb("rs", [P, 4, TT])
        gss = sb("gss", [P, 2, TT])
        grs = sb("grs", [P, 2, TT])
        nmax = sb("nmax", [P, 2, 2])
        psum_p = sb("psum_p", [P, 2, 2])
        pinv = sb("pinv", [P, 2, 2])
        lg = sb("lg", [P, TT, NR])
        rt = sb("rt", [P, 8, TT, NE])
        hot = sb("hot", [P, 2, TT, NE])
        sm = sb("sm", [P, 8, TT])
        by8 = sb("by8", [P, 7, 2 * TT])
        gw = sb("gw", [P, 2, TT])
        beyond = sb("beyond", [P, NE])
        scan = sb("scan", [P, 3, PAIRS // 2 + PAIRS])
        ofpair = sb("ofpair", [P, 2, MOST])
        fewer = sb("fewer", [P, HALVES + 1])
        halves = sb("halves", [1, 2], I32)
        first = sb("first", [1, PAIRS], I32)
        pass_of = sb("pass_of", [1, 2, MOST], I32)
        tlist = sb("tlist", [P, 2, LISTS], I32)
        tcur = sb("tcur", [P, 2], I32)
        ycur = sb("ycur", [P, 2], I32)

        def ar(lo, n):
            return arena[:, lo:lo + n]

        ident = c[:, C_ID:C_ID + P]
        logT = lnr[0:NR, :]
        mixc = mix[:, 0:CM * S].rearrange("p (m t) -> p m t", m=CM)
        mixa = mix[:, CM * S:2 * CM * S].rearrange("p (m t) -> p m t", m=CM)
        plep = mix[:, :].rearrange("p (t n) -> p t n", t=TT)
        hT = ar(0, DK * S).rearrange("p (k t) -> p k t", k=DK)
        probT = ar(0, 4 * 2 * S).rearrange("p (b h k) -> p b h k", b=4, h=2)
        xg = ar(0, 2 * D).rearrange("p (b n) -> p b n", b=2)
        xgT = ar(2048, 2 * D).rearrange("p (b k t) -> p b k t", b=2, k=DK)
        qz = ar(4096, NH * S).rearrange("p (h t) -> p h t", h=NH)
        xn = ar(4096, TT * D).rearrange("p (t k n) -> p t k n", t=TT, k=DK)
        xn_rows = ar(4096, TT * D).rearrange("p (t n) -> p t n", t=TT)
        yb = ar(4096, 2 * D).rearrange("p (b n) -> p b n", b=2)
        sil = ar(6144, 2 * F).rearrange("p (b n) -> p b n", b=2)
        hid = ar(6656, 2 * F).rearrange("p (b k n) -> p b k n", b=2, k=FK)
        hidT = ar(7168, 2 * F).rearrange("p (b k t) -> p b k t", b=2, k=FK)
        kT = ar(8192, CM * S).rearrange("p (m t) -> p m t", m=CM)
        wpp = ar(8192, PK * D).rearrange("p (k n) -> p k n", k=PK)
        vr = ar(10240, TT * CH).rearrange("p (t n) -> p t n", t=TT)
        pTs = ar(10240, PK * S).rearrange("p (k t) -> p k t", k=PK)
        onehot = ar(11264, 2 * TT * P).rearrange("p (j n) -> p j n", j=2 * TT)
        U = S + TAPS - 1
        u = ar(12288, CM * U).rearrange("p (m t) -> p m t", m=CM)
        sqa = ar(12288, CM * S).rearrange("p (m t) -> p m t", m=CM)
        free = 12288 + D
        cmp8 = ar(free, 2 * TT * LISTS).rearrange("p (j g) -> p j g", j=2 * TT)
        passhot = ar(free + 2 * TT * LISTS, 2 * TT * LISTS).rearrange("p (j g) -> p j g", j=2 * TT)
        numhot = ar(free + 4 * TT * LISTS, 4 * TT * LISTS).rearrange("p (j a g) -> p j a g", j=2 * TT, a=2)
        ended = ar(12288, MOST * PAIRS).rearrange("p (n g) -> p n g", n=MOST)
        sg = mixa
        qraw = mixa[:, 0:2, :]
        qsin = mixa[:, 2:4, :]
        sqc = mixa

        junk0 = mix[:, 0:D]
        junk = ar(12288, D)

        flat = [wring[:, s].rearrange("p a n -> p (a n)") for s in range(2)]
        win = [flat[i // 3][:, (i % 3) * 4096:(i % 3 + 1) * 4096].rearrange("p (k n) -> p k n", k=DK)
               for i in (0, 1, 2, 3, 2)]
        woc = flat[1][:, 8192:12288].rearrange("p (m n) -> p m n", m=CM)
        woa = flat[1][:, 0:4096].rearrange("p (m n) -> p m n", m=CM)
        prob = flat[1][:, 4096:8192].rearrange("p (b h k) -> p b h k", b=4, h=2)
        wpg = [ar(8192, 4096).rearrange("p (k n) -> p k n", k=DK), flat[0][:, 0:4096].rearrange("p (k n) -> p k n", k=DK)]
        hT_hi, hT_lo = over("hT_hi", arena_start, 0, DK, S), over("hT_lo", xs_start, 0, DK, S)
        win_lo = [over(f"win_lo{i}", wring_start, 4096 * i, DK, 512) for i in range(4)]
        win_hi = [over(f"win_hi{i}", wring_start, 12288 + 4096 * (i + 1), DK, 512) for i in range(2)]
        win_hi += [win_hi[0], win_hi[1], win_lo[1]]
        win_lo += [win_lo[2]]
        wo_hi = [over("woc_hi", wring_start, 0, CM, D), over("woa_hi", wring_start, 6144, CM, D)]
        wo_lo = [over("woc_lo", wring_start, 12288 + 8192, CM, D), over("woa_lo", wring_start, 12288, CM, D)]
        mix_hi = [over("mixc_hi", wring_start, 4096, CM, S), over("mixa_hi", wring_start, 10240, CM, S)]
        mix_lo = [over("mixc_lo", mix_start, 0, CM, S), over("mixa_lo", mix_start, CM * S, CM, S)]
        wpg_hi = [over("wpg_hi0", wring_start, 8192, DK, 512), over("wpg_hi1", wring_start, 4096, DK, 512)]
        wpg_lo = [over("wpg_lo0", arena_start, 8192, DK, 512), over("wpg_lo1", wring_start, 0, DK, 512)]
        x2_hi = over("x2_hi", arena_start, 0, DK, S)
        x2_lo = [over(f"x2_lo{t}", wring_start, 12288 + 2 * t * D, DK, P) for t in range(TT)]
        rootT = lnr[0:1, :]
        yg = flat[1][:, 0:8 * D].rearrange("p (j n) -> p j n", j=8)
        gfin = flat[1][:, 8 * D:9 * D]
        brow = flat[1][0:1, 9 * D:10 * D]
        sgate = flat[1][:, 10 * D:12 * D].rearrange("p (b n) -> p b n", b=4)

        def up_w(s, a):
            return wring[:, s, a, 0:4096].rearrange("p (w k n) -> p w k n", w=2, k=DK)

        def dn_w(s, a):
            return wring[:, s, a, 4096:6144].rearrange("p (k n) -> p k n", k=FK)

        pb = [ctx.enter_context(nc.psum_tensor(f"bank{i}", [P, 512], F32)) for i in range(8)]
        banks = Banks([sem(f"bank_full{i}") for i in range(8)], [sem(f"bank_free{i}") for i in range(8)])
        plan_banks(banks)

        def bk(name):
            return pb[banks.bank(name)]

        def filled(ins, name):
            ins.then_inc(banks.full[banks.bank(name)], 1)

        def emptied(ins, name):
            ins.then_inc(banks.free[banks.bank(name)], 1)

        x_loaded = [sem(f"x_loaded{t}") for t in range(TT)]
        x_again = sem("x_again")
        hT_hi_ready = sem("hT_hi_ready")
        win_hi_ready = [sem(f"win_hi_ready{i}") for i in range(5)]
        win_lo_ready = [sem(f"win_lo_ready{i}") for i in range(5)]
        win_loaded = [sem(f"win_loaded{i}") for i in range(5)]
        woc_loaded, woa_loaded = sem("woc_loaded"), sem("woa_loaded")
        const_loaded = sem("const_loaded")
        prm_loaded = sem("prm_loaded")
        ple_loaded = sem("ple_loaded")
        pg_loaded = [sem(f"pg_loaded{h}") for h in range(2)]
        last_loaded = sem("last_loaded")
        pads_set = sem("pads_set")
        qz_set = sem("qz_set")
        root_ready = sem("root_ready")
        xn_ready = sem("xn_ready")
        tap_done = sem("tap_done")
        qcos_done = sem("qcos_done")
        rope_done = sem("rope_done")
        centred = sem("centred")
        csq_ready = sem("csq_ready")
        lnr_ready = sem("lnr_ready")
        z_ready = sem("z_ready")
        silu_ready = sem("silu_ready")
        osq_ready = sem("osq_ready")
        wo_hi_ready = [sem(f"wo_hi_ready{w}") for w in range(2)]
        wo_lo_ready = [sem(f"wo_lo_ready{w}") for w in range(2)]
        mix_hi_ready = [sem(f"mix_hi_ready{w}") for w in range(2)]
        mix_lo_ready = [sem(f"mix_lo_ready{w}") for w in range(2)]
        exp_ready = sem("exp_ready")
        pinv_ready = sem("pinv_ready")
        prob_ready = sem("prob_ready")
        sqa_ready = sem("sqa_ready")
        attended = sem("attended")
        rs_ready = sem("rs_ready")
        rows_stored = sem("rows_stored")
        rstep = sem("rstep")
        exp_in = sem("exp_in")
        exp_out = sem("exp_out")
        chosen = sem("chosen")
        list_in = sem("list_in")
        list_ready = sem("list_ready")
        list_full = sem("list_full")
        plan_ready = sem("plan_ready")
        up_loaded = [sem(f"up_loaded{s}") for s in range(2)]
        dn_loaded = [sem(f"dn_loaded{s}") for s in range(2)]
        up_ready, dn_ready = sem("up_ready"), sem("dn_ready")
        sp_go = sem("sp_go")
        pool_go = sem("pool_go")
        tcur_ready = sem("tcur_ready")
        ycur_ready = sem("ycur_ready")
        gathered = [sem(f"gathered{s}") for s in range(2)]
        xgT_full = sem("xgT_full")
        xgT_ready = sem("xgT_ready")
        up_done = sem("up_done")
        sil_ready = sem("sil_ready")
        hid_ready = sem("hid_ready")
        hidT_full = sem("hidT_full")
        hidT_ready = sem("hidT_ready")
        down_done = sem("down_done")
        ya_ready, yd_ready = sem("ya_ready"), sem("yd_ready")
        y_stored = [sem(f"y_stored{s}") for s in range(2)]
        yg_loaded = [sem(f"yg_loaded{j}") for j in range(2 * TT)]
        x2_ready = sem("x2_ready")
        whi_ready, wlo_ready = sem("whi_ready"), sem("wlo_ready")
        xhi_ready = sem("xhi_ready")
        x3_ready = sem("x3_ready")
        o_ready = sem("o_ready")
        out_stored = sem("out_stored")

        def wait(eng, s, v):
            if not isinstance(v, int) or v > 0:
                eng.wait_ge(s, v)

        def number(eng, ap, least, most):
            return eng.value_load(ap, min_val=least, max_val=most)

        def all_passes(eng, one):
            for s in range(2):
                one(s, s, 0)
            eng.wait_ge(plan_ready, 1)
            half = number(eng, halves[0:1, 0:1], PAIRS // 2, HALVES)
            with eng.Fori(1, half) as i:
                for s in range(2):
                    one(2 * i + s, s, i)
            return half

        block = ctx.enter_context(nc.Block())

        @block.sync
        def _(sp):
            for t in range(TT):
                sp.dma_start(xs[:, t, :], x[t * P:(t + 1) * P, :]).then_inc(x_loaded[t], 16)
            w_in_k = w_in.rearrange("(p k) n -> p k n", k=DK)
            for i in range(4):
                sp.dma_start(win[i], w_in_k[:, :, i * 512:(i + 1) * 512]).then_inc(win_loaded[i], 16)
            banks.wait_full(sp, ("raw", 3))
            sp.dma_start(win[4], w_in_k[:, :, 4 * 512:5 * 512]).then_inc(win_loaded[4], 16)
            banks.wait_full(sp, ("raw", 7))
            sp.dma_start(woc, w_out[0:CH, :].rearrange("(m p) n -> p m n", p=P)).then_inc(woc_loaded, 16)
            sp.dma_start(woa, w_out[CH:2 * CH, :].rearrange("(m p) n -> p m n", p=P)).then_inc(woa_loaded, 16)
            banks.wait_full(sp, ("v", TT - 1))
            sp.dma_start(xs[:], x.rearrange("(t p) n -> p t n", p=P)).then_inc(x_again, 16)

            def load_up(s, g, a):
                for w, src in enumerate((w_gate, w_up)):
                    sp.dma_start(up_w(s, a)[:, w],
                                 src[bass.ds(2 * g + a, 1)].rearrange("e (p k) n -> p (e k) n", k=DK)
                                 ).then_inc(up_loaded[s], 16)

            def load_down(s, g, a):
                sp.dma_start(dn_w(s, a),
                             w_down[bass.ds(2 * g + a, 1)].rearrange("e (p k) n -> p (e k) n", k=FK)
                             ).then_inc(dn_loaded[s], 16)

            def passed_on(s, h):
                sp.wait_ge(up_loaded[s], 64 * h)
                sp.sem_inc(up_ready, 1)
                sp.wait_ge(dn_loaded[s], 32 * h)
                sp.sem_inc(dn_ready, 1)

            banks.wait_full(sp, ("outc", 2 * TT - 1))
            load_up(0, 0, 0)
            load_down(0, 0, 0)
            banks.wait_full(sp, ("attn", CM - 1))
            sp.dma_start(wpp, w_pp.rearrange("(p k) n -> p k n", k=PK)).then_inc(ple_loaded, 16)
            sp.dma_start(pTs, pT.rearrange("(p k) n -> p k n", k=PK)).then_inc(ple_loaded, 16)
            banks.wait_full(sp, ("outa", 2 * TT - 1))
            load_up(0, 0, 1)
            load_down(0, 0, 1)
            for a in range(2):
                load_up(1, 1, a)
            for a in range(2):
                load_down(1, 1, a)
            passed_on(0, 1)
            for q in range(TT, 2 * TT):
                banks.wait_full(sp, ("ple", q))
            sp.wait_ge(list_full, 1)
            pg = w_pg.rearrange("(k p) n -> p k n", k=DK)
            sp.dma_start(wpg[0], pg[:, :, 0:512]).then_inc(pg_loaded[0], 16)
            sp.wait_ge(plan_ready, 1)
            with sp.Fori(1, PAIRS // 2) as i:
                for s in range(2):
                    g = 2 * i + s
                    done = number(sp, first[0:1, bass.ds(g - 1, 1)], 1, MOST)
                    sp.wait_ge(up_done, done)
                    sp.sem_inc(sp_go, 1)
                    for a in range(2):
                        load_up(s, g, a)
                    sp.wait_ge(down_done, done)
                    sp.sem_inc(sp_go, 1)
                    for a in range(2):
                        load_down(s, g, a)
                    passed_on(1 - s, i + s)
            passed_on(1, PAIRS // 2)
            half = number(sp, halves[0:1, 0:1], PAIRS // 2, HALVES)
            sp.wait_ge(down_done, 2 * half)
            sp.sem_inc(sp_go, 1)
            for s in range(2):
                sp.wait_ge(y_stored[s], 16 * half)
                sp.sem_inc(sp_go, 1)
            y_rows = y_d.rearrange("(k t p) n -> p t k n", k=2, p=P)
            for t in range(TT):
                for k in range(2):
                    sp.dma_start(yg[:, 2 * t + k, :], y_rows[:, t, k]).then_inc(yg_loaded[2 * t + k], 16)
            sp.dma_start(wpg[1], pg[:, :, 512:D]).then_inc(pg_loaded[1], 16)
            sp.dma_start(gfin, g_final.partition_broadcast(P)).then_inc(last_loaded, 16)
            sp.dma_start(brow, b_pg).then_inc(last_loaded, 16)
            for q in range(2 * TT):
                t, cols = q // 2, slice(q % 2 * 512, (q % 2 + 1) * 512)
                sp.wait_ge(o_ready, q + 1)
                sp.dma_start(out[t * P:(t + 1) * P, cols], xn_rows[:, t, cols]).then_inc(out_stored, 16)
            sp.wait_ge(out_stored, 16 * 2 * TT)

        @block.gpsimd
        def _(pool):
            qz_h = qz.rearrange("p (m h) t -> p m h t", h=2)
            def split_in(i, lo, hi):
                pool.tensor_tensor(win_lo[i][:, :, lo:hi], win[i][:, :, lo:hi], win_hi[i][:, :, lo:hi].bitcast(F32),
                                   ALU.subtract).then_inc(win_lo_ready[i], 1)

            for i in (0, 2):
                for m in range(CM):
                    for j in range(i, i + 2):
                        pool.wait_ge(win_hi_ready[j], m + 1)
                        split_in(j, m * P, (m + 1) * P)
                if i == 0:
                    banks.wait_full(pool, ("x", DK - 1))
                    pool.wait_ge(win_lo_ready[1], CM)
                    pool.memset(qz_h[64:128, :, 0, :], 0.0).then_inc(qz_set, 1)
                    pool.wait_ge(qz_set, 1)
                    pool.memset(qz_h[0:64, :, 1, :], 0.0).then_inc(qz_set, 1)
                    pool.wait_ge(qz_set, 2)
            pool.wait_ge(const_loaded, 32)
            for j in range(2 * CM):
                b = j % 2
                if j == CM:
                    pool.wait_ge(rope_done, 2 * CM)
                    for m in range(CM):
                        pool.wait_ge(win_hi_ready[4], m + 1)
                        split_in(4, m * P, (m + 1) * P)
                banks.wait_full(pool, ("rot", j))
                if j >= 1:
                    pool.wait_ge(rope_done, 2 * j if j <= CM else CM + j)
                pool.tensor_tensor(qraw[:, b, :], qraw[:, b, :], c[:, C_COS:C_COS + S], ALU.mult).then_inc(qcos_done, 1)
                pool.wait_ge(qcos_done, j + 1)
                banks.wait_emptied(pool, ("rot", j))
                if j < CM:
                    for hh in range(2):
                        rows = slice(hh * DH, (hh + 1) * DH)
                        if hh == 1:
                            pool.wait_ge(rope_done, 2 * j + 1)
                        pool.tensor_tensor(qz[rows, 2 * j + hh, :], qraw[rows, b, :], qsin[rows, b, :],
                                           ALU.add).then_inc(rope_done, 1)
                else:
                    pool.tensor_tensor(kT[:, j - CM, :], qraw[:, b, :], qsin[:, b, :], ALU.add).then_inc(rope_done, 1)
            pool.wait_ge(rope_done, 3 * CM)
            for w, (squares, whole) in enumerate(((osq_ready, mixc), (sqa_ready, mixa))):
                for m in range(CM):
                    pool.wait_ge(squares, m + 1)
                    pool.wait_ge(mix_hi_ready[w], m + 1)
                    pool.tensor_tensor(mix_lo[w][:, m, :], whole[:, m, :], mix_hi[w][:, m, :].bitcast(F32),
                                       ALU.subtract).then_inc(mix_lo_ready[w], 1)
            for t in range(TT):
                pool.wait_ge(xn_ready, TT + t + 1)
                pool.dma_start(rows_d[t * P:(t + 1) * P, :], xn_rows[:, t, :]).then_inc(rows_stored, 16)
            pool.wait_ge(rows_stored, 16 * TT)

            def gather(n, s, h):
                wait(pool, xgT_full, n - 1)
                pool.sem_inc(pool_go, 1)
                wait(pool, gathered[s], 16 * h)
                pool.sem_inc(pool_go, 1)
                pool.tensor_copy(tcur[:, s:s + 1], tlist[:, 0, bass.ds(n, 1)]).then_inc(tcur_ready, 1)
                pool.wait_ge(tcur_ready, n + 1)
                pool.sem_inc(pool_go, 1)
                pool.indirect_dma_start(xg[:, s, :], None, rows_d,
                                        bass.IndirectOffsetOnAxis(ap=tcur[:, s:s + 1], axis=0),
                                        bounds_check=S - 1, oob_is_err=False).then_inc(gathered[s], 16)

            def scatter(n, s, h):
                pool.wait_ge(ya_ready, n + 1)
                pool.sem_inc(pool_go, 1)
                pool.wait_ge(yd_ready, n + 1)
                pool.sem_inc(pool_go, 1)
                wait(pool, y_stored[s], 16 * h)
                pool.sem_inc(pool_go, 1)
                pool.tensor_copy(ycur[:, s:s + 1], tlist[:, 1, bass.ds(n, 1)]).then_inc(ycur_ready, 1)
                pool.wait_ge(ycur_ready, n + 1)
                pool.sem_inc(pool_go, 1)
                pool.indirect_dma_start(y_d, bass.IndirectOffsetOnAxis(ap=ycur[:, s:s + 1], axis=0), yb[:, s, :], None,
                                        bounds_check=2 * S - 1, oob_is_err=False).then_inc(y_stored[s], 16)

            pool.wait_ge(list_ready, 2)
            for s in range(2):
                gather(s, s, 0)
            pool.wait_ge(plan_ready, 1)
            half = number(pool, halves[0:1, 0:1], PAIRS // 2, HALVES)
            with pool.Fori(1, half) as i:
                for s in range(2):
                    gather(2 * i + s, s, i)
                    scatter(2 * i + s - 2, s, i - 1)
            before = number(pool, halves[0:1, 1:2], PAIRS // 2 - 1, HALVES - 1)
            gather(2 * before + 2, 0, before + 1)
            for s in range(2):
                scatter(2 * before + s, s, before)

        @block.scalar
        def _(act):
            act.dma_start(c[:, 0:C_MASK], cst[:, 0:C_MASK]).then_inc(const_loaded, 16)
            act.dma_start(c[:, C_MASK:C_END], cst[:, C_MASK:C_END]).then_inc(const_loaded, 16)
            act.dma_start(pr[:], prm).then_inc(prm_loaded, 16)
            act.dma_start(wr[:], w_r.rearrange("(p k) n -> p k n", k=DK)).then_inc(prm_loaded, 16)
            eps = c[:, C_EPS:C_EPS + 1]

            def mean_root(which, t, unused):
                act.activation(unused, xs[:, t, :], ACT.Square, accum_out=sq[:, which, t:t + 1]).then_inc(root_ready, 1)
                act.wait_ge(root_ready, 2 * (which * TT + t) + 1)
                act.activation(ss[:, which, t:t + 1], sq[:, which, t:t + 1], ACT.Sqrt, scale=1.0 / D, bias=eps).then_inc(root_ready, 1)

            act.wait_ge(const_loaded, 32)
            for t in range(TT):
                act.wait_ge(x_loaded[t], 16)
                mean_root(0, t, junk0)
            act.wait_ge(prm_loaded, 32)
            def split_in(i, m):
                if m == 0:
                    act.wait_ge(win_loaded[i], 16)
                cols = slice(m * P, (m + 1) * P)
                act.activation(win_hi[i][:, :, cols], win[i][:, :, cols], ACT.Copy).then_inc(win_hi_ready[i], 1)

            split_in(0, 0)
            for k in range(DK):
                banks.wait_full(act, ("x", k))
                act.activation(hT_hi[:, k, :], bk(("x", k))[:], ACT.Copy,
                               scale=pr[:, Q_MIX + k:Q_MIX + k + 1]).then_inc(hT_hi_ready, 1)

            for m in range(CM):
                for i in range(2):
                    if m + i > 0:
                        split_in(i, m)
            for m in range(CM):
                banks.wait_full(act, ("gate", m))
                emptied(act.activation(sg[:, m, :], bk(("gate", m))[:], ACT.Sigmoid), ("gate", m))
                for i in range(2, 4):
                    split_in(i, m)

            def split_out(w, m):
                gain = (m * PM + TAPS + 3, Q_BETA + m)[w]
                act.activation(wo_hi[w][:, m, :], (woc, woa)[w][:, m, :], ACT.Copy,
                               scale=pr[:, gain:gain + 1]).then_inc(wo_hi_ready[w], 1)

            for j in range(2 * CM):
                banks.wait_full(act, ("raw", j))
                banks.wait_emptied(act, ("val", CM - 1))
                if j >= 2:
                    act.wait_ge(rope_done, 2 * (j - 1) if j <= CM else CM + j - 1)
                emptied(act.activation(qraw[:, j % 2, :], bk(("raw", j))[:], ACT.Copy), ("raw", j))
                if j == CM:
                    for m in range(CM):
                        split_in(4, m)
            for t in range(2):
                banks.wait_full(act, ("v", t))
                emptied(act.activation(vr[:, t, :], bk(("v", t))[:], ACT.Copy), ("v", t))
            act.wait_ge(woc_loaded, 16)
            for m in range(CM):
                split_out(0, m)
            act.wait_ge(rope_done, 3 * CM)
            for m in range(CM):
                if m < CM - 1:
                    act.wait_ge(centred, m + 1)
                else:
                    banks.wait_emptied(act, "mean")
                act.activation(sqc[:, m, :], mixc[:, m, :], ACT.Square).then_inc(csq_ready, 1)
            banks.wait_full(act, "var")
            emptied(act.activation(lnr[:], bk("var")[:], ACT.Sqrt, bias=eps), "var")
            for m in range(CM):
                act.wait_ge(z_ready, m + 1)
                base = m * PM + TAPS
                act.activation(mixc[:, m, :], mixc[:, m, :], ACT.Silu, scale=pr[:, base + 1:base + 2],
                               bias=pr[:, base + 2:base + 3]).then_inc(silu_ready, 1)

            def conv_group(u_):
                if u_ == 1:
                    for m in range(CM):
                        act.wait_ge(silu_ready, m + 1)
                        act.activation(sqc[:, m, :], mixc[:, m, :], ACT.Square).then_inc(osq_ready, 1)
                if u_ == 5:
                    act.wait_ge(woa_loaded, 16)
                if 5 <= u_ < 5 + CM:
                    split_out(1, u_ - 5)
                if u_ == 4:
                    banks.wait_full(act, "conv_sq")
                    emptied(act.activation(gss[:, 0, :], bk("conv_sq")[:, 0:TT], ACT.Sqrt, scale=1.0 / CH, bias=eps), "conv_sq")

            def exps(u_):
                i, b = u_ % TT, u_ % 2
                n = P * (i + 1)
                for hh in range(2):
                    banks.wait_emptied(act, ("score", u_, hh))
                    act.activation(prob[:, u_ % 4, hh, 0:n], prob[:, u_ % 4, hh, 0:n], ACT.Exp, scale=-1.0,
                                   bias=nmax[:, b, hh:hh + 1], accum_out=psum_p[:, b, hh:hh + 1]).then_inc(exp_ready, 1)

            def probs_out(u_):
                n = P * (u_ % TT + 1)
                if u_ >= 4:
                    mb, ib = (u_ - 4) // TT, (u_ - 4) % TT
                    if ib == TT - 1:
                        banks.wait_full(act, ("attn", mb))
                    else:
                        act.wait_ge(attended, mb * (TT - 1) + ib + 1)
                for hh in range(2):
                    banks.wait_full(act, ("probT", u_, hh))
                    emptied(act.activation(probT[:, u_ % 4, hh, 0:n], bk(("probT", u_, hh))[:, 0:n], ACT.Copy), ("probT", u_, hh))

            def attn_sq(m):
                banks.wait_emptied(act, ("attn", m))
                act.activation(mix_hi[1][:, m, :], mixa[:, m, :], ACT.Copy).then_inc(mix_hi_ready[1], 1)
                act.activation(sqa[:, m, :], mixa[:, m, :], ACT.Square).then_inc(sqa_ready, 1)

            units = CM * TT
            for u_ in range(units + 2):
                if u_ < units:
                    exps(u_)
                conv_group(u_)
                if u_ % TT == 3 and u_ > TT:
                    attn_sq(u_ // TT - 1)
                if u_ >= 2:
                    probs_out(u_ - 2)
            attn_sq(CM - 1)
            banks.wait_full(act, "attn_sq")
            emptied(act.activation(gss[:, 1, :], bk("attn_sq")[:, 0:TT], ACT.Sqrt, scale=1.0 / CH, bias=eps), "attn_sq")
            for t in range(TT):
                banks.wait_emptied(act, ("outa", 2 * t + 1))
                mean_root(1, t, junk)
            banks.wait_full(act, "logitT")
            emptied(act.activation(logT, bk("logitT")[0:NR, :], ACT.Identity, bias=pr[0:NR, Q_RB:Q_RB + 1]), "logitT")

            def ple_out(q):
                banks.wait_full(act, ("ple", q))
                if q == 0:
                    banks.wait_full(act, ("outa", 2 * TT - 1))
                emptied(act.activation(plep[:, q // 2, (q % 2) * 512:(q % 2 + 1) * 512], bk(("ple", q))[:], ACT.Copy),
                        ("ple", q))

            act.wait_ge(exp_in, 1)
            act.activation(rt[:, 0, :, 0:NG], rt[:, 0, :, 0:NG], ACT.Exp).then_inc(exp_out, 1)
            act.wait_ge(exp_in, 2)
            act.activation(sm[:, 6, :], sm[:, 6, :], ACT.Exp).then_inc(exp_out, 1)
            for q in range(2 * TT):
                ple_out(q)

            def one(n, s, h):
                act.wait_ge(up_done, n + 1)
                wait(act, hid_ready, n - 1)
                act.activation(sil[:, s, :], pb[2 + s][:, 0:F], ACT.Silu).then_inc(sil_ready, 1)
                act.wait_ge(hidT_full, n + 1)
                wait(act, down_done, n - 1)
                act.activation(hidT[:, s], pb[4 + s][:, 0:F].rearrange("p (k t) -> p k t", k=FK), ACT.Copy).then_inc(hidT_ready, 1)
                act.wait_ge(down_done, n + 1)
                wait(act, y_stored[s], 16 * h)
                act.activation(yb[:, s, 0:512], pb[6][:], ACT.Copy).then_inc(ya_ready, 1)

            half = all_passes(act, one)

            def split_gate(h):
                act.wait_ge(pg_loaded[h], 16)
                for k in range(DK):
                    act.activation(wpg_hi[h][:, k, :], wpg[h][:, k, :], ACT.Copy,
                                   scale=pr[:, Q_PLE + k:Q_PLE + k + 1]).then_inc(whi_ready, 1)

            split_gate(0)
            act.wait_ge(gathered[0], 16 * half + 16)
            for t in range(TT):
                for kh in range(2):
                    banks.wait_full(act, ("x2", t, kh))
                    act.activation(x2_hi[:, 4 * kh:4 * kh + 4, t * P:(t + 1) * P],
                                   bk(("x2", t, kh))[:].rearrange("p (k n) -> p k n", k=4), ACT.Copy).then_inc(xhi_ready, 1)
                mean_root(2, t, junk)
            split_gate(1)
            banks.wait_full(act, "rootT")
            emptied(act.activation(rootT, bk("rootT")[0:1, :], ACT.Copy), "rootT")
            for q in range(2 * TT):
                banks.wait_full(act, ("pgate", q))
                if q >= 4:
                    act.wait_ge(x3_ready, 2 * (q - 3))
                if q == 0:
                    act.wait_ge(rs_ready, ROOTS)
                emptied(act.activation(sgate[:, q % 4, :], bk(("pgate", q))[:], ACT.Sigmoid,
                                       scale=rs[:, 2, q % TT:q % TT + 1]), ("pgate", q))
                if q >= TT:
                    act.wait_ge(x3_ready, 2 * (q + 1))
                    mean_root(3, q - TT, junk)

        @block.vector
        def _(dve):
            dve.memset(ones[:], 1.0).then_inc(pads_set, 1)
            dve.memset(mean_w[:], 1.0 / CH).then_inc(pads_set, 1)
            dve.memset(u[:, :, 0:TAPS - 1], 0.0).then_inc(pads_set, 1)
            dve.memset(scan[:], 0.0).then_inc(pads_set, 1)
            rsn = [0]

            def recip(out_ap, in_ap):
                dve.reciprocal(out_ap, in_ap).then_inc(rs_ready, 1)
                rsn[0] += 1
                dve.wait_ge(rs_ready, rsn[0])

            def permuted(ap):
                return ap.rearrange("p (n k) -> p k n", k=DK)

            def inverse(which, t):
                dve.wait_ge(root_ready, 2 * (which * TT + t) + 2)
                recip(rs[:, which, t:t + 1], ss[:, which, t:t + 1])

            def normal_rows(which, t):
                inverse(which, t)
                dve.tensor_scalar(xn[:, t], permuted(xs[:, t, :]), rs[:, which, t:t + 1], None, ALU.mult).then_inc(xn_ready, 1)

            for t in range(TT):
                normal_rows(0, t)
            dve.wait_ge(prm_loaded, 32)
            for t in range(TT):
                dve.wait_ge(xn_ready, t + 1)
            for k in range(DK):
                dve.wait_ge(hT_hi_ready, k + 1)
                emptied(dve.scalar_tensor_tensor(out=hT_lo[:, k, :], in0=bk(("x", k))[:], scalar=pr[:, Q_MIX + k:Q_MIX + k + 1],
                                                 in1=hT_hi[:, k, :].bitcast(F32), op0=ALU.mult, op1=ALU.subtract), ("x", k))
            taps = [0]

            def glu(m):
                banks.wait_full(dve, ("val", m))
                banks.wait_emptied(dve, ("gate", m))
                if m == 0:
                    dve.wait_ge(pads_set, 4)
                emptied(dve.tensor_tensor(u[:, m, TAPS - 1:U], bk(("val", m))[:], sg[:, m, :], ALU.mult), ("val", m))

            def tap(m, j):
                for mm in (m, m + 1):
                    w = pr[:, mm * PM + j:mm * PM + j + 1]
                    if j == 0:
                        ins = dve.tensor_scalar(mixc[:, mm, :], u[:, mm, 0:S], w, pr[:, mm * PM + TAPS:mm * PM + TAPS + 1],
                                                ALU.mult, ALU.add)
                    else:
                        dve.wait_ge(tap_done, taps[0] - 1)
                        ins = dve.scalar_tensor_tensor(out=mixc[:, mm, :], in0=u[:, mm, j:j + S], scalar=w,
                                                       in1=mixc[:, mm, :], op0=ALU.mult, op1=ALU.add)
                    ins.then_inc(tap_done, 1)
                    taps[0] += 1

            def turn(j):
                banks.wait_full(dve, ("rot", j))
                if j >= 2:
                    dve.wait_ge(rope_done, 2 * (j - 1) if j <= CM else CM + j - 1)
                emptied(dve.tensor_tensor(qsin[:, j % 2, :], bk(("rot", j))[:], c[:, C_SIN:C_SIN + S], ALU.mult), ("rot", j))

            glu(0)
            glu(1)
            banks.wait_emptied(dve, ("val", 1))
            done = 0
            for j in range(TAPS):
                tap(0, j)
                if j in (GLU2, GLU3):
                    glu(2 if j == GLU2 else 3)
                if j in TURNS0:
                    turn(done)
                    done += 1
            banks.wait_emptied(dve, ("val", 3))
            for j in range(TAPS):
                tap(2, j)
                if j in TURNS2:
                    turn(done)
                    done += 1
            banks.wait_full(dve, "mean")
            for m in range(CM):
                ins = dve.tensor_tensor(mixc[:, m, :], mixc[:, m, :], bk("mean")[:], ALU.subtract)
                if m < CM - 1:
                    ins.then_inc(centred, 1)
            emptied(ins, "mean")

            def split_out(w, m):
                gain = (m * PM + TAPS + 3, Q_BETA + m)[w]
                dve.wait_ge(wo_hi_ready[w], m + 1)
                dve.scalar_tensor_tensor(out=wo_lo[w][:, m, :], in0=(woc, woa)[w][:, m, :], scalar=pr[:, gain:gain + 1],
                                         in1=wo_hi[w][:, m, :].bitcast(F32), op0=ALU.mult,
                                         op1=ALU.subtract).then_inc(wo_lo_ready[w], 1)

            for m in range(CM):
                split_out(0, m)
            banks.wait_emptied(dve, "var")
            dve.reciprocal(lnr[:], lnr[:]).then_inc(lnr_ready, 1)
            dve.wait_ge(lnr_ready, 1)
            dve.wait_ge(csq_ready, CM)
            for m in range(CM):
                dve.tensor_tensor(mixc[:, m, :], mixc[:, m, :], lnr[:], ALU.mult).then_inc(z_ready, 1)

            def scores(u_):
                i, b = u_ % TT, u_ % 2
                n = P * (i + 1)
                for hh in range(2):
                    banks.wait_full(dve, ("score", u_, hh))
                    if u_ >= 4 and hh == 0:
                        banks.wait_full(dve, ("probT", u_ - 4, 1))
                    ins = nc.vector.tensor_tensor_reduce(out=prob[:, u_ % 4, hh, 0:n], in0=bk(("score", u_, hh))[:, 0:n],
                                                         in1=c[:, C_MASK + S - n:C_MASK + S], scale=-1.0 / 8, scalar=FAR,
                                                         op0=ALU.add, op1=ALU.min, accum_out=nmax[:, b, hh:hh + 1])
                    emptied(ins, ("score", u_, hh))

            def normalise(u_):
                i, b = u_ % TT, u_ % 2
                n = P * (i + 1)
                dve.wait_ge(exp_ready, 2 * u_ + 2)
                dve.reciprocal(pinv[:, b, :], psum_p[:, b, :]).then_inc(pinv_ready, 1)
                dve.wait_ge(pinv_ready, u_ + 1)
                for hh in range(2):
                    dve.tensor_scalar(prob[:, u_ % 4, hh, 0:n], prob[:, u_ % 4, hh, 0:n], pinv[:, b, hh:hh + 1], None,
                                      ALU.mult).then_inc(prob_ready, 1)

            def attn_out(m):
                banks.wait_full(dve, ("attn", m))
                emptied(dve.tensor_copy(mixa[:, m, :], bk(("attn", m))[:]), ("attn", m))

            def add_scaled(name, w, q):
                t, half = q // 2, q % 2
                cols = xs[:, t, half * 512:(half + 1) * 512]
                banks.wait_full(dve, name)
                emptied(dve.scalar_tensor_tensor(out=cols, in0=bk(name)[:], scalar=grs[:, w, t:t + 1], in1=cols,
                                                 op0=ALU.mult, op1=ALU.add), name)

            units = CM * TT
            for u_ in range(units + 1):
                if u_ == 1:
                    for t in range(2, TT):
                        banks.wait_full(dve, ("v", t))
                        emptied(dve.tensor_copy(vr[:, t, :], bk(("v", t))[:]), ("v", t))
                if u_ == 6:
                    banks.wait_emptied(dve, "conv_sq")
                    dve.wait_ge(x_again, 16)
                    recip(grs[:, 0, :], gss[:, 0, :])
                if u_ >= 6 and u_ % 2 == 0:
                    add_scaled(("outc", (u_ - 6) // 2), 0, (u_ - 6) // 2)
                if u_ % TT == 3 and u_ > TT:
                    attn_out(u_ // TT - 1)
                if u_ < units:
                    scores(u_)
                if u_ >= 1:
                    normalise(u_ - 1)
                if 9 <= u_ < 9 + CM:
                    split_out(1, u_ - 9)
                if u_ == 2:
                    for m in range(CM):
                        dve.wait_ge(silu_ready, m + 1)
                        dve.tensor_copy(mix_hi[0][:, m, :], mixc[:, m, :]).then_inc(mix_hi_ready[0], 1)
            add_scaled(("outc", 2 * TT - 2), 0, 2 * TT - 2)
            attn_out(CM - 1)
            add_scaled(("outc", 2 * TT - 1), 0, 2 * TT - 1)
            banks.wait_emptied(dve, "attn_sq")
            recip(grs[:, 1, :], gss[:, 1, :])
            banks.wait_emptied(dve, ("outc", 2 * TT - 1))

            def columns_out(kind, t, gains):
                for kh in range(2):
                    name = (kind, t, kh)
                    banks.wait_full(dve, name)
                    emptied(dve.tensor_tensor(
                        hT[:, 4 * kh:4 * kh + 4, t * P:(t + 1) * P], bk(name)[:].rearrange("p (k n) -> p k n", k=4),
                        pr[:, gains + 4 * kh:gains + 4 * kh + 4].rearrange("p (k n) -> p k n", n=1).broadcast_to([P, 4, P]),
                        ALU.mult), name)

            for q in range(2 * TT):
                t, half = q // 2, q % 2
                add_scaled(("outa", q), 1, q)
                banks.wait_emptied(dve, ("outa", q))
                if half == 0 and t >= 1:
                    normal_rows(1, t - 1)
                if half == 1 and t >= 2:
                    columns_out("h2", t - 2, Q_FFN)
            normal_rows(1, TT - 1)
            columns_out("h2", TT - 2, Q_FFN)
            columns_out("h2", TT - 1, Q_FFN)

            n = [0]

            def step(ins):
                n[0] += 1
                ins.then_inc(rstep, 1)
                dve.wait_ge(rstep, n[0])

            def wide(ap, k):
                return ap.rearrange("p (t n) -> p t n", n=1).broadcast_to([P, TT, k])

            def table(col, k):
                return c[:, col:col + k].rearrange("p (a n) -> p a n", a=1).broadcast_to([P, TT, k])

            def first_hot(out_ap, in_ap, top, scratch, weights, k):
                step(dve.tensor_tensor(scratch, in_ap, wide(top, k), ALU.is_equal))
                step(dve.tensor_tensor(scratch, scratch, table(weights, k), ALU.mult))
                step(dve.tensor_reduce(sm[:, 0, :], scratch, AX.X, ALU.max))
                step(dve.tensor_tensor(out_ap, scratch, wide(sm[:, 0, :], k), ALU.is_equal))

            banks.wait_full(dve, "logit")
            emptied(dve.tensor_copy(lg[:], bk("logit")[:, 0:TT * NR].rearrange("p (t n) -> p t n", t=TT)), "logit")
            banks.wait_emptied(dve, "logit")
            grp = lg[:, :, 0:NG]
            step(dve.tensor_reduce(sm[:, 1, :], grp, AX.X, ALU.max))
            dve.tensor_tensor(rt[:, 0, :, 0:NG], grp, wide(sm[:, 1, :], NG), ALU.subtract).then_inc(exp_in, 1)
            first_hot(rt[:, 1, :, 0:NG], grp, sm[:, 1, :], rt[:, 2, :, 0:NG], C_GRP, NG)
            step(dve.tensor_scalar(rt[:, 2, :, 0:NG], rt[:, 1, :, 0:NG], -1.0, FAR, ALU.add, ALU.mult))
            for t in range(TT):
                ins = dve.tensor_tensor(
                    rt[:, 3, t, :].rearrange("p (g e) -> p g e", g=NG), lg[:, t, NG:NR].rearrange("p (g e) -> p g e", g=NG),
                    rt[:, 2, t, 0:NG].rearrange("p (g e) -> p g e", e=1).broadcast_to([P, NG, EG]), ALU.add)
            step(ins)
            step(dve.tensor_reduce(sm[:, 2, :], rt[:, 3], AX.X, ALU.max))
            first_hot(hot[:, 0], rt[:, 3], sm[:, 2, :], rt[:, 4], C_RANK, NE)
            step(dve.tensor_scalar(rt[:, 4], hot[:, 0], -FAR, None, ALU.mult))
            step(dve.tensor_tensor(rt[:, 5], rt[:, 3], rt[:, 4], ALU.add))
            step(dve.tensor_reduce(sm[:, 3, :], rt[:, 5], AX.X, ALU.max))
            first_hot(hot[:, 1], rt[:, 5], sm[:, 3, :], rt[:, 4], C_RANK, NE)
            dve.tensor_tensor(rt[:, 6], hot[:, 0], hot[:, 1], ALU.add).then_inc(chosen, 1)
            dve.tensor_tensor(sm[:, 6, :], sm[:, 3, :], sm[:, 2, :], ALU.subtract).then_inc(exp_in, 1)
            def over8(ap, k):
                return ap.rearrange("p (j n) -> p j n", n=1).broadcast_to([P, 2 * TT, k])

            def table8(col, k):
                return c[:, col:col + k].rearrange("p (a n) -> p a n", a=1).broadcast_to([P, 2 * TT, k])

            hot8 = hot[:].rearrange("p k t n -> p (k t) n")
            rt8 = rt[:, 4:6].rearrange("p k t n -> p (k t) n")
            R, X, H, SIDE, KEY, T0, T1 = (by8[:, i, :] for i in range(7))

            def chosen_value(out8, values):
                step(dve.tensor_tensor(rt8, hot8, values, ALU.mult))
                step(dve.tensor_reduce(out8, rt8, AX.X, ALU.add))

            chosen_value(SIDE, table8(C_SIDE, NE))
            zero = PAIRS // 2
            thr = rt[:, 1:3].rearrange("p a t n -> p (a t n)")[:, 0:NE * STEPS].rearrange("p (e j) -> p e j", e=NE)
            banks.wait_full(dve, "count")
            emptied(dve.tensor_tensor(thr, bk("count")[:, 0:NE].rearrange("p (e j) -> p e j", j=1).broadcast_to([P, NE, STEPS]),
                                      c[:, C_THR:C_THR + STEPS].rearrange("p (e j) -> p e j", e=1).broadcast_to([P, NE, STEPS]),
                                      ALU.is_gt), "count")
            banks.wait_emptied(dve, "count")
            step(dve.tensor_reduce(beyond[:], thr, AX.X, ALU.add))
            step(dve.tensor_reduce(scan[:, 0, zero:], beyond[:].rearrange("p (g a) -> p g a", a=2), AX.X, ALU.max))
            step(dve.tensor_scalar(scan[:, 0, zero:], scan[:, 0, zero:], 1.0, None, ALU.add))
            here = 0
            for to, shift in ((1, 1), (2, 2), (1, 4), (2, 8)):
                step(dve.tensor_tensor(scan[:, to, zero:], scan[:, here, zero:], scan[:, here, zero - shift:zero - shift + PAIRS],
                                       ALU.add))
                here = to
            ends = scan[:, 2, zero:]
            firsts = scan[:, 2, zero - 1:zero - 1 + PAIRS]
            step(dve.tensor_copy(beyond[:].rearrange("p (g a) -> p g a", a=2),
                                 firsts.rearrange("p (g a) -> p g a", a=1).broadcast_to([P, PAIRS, 2])))
            banks.wait_full(dve, "rank")
            emptied(dve.tensor_tensor(
                rt[:, 4:6].rearrange("p k t n -> p k (t n)"), hot[:].rearrange("p k t n -> p k (t n)"),
                bk("rank")[:, 0:TT * NE].rearrange("p (a n) -> p a n", a=1).broadcast_to([P, 2, TT * NE]), ALU.mult), "rank")
            banks.wait_emptied(dve, "rank")
            step(dve.tensor_reduce(R, rt8, AX.X, ALU.add))
            step(dve.tensor_tensor(cmp8[:, :, 0:STEPS], over8(R, STEPS), table8(C_THR, STEPS), ALU.is_ge))
            step(dve.tensor_reduce(X, cmp8[:, :, 0:STEPS], AX.X, ALU.add))
            chosen_value(T0, beyond[:].rearrange("p (a n) -> p a n", a=1).broadcast_to([P, 2 * TT, NE]))
            step(dve.tensor_tensor(H, T0, X, ALU.add))
            step(dve.scalar_tensor_tensor(out=T1, in0=X, scalar=-float(CAP), in1=R, op0=ALU.mult, op1=ALU.add))
            step(dve.tensor_tensor(KEY, T1, SIDE, ALU.add))
            step(dve.tensor_tensor(passhot, over8(H, LISTS), table8(C_IOTA, LISTS), ALU.is_equal))
            step(dve.tensor_tensor(numhot[:, :, 0, :], passhot, over8(c[:, C_TOK:C_TOK + 2 * TT], LISTS), ALU.mult))
            step(dve.tensor_tensor(numhot[:, :, 1, :], passhot, over8(c[:, C_ROW:C_ROW + 2 * TT], LISTS), ALU.mult))
            dve.tensor_tensor(onehot, table8(C_IOTA, P), over8(KEY, P), ALU.is_equal).then_inc(list_in, 1)
            dve.memset(xg, 0.0).then_inc(list_ready, 1)
            dve.wait_ge(list_full, 1)
            dve.tensor_scalar(tlist[:].rearrange("p a g -> p (a g)"), pb[0][:, 0:2 * LISTS], -1.0, float(NOWHERE), ALU.mult,
                              ALU.add).then_inc(list_ready, 1)
            step(dve.tensor_tensor(
                ended, c[:, C_IOTA:C_IOTA + MOST].rearrange("p (n g) -> p n g", g=1).broadcast_to([P, MOST, PAIRS]),
                ends.rearrange("p (n g) -> p n g", n=1).broadcast_to([P, MOST, PAIRS]), ALU.is_ge))
            step(dve.tensor_reduce(ofpair[:, 0, :], ended[:, :, 0:PAIRS - 1:2], AX.X, ALU.add))
            step(dve.tensor_reduce(ofpair[:, 1, :], ended[:, :, 1:PAIRS - 1:2], AX.X, ALU.add))
            step(dve.tensor_scalar(fewer[:, 0:HALVES], c[:, C_TWO:C_TWO + HALVES], scan[:, 2, zero + PAIRS - 1:zero + PAIRS],
                                   None, ALU.is_lt))
            step(dve.tensor_reduce(fewer[:, HALVES:HALVES + 1], fewer[:, 0:HALVES], AX.X, ALU.add))
            dve.tensor_tensor(pass_of[:, 0, :], ofpair[0:1, 0, :], ofpair[0:1, 1, :], ALU.add)
            dve.tensor_tensor(pass_of[:, 1, :], ofpair[0:1, 0, :], ofpair[0:1, 1, :], ALU.subtract)
            dve.tensor_copy(first[:], firsts[0:1, :])
            dve.tensor_scalar(halves[:, 1:2], fewer[0:1, HALVES:HALVES + 1], -1.0, None, ALU.add)
            dve.tensor_copy(halves[:, 0:1], fewer[0:1, HALVES:HALVES + 1]).then_inc(plan_ready, 1)
            dve.wait_ge(exp_out, 2)
            step(dve.tensor_reduce(sm[:, 4, :], rt[:, 0, :, 0:NG], AX.X, ALU.add))
            step(dve.tensor_scalar(sm[:, 5, :], sm[:, 6, :], 1.0, None, ALU.add))
            step(dve.tensor_tensor(sm[:, 4, :], sm[:, 4, :], sm[:, 5, :], ALU.mult))
            step(dve.reciprocal(gw[:, 0, :], sm[:, 4, :]))
            step(dve.tensor_tensor(gw[:, 1, :], gw[:, 0, :], sm[:, 6, :], ALU.mult))

            def x_out(n_, s):
                dve.wait_ge(xgT_full, n_ + 1)
                wait(dve, up_done, n_ - 1)
                for kh in range(2):
                    dve.tensor_tensor(
                        xgT[:, s, 4 * kh:4 * kh + 4, :], pb[kh][:].rearrange("p (k n) -> p k n", k=4),
                        pr[:, Q_FFN + 4 * kh:Q_FFN + 4 * kh + 4].rearrange("p (k n) -> p k n", n=1).broadcast_to([P, 4, P]),
                        ALU.mult).then_inc(xgT_ready, 1)

            def one(n_, s, h):
                dve.wait_ge(sil_ready, n_ + 1)
                wait(dve, hidT_full, n_ - 1)
                dve.tensor_tensor(hid[:, s], sil[:, s, :].rearrange("p (n k) -> p k n", k=FK),
                                  pb[2 + s][:, F:2 * F].rearrange("p (n k) -> p k n", k=FK), ALU.mult).then_inc(hid_ready, 1)
                x_out(n_ + 1, 1 - s)
                dve.wait_ge(down_done, n_ + 1)
                wait(dve, y_stored[s], 16 * h)
                dve.tensor_copy(yb[:, s, 512:D], pb[7][:]).then_inc(yd_ready, 1)

            x_out(0, 0)
            half = all_passes(dve, one)

            def split_gate(h):
                for k in range(DK):
                    dve.wait_ge(whi_ready, h * DK + k + 1)
                    dve.scalar_tensor_tensor(out=wpg_lo[h][:, k, :], in0=wpg[h][:, k, :], scalar=pr[:, Q_PLE + k:Q_PLE + k + 1],
                                             in1=wpg_hi[h][:, k, :].bitcast(F32), op0=ALU.mult,
                                             op1=ALU.subtract).then_inc(wlo_ready, 1)

            split_gate(0)
            for t in range(TT + 1):
                if t < TT:
                    for k in range(2):
                        dve.wait_ge(yg_loaded[2 * t + k], 16)
                        dve.scalar_tensor_tensor(out=xs[:, t, :], in0=yg[:, 2 * t + k, :], scalar=gw[:, k, t:t + 1],
                                                 in1=xs[:, t, :], op0=ALU.mult, op1=ALU.add).then_inc(x2_ready, 1)
                        dve.wait_ge(x2_ready, 2 * t + k + 1)
                if t >= 1:
                    for kh in range(2):
                        name = ("x2", t - 1, kh)
                        dve.wait_ge(xhi_ready, 2 * (t - 1) + kh + 1)
                        emptied(dve.tensor_tensor(
                            x2_lo[t - 1][:, 4 * kh:4 * kh + 4, :], bk(name)[:].rearrange("p (k n) -> p k n", k=4),
                            x2_hi[:, 4 * kh:4 * kh + 4, (t - 1) * P:t * P].bitcast(F32), ALU.subtract), name)
            for t in range(TT):
                inverse(2, t)
            assert rsn[0] == ROOTS
            split_gate(1)
            x3 = 0
            for q in range(2 * TT):
                half, t = q // TT, q % TT
                name = ("pgate", q)
                cols = slice(half * 512, (half + 1) * 512)
                banks.wait_emptied(dve, name)
                dve.tensor_tensor(sgate[:, q % 4, :], sgate[:, q % 4, :], plep[:, t, cols], ALU.mult).then_inc(x3_ready, 1)
                x3 += 1
                dve.wait_ge(x3_ready, x3)
                dve.tensor_tensor(xs[:, t, cols], xs[:, t, cols], sgate[:, q % 4, :], ALU.add).then_inc(x3_ready, 1)
                x3 += 1
                if half == 1:
                    if t == 0:
                        dve.wait_ge(last_loaded, 32)
                    inverse(3, t)
                    for cols in (slice(0, 512), slice(512, D)):
                        dve.scalar_tensor_tensor(out=xn_rows[:, t, cols], in0=xs[:, t, cols], scalar=rs[:, 3, t:t + 1],
                                                 in1=gfin[:, cols], op0=ALU.mult, op1=ALU.mult).then_inc(o_ready, 1)

        @block.tensor
        def _(pe):
            pe.wait_ge(const_loaded, 32)
            for t in range(TT):
                pe.wait_ge(xn_ready, t + 1)
                for k in range(DK):
                    ins = pe.transpose(bk(("x", k))[:, t * P:(t + 1) * P], xn[:, t, k, :], ident)
                    if t == TT - 1:
                        filled(ins, ("x", k))
            def project(name, chunk, m):
                banks.wait_free(pe, name)
                pe.wait_ge(win_hi_ready[chunk], m + 1)
                parts = ((win_hi[chunk], hT_hi), (win_hi[chunk], hT_lo), (win_lo[chunk], hT_hi))
                for j, (w, h) in enumerate(parts):
                    if j == 2:
                        pe.wait_ge(win_lo_ready[chunk], m + 1)
                    for k in range(DK):
                        if name == ("val", 0) and j == 0:
                            pe.wait_ge(hT_hi_ready, k + 1)
                        if name == ("val", 0) and j == 1:
                            banks.wait_emptied(pe, ("x", k))
                        ins = pe.matmul(bk(name)[:], w[:, k, m * P:(m + 1) * P], h[:, k, :],
                                        start=(j == 0 and k == 0), stop=(j == 2 and k == DK - 1))
                filled(ins, name)

            for m in range(CM):
                for i, name in enumerate(("val", "gate")):
                    project((name, m), i, m)

            def rotate(j):
                banks.wait_free(pe, ("rot", j))
                banks.wait_emptied(pe, ("raw", j))
                filled(pe.matmul(bk(("rot", j))[:], c[:, C_ROT:C_ROT + P], qraw[:, j % 2, :], start=True, stop=True), ("rot", j))

            def values(t):
                banks.wait_free(pe, ("v", t))
                parts = ((hT_hi, win_hi[4]), (hT_lo, win_hi[4]), (hT_hi, win_lo[4]))
                for j, (h, w) in enumerate(parts):
                    if t == 0 and j != 1:
                        pe.wait_ge((win_hi_ready, None, win_lo_ready)[j][4], CM)
                    for k in range(DK):
                        ins = pe.matmul(bk(("v", t))[:], h[:, k, t * P:(t + 1) * P], w[:, k, :],
                                        start=(j == 0 and k == 0), stop=(j == 2 and k == DK - 1))
                filled(ins, ("v", t))

            for j in range(2 * CM + 1):
                if j < 2 * CM:
                    project(("raw", j), 2 + j // CM, j % CM)
                if j >= 1:
                    rotate(j - 1)
                if j > CM + 1:
                    values(j - CM - 2)

            def channel_sum(name, src):
                banks.wait_free(pe, name)
                for t in range(TT):
                    for m in range(CM):
                        ins = pe.matmul(bk(name)[:, t:t + 1], src[:, m, t * P:(t + 1) * P], ones[:, 0:1],
                                        start=(m == 0), stop=(m == CM - 1))
                filled(ins, name)

            values(TT - 1)
            pe.wait_ge(tap_done, CM * TAPS)
            banks.wait_free(pe, "mean")
            for m in range(CM):
                ins = pe.matmul(bk("mean")[:], mean_w[:], mixc[:, m, :], start=(m == 0), stop=(m == CM - 1))
            filled(ins, "mean")
            banks.wait_free(pe, "var")
            pe.wait_ge(csq_ready, CM)
            for m in range(CM):
                ins = pe.matmul(bk("var")[:], mean_w[:], sqc[:, m, :], start=(m == 0), stop=(m == CM - 1))
            filled(ins, "var")

            pe.wait_ge(qz_set, 2)
            pe.wait_ge(rope_done, 3 * CM)

            def score(u_):
                m, i = u_ // TT, u_ % TT
                n = P * (i + 1)
                for hh in range(2):
                    name = ("score", u_, hh)
                    banks.wait_free(pe, name)
                    filled(pe.matmul(bk(name)[:, 0:n], qz[:, 2 * m + hh, i * P:(i + 1) * P], kT[:, m, 0:n],
                                     start=True, stop=True), name)

            def transpose_probs(u_):
                m, i, b = u_ // TT, u_ % TT, u_ % 4
                for hh in range(2):
                    name = ("probT", u_, hh)
                    pe.wait_ge(prob_ready, 2 * u_ + hh + 1)
                    banks.wait_free(pe, name)
                    for j in range(i + 1):
                        ins = pe.transpose(bk(name)[:, j * P:(j + 1) * P], prob[:, b, hh, j * P:(j + 1) * P], ident)
                    filled(ins, name)

            def attend(u_):
                m, i, b = u_ // TT, u_ % TT, u_ % 4
                name = ("attn", m)
                if i == 0:
                    banks.wait_free(pe, name)
                for hh in range(2):
                    pt = ("probT", u_, hh)
                    banks.wait_emptied(pe, pt)
                for j in range(i + 1):
                    for hh in range(2):
                        ins = pe.matmul(bk(name)[hh * DH:(hh + 1) * DH, i * P:(i + 1) * P],
                                        vr[:, j, (2 * m + hh) * DH:(2 * m + hh + 1) * DH],
                                        probT[:, b, hh, j * P:(j + 1) * P], start=(j == 0), stop=(j == i))
                if i == TT - 1:
                    filled(ins, name)
                else:
                    ins.then_inc(attended, 1)

            def out_part(name, w, q, lo, hi):
                t, half = q // 2, q % 2
                if lo == 0:
                    banks.wait_free(pe, name)
                parts = ((wo_hi[w], mix_hi[w]), (wo_lo[w], mix_hi[w]), (wo_hi[w], mix_lo[w]))
                for j in range(lo, hi):
                    weight, src = parts[j // CM]
                    m = j % CM
                    if q == 0 and m == 0:
                        pe.wait_ge((mix_hi_ready, wo_lo_ready, mix_lo_ready)[j // CM][w], CM)
                    ins = pe.matmul(bk(name)[:], src[:, m, t * P:(t + 1) * P], weight[:, m, half * 512:(half + 1) * 512],
                                    start=(j == 0), stop=(j == 3 * CM - 1))
                if hi == 3 * CM:
                    filled(ins, name)

            units = CM * TT
            for u_ in range(units + 3):
                if u_ < units:
                    score(u_)
                if 2 <= u_ < units + 2:
                    transpose_probs(u_ - 2)
                if u_ == 3:
                    for t in range(TT):
                        banks.wait_emptied(pe, ("v", t))
                if u_ == 4:
                    pe.wait_ge(osq_ready, CM)
                    channel_sum("conv_sq", sqc)
                    pe.wait_ge(wo_hi_ready[0], CM)
                if u_ >= 4:
                    q, part = (u_ - 4) // 2, (u_ - 4) % 2
                    out_part(("outc", q), 0, q, part * 3 * CM // 2, (part + 1) * 3 * CM // 2)
                if u_ >= 3:
                    attend(u_ - 3)
            out_part(("outc", 2 * TT - 1), 0, 2 * TT - 1, 3 * CM // 2, 3 * CM)

            def turn_rows(kind, t, first):
                pe.wait_ge(xn_ready, first + t + 1)
                for kh in range(2):
                    name = (kind, t, kh)
                    banks.wait_free(pe, name)
                    for k in range(4):
                        ins = pe.transpose(bk(name)[:, k * P:(k + 1) * P], xn[:, t, 4 * kh + k, :], ident)
                    filled(ins, name)

            pe.wait_ge(wo_hi_ready[1], CM)
            banks.wait_emptied(pe, ("attn", CM - 1))
            for q in range(2 * TT):
                t, half = q // 2, q % 2
                out_part(("outa", q), 1, q, 0, 3 * CM)
                if q == 0:
                    pe.wait_ge(sqa_ready, CM)
                    channel_sum("attn_sq", sqa)
                if half == 1 and t >= 1:
                    turn_rows("h2", t - 1, TT)
            banks.wait_free(pe, "logitT")
            for tiles in ((0, TT // 2), (TT // 2, TT)):
                if tiles[1] == TT:
                    turn_rows("h2", TT - 1, TT)
                for t in range(*tiles):
                    for kh in range(2):
                        banks.wait_emptied(pe, ("h2", t, kh))
                cols = slice(tiles[0] * P, tiles[1] * P)
                for k in range(DK):
                    ins = pe.matmul(bk("logitT")[0:NR, cols], wr[:, k, :], hT[:, k, cols], start=(k == 0), stop=(k == DK - 1))
            filled(ins, "logitT")

            def ple(q):
                t, half = q // 2, q % 2
                banks.wait_free(pe, ("ple", q))
                for k in range(PK):
                    ins = pe.matmul(bk(("ple", q))[:], pTs[:, k, t * P:(t + 1) * P], wpp[:, k, half * 512:(half + 1) * 512],
                                    start=(k == 0), stop=(k == PK - 1))
                filled(ins, ("ple", q))

            pe.wait_ge(ple_loaded, 32)
            ple(0)
            banks.wait_emptied(pe, "logitT")
            banks.wait_free(pe, "logit")
            for t in range(TT):
                ins = pe.transpose(bk("logit")[:, t * NR:(t + 1) * NR], logT[:, t * P:(t + 1) * P], ident[0:NR, 0:NR])
            filled(ins, "logit")
            for q in range(1, 4):
                ple(q)
            pe.wait_ge(chosen, 1)
            banks.wait_free(pe, "count")
            for t in range(TT):
                ins = pe.matmul(bk("count")[:, 0:NE], ones[:], rt[:, 6, t, :], start=(t == 0), stop=(t == TT - 1))
            filled(ins, "count")
            banks.wait_free(pe, "rank")
            for t in range(TT):
                for j in range(t + 1):
                    ins = pe.matmul(bk("rank")[:, t * NE:(t + 1) * NE], ones[:] if j < t else c[:, C_UP:C_UP + P],
                                    rt[:, 6, j, :], start=(j == 0), stop=(j == t))
            filled(ins, "rank")
            for q in range(4, 6):
                ple(q)
            pe.wait_ge(list_in, 1)
            for j in range(2 * TT):
                ins = pe.matmul(pb[0][:, 0:2 * LISTS], onehot[:, j, :], numhot[:, j].rearrange("p a g -> p (a g)"),
                                start=(j == 0), stop=(j == 2 * TT - 1))
            ins.then_inc(list_full, 1)
            for q in range(6, 2 * TT):
                ple(q)

            def turn_tokens(n, s, h):
                if isinstance(n, int) and n == 0:
                    pe.wait_ge(list_ready, 2)
                else:
                    pe.wait_ge(xgT_ready, 2 * n)
                pe.wait_ge(gathered[s], 16 * h + 16)
                for k in range(DK):
                    ins = pe.transpose(pb[k // 4][:, k % 4 * P:(k % 4 + 1) * P], xg[:, s, k * P:(k + 1) * P], ident)
                ins.then_inc(xgT_full, 1)

            def one(n, s, h):
                if isinstance(n, int) and n == 0:
                    multiply(n, s, h, 0, 0)
                else:
                    g = number(pe, pass_of[0:1, 0, bass.ds(n, 1)], 0, PAIRS - 1)
                    odd = number(pe, pass_of[0:1, 1, bass.ds(n, 1)], 0, 1)
                    with pe.If(odd < 1):
                        multiply(n, s, h, g, 0)
                    with pe.Else():
                        multiply(n, s, h, g, 1)

            def multiply(n, s, h, g, w):
                pe.wait_ge(xgT_ready, 2 * (n + 1))
                wait(pe, hid_ready, n - 1)
                pe.wait_ge(up_ready, g + 1)
                for k in range(DK):
                    for a in range(2):
                        ins = pe.matmul(pb[2 + s][a * CAP:(a + 1) * CAP, :], xgT[:, s, k, a * CAP:(a + 1) * CAP],
                                        up_w(w, a)[:, :, k, :], start=(k == 0), stop=(k == DK - 1))
                ins.then_inc(up_done, 1)
                turn_tokens(n + 1, 1 - s, h + s)
                pe.wait_ge(hid_ready, n + 1)
                wait(pe, hidT_ready, n - 1)
                for k in range(FK):
                    ins = pe.transpose(pb[4 + s][:, k * P:(k + 1) * P], hid[:, s, k, :], ident)
                ins.then_inc(hidT_full, 1)
                pe.wait_ge(hidT_ready, n + 1)
                wait(pe, ya_ready, n)
                wait(pe, yd_ready, n)
                pe.wait_ge(dn_ready, g + 1)
                for half in range(2):
                    for k in range(FK):
                        for a in range(2):
                            ins = pe.matmul(pb[6 + half][a * CAP:(a + 1) * CAP, :], hidT[:, s, k, a * CAP:(a + 1) * CAP],
                                            dn_w(w, a)[:, k, half * 512:(half + 1) * 512], start=(k == 0), stop=(k == FK - 1))
                ins.then_inc(down_done, 1)

            turn_tokens(0, 0, 0)
            for q in range(4, 2 * TT):
                banks.wait_emptied(pe, ("ple", q))
            pe.wait_ge(plan_ready, 1)
            half = all_passes(pe, one)
            pe.wait_ge(ya_ready, 2 * half)
            pe.wait_ge(yd_ready, 2 * half)
            pe.wait_ge(xgT_ready, 4 * half + 2)

            def product(q):
                half, t = q // TT, q % TT
                name = ("pgate", q)
                if t == 0:
                    pe.wait_ge(whi_ready, (half + 1) * DK)
                banks.wait_free(pe, name)
                parts = ((wpg_hi[half], 0), (wpg_hi[half], 1), (wpg_lo[half], 0))
                for j, (w, rest) in enumerate(parts):
                    if t == 0 and j == 2:
                        pe.wait_ge(wlo_ready, (half + 1) * DK)
                    for k in range(DK):
                        lhs = x2_lo[t][:, k, :] if rest else x2_hi[:, k, t * P:(t + 1) * P]
                        pe.matmul(bk(name)[:], lhs, w[:, k, :], start=(j == 0 and k == 0), stop=False)

            def add_bias(q):
                half, t = q // TT, q % TT
                filled(pe.matmul(bk(("pgate", q))[:], rootT[:, t * P:(t + 1) * P], brow[:, half * 512:(half + 1) * 512],
                                 start=False, stop=True), ("pgate", q))

            def turn_x2(t):
                pe.wait_ge(x2_ready, 2 * (t + 1))
                for kh in range(2):
                    name = ("x2", t, kh)
                    banks.wait_free(pe, name)
                    for k in range(4):
                        cols = slice((4 * kh + k) * P, (4 * kh + k + 1) * P)
                        ins = pe.transpose(bk(name)[:, k * P:(k + 1) * P], xs[:, t, cols], ident)
                    filled(ins, name)

            turn_x2(0)
            for t in range(1, TT):
                turn_x2(t)
                for kh in range(2):
                    banks.wait_emptied(pe, ("x2", t - 1, kh))
                product(t - 1)
            banks.wait_free(pe, "rootT")
            for t in range(TT):
                pe.wait_ge(root_ready, 2 * (2 * TT + t) + 2)
                ins = pe.matmul(bk("rootT")[0:1, t * P:(t + 1) * P], ss[:, 2, t:t + 1], ident, start=True, stop=True)
            filled(ins, "rootT")
            banks.wait_emptied(pe, "rootT")
            pe.wait_ge(last_loaded, 32)
            for t in range(TT - 1):
                add_bias(t)
            for kh in range(2):
                banks.wait_emptied(pe, ("x2", TT - 1, kh))
            for q in range(TT - 1, 2 * TT):
                product(q)
                add_bias(q)


def kernel(x, p, g_mix, w_in, w_dw, b_dw, conv_ln_g, conv_ln_b, beta_conv, beta_attn, w_out, g_ffn, w_group, b_group,
           w_erouter, b_erouter, w_gate, w_up, w_down, g_ple, w_ple_gate, b_ple_gate, w_ple_proj, g_final):
    import concourse.bacc as bacc
    from concourse.bass_utils import run_bass_kernel_spmd

    a = np.asarray
    by_channel = np.concatenate([a(w_dw)[0].T, a(b_dw)[0][:, None], a(conv_ln_g)[0][:, None], a(conv_ln_b)[0][:, None],
                                 a(beta_conv)[0][:, None]], axis=1).reshape(CM, P, PM)
    router_bias = np.concatenate([a(b_group)[0], a(b_erouter)[0].reshape(NE), np.zeros(P - NR, np.float32)])
    prm = np.concatenate([by_channel.transpose(1, 0, 2).reshape(P, CM * PM), a(beta_attn)[0].reshape(CM, P).T,
                          a(g_mix)[0].reshape(P, DK), a(g_ffn)[0].reshape(P, DK), a(g_ple)[0].reshape(DK, P).T,
                          router_bias[:, None]], axis=1)
    w_r = np.concatenate([a(w_group)[0], a(w_erouter)[0].transpose(1, 0, 2).reshape(D, NE)], axis=1)
    arrays = {
        "x_in": a(x)[0], "w_in_in": a(w_in)[0], "w_out_in": a(w_out)[0], "w_r_in": w_r, "w_gate_in": a(w_gate)[0],
        "w_up_in": a(w_up)[0], "w_down_in": a(w_down)[0], "w_pg_in": a(w_ple_gate)[0], "w_pp_in": a(w_ple_proj)[0],
        "pT_in": a(p)[0, 0].T, "b_pg_in": a(b_ple_gate), "g_final_in": a(g_final), "prm_in": prm, "cst_in": constants(),
    }
    arrays = {name: np.ascontiguousarray(v) for name, v in arrays.items()}
    nc = bacc.Bacc("TRN2", target_bir_lowering=False, num_devices=1)
    args = [nc.dram_tensor(name, v.shape, mybir.dt.from_np(v.dtype), kind="ExternalInput").ap() for name, v in arrays.items()]
    out = nc.dram_tensor("out_rows", (S, D), F32, kind="ExternalOutput").ap()
    build(nc, *args, out)
    result = run_bass_kernel_spmd(nc, [arrays], core_ids=[0])
    return result.results[0]["out_rows"].reshape(1, S, D)
```
